# Optimizing a Trainium2 kernel written in Bass

```python
import jax
import jax.numpy as jnp
from jax import lax
import numpy as np
import math
import jax, jax.numpy as jnp

D_MODEL = 1024
BATCH = 1
SEQ = 512
DEPTH = 2

HEAD_DIM = 64
ROPE_THETA = 10000.0
NORM_EPS = 1e-6
Q_BLOCK = 128
NEG_INF = -1e30
FORCE_SELECT = 1e9

NSA_HEADS = 8
NSA_KV_GROUPS = 2
NSA_HEADS_PER_GROUP = NSA_HEADS // NSA_KV_GROUPS
NSA_CMP_LEN = 32
NSA_CMP_STRIDE = 16
NSA_SEL_LEN = 64
NSA_SEL_TOPK = 16
NSA_WINDOW = 512
NSA_BRANCHES = 3

MOBA_HEADS = 8
MOBA_BLOCK = 256
MOBA_TOPK = 3

MEM_LEN = 256
MEM_HEADS = 4

RET_HEADS = 4
RET_QK_DIM = D_MODEL // RET_HEADS
RET_V_DIM = 2 * D_MODEL // RET_HEADS
RET_CHUNK = 128

NSA_Q_W = NSA_HEADS * HEAD_DIM
NSA_KV_W = NSA_KV_GROUPS * HEAD_DIM
MOBA_W = MOBA_HEADS * HEAD_DIM
MEM_W = MEM_HEADS * HEAD_DIM
RET_QK_W = RET_HEADS * RET_QK_DIM
RET_V_W = RET_HEADS * RET_V_DIM

EVEN_SPLITS = (NSA_Q_W, NSA_KV_W, NSA_KV_W, NSA_KV_W, NSA_KV_W, NSA_KV_W, NSA_KV_W,
               NSA_BRANCHES * NSA_HEADS, NSA_Q_W,
               MOBA_W, MOBA_W, MOBA_W, MOBA_W,
               MEM_W, MEM_W)
ODD_SPLITS = (RET_QK_W, RET_QK_W, RET_V_W, RET_V_W, MEM_W, MEM_W)
EVEN_IN_W = sum(EVEN_SPLITS)
EVEN_OUT_W = NSA_Q_W + MOBA_W + MEM_W
ODD_IN_W = sum(ODD_SPLITS)
ODD_OUT_W = RET_V_W + MEM_W


def _split(h, sizes):
    cuts = np.cumsum(np.array(sizes))[:-1].tolist()
    return jnp.split(h, cuts, axis=-1)

def rms_norm(x, g):
    xf = x.astype(jnp.float32)
    y = xf * lax.rsqrt(jnp.mean(xf * xf, axis=-1, keepdims=True) + NORM_EPS)
    return (y * g.astype(jnp.float32)).astype(x.dtype)

def rotary_tables(positions, inv_freq):
    ang = positions.astype(jnp.float32)[..., None] * inv_freq
    return jnp.cos(ang), jnp.sin(ang)

def apply_rotary(x, cos, sin):
    x1, x2 = jnp.split(x, 2, axis=-1)
    c = cos[:, :, None, :].astype(x.dtype)
    s = sin[:, :, None, :].astype(x.dtype)
    return jnp.concatenate([x1 * c - x2 * s, x1 * s + x2 * c], axis=-1)

def masked_softmax(s, mask):
    s = jnp.where(mask, s.astype(jnp.float32), NEG_INF)
    m = jnp.max(s, axis=-1, keepdims=True)
    p = jnp.where(mask, jnp.exp(s - m), 0.0)
    return p / jnp.maximum(jnp.sum(p, axis=-1, keepdims=True), 1e-30)

def nsa_compress(a, pe, w1, w2):
    T = a.shape[1]
    n_cmp = (T - NSA_CMP_LEN) // NSA_CMP_STRIDE + 1
    idx = np.arange(n_cmp)[:, None] * NSA_CMP_STRIDE + np.arange(NSA_CMP_LEN)[None, :]
    blocks = a[:, idx] + pe[None, None, :, None, :].astype(a.dtype)
    hid = jax.nn.silu(jnp.einsum('bnlgd,lde->bnge', blocks, w1))
    return jnp.einsum('bnge,ef->bngf', hid, w2)

def nsa_attention(q, kc, vc, ks, vs, kw, vw, gates):
    Bsz, T = q.shape[0], q.shape[1]
    G, I, D = NSA_KV_GROUPS, NSA_HEADS_PER_GROUP, HEAD_DIM
    n_cmp = kc.shape[1]
    n_sel = T // NSA_SEL_LEN
    k_sel = min(NSA_SEL_TOPK, n_sel)
    scale = HEAD_DIM ** -0.5
    cmp_start = jnp.arange(n_cmp) * NSA_CMP_STRIDE
    cmp_end = cmp_start + NSA_CMP_LEN - 1
    sel_start = jnp.arange(n_sel) * NSA_SEL_LEN
    overlap = ((cmp_start[:, None] < sel_start[None, :] + NSA_SEL_LEN) &
               (cmp_start[:, None] + NSA_CMP_LEN > sel_start[None, :])).astype(jnp.float32)
    ks_blk = ks.reshape(Bsz, n_sel, NSA_SEL_LEN, G, D).transpose(0, 3, 1, 2, 4)
    vs_blk = vs.reshape(Bsz, n_sel, NSA_SEL_LEN, G, D).transpose(0, 3, 1, 2, 4)
    kw_pad = jnp.pad(kw, ((0, 0), (NSA_WINDOW, 0), (0, 0), (0, 0)))
    vw_pad = jnp.pad(vw, ((0, 0), (NSA_WINDOW, 0), (0, 0), (0, 0)))
    b_idx = jnp.arange(Bsz)[:, None, None, None]
    g_idx = jnp.arange(G)[None, :, None, None]
    sel_blocks = jnp.arange(n_sel)

    def block(bi):
        t0 = bi * Q_BLOCK
        t = t0 + jnp.arange(Q_BLOCK)
        qb = lax.dynamic_slice_in_dim(q, t0, Q_BLOCK, axis=1).reshape(Bsz, Q_BLOCK, G, I, D)
        gb = lax.dynamic_slice_in_dim(gates, t0, Q_BLOCK, axis=1).reshape(Bsz, Q_BLOCK, NSA_BRANCHES, G, I)
        s_c = jnp.einsum('bqgid,bngd->bgiqn', qb, kc) * scale
        p_c = masked_softmax(s_c, cmp_end[None, :] <= t[:, None])
        o_c = jnp.einsum('bgiqn,bngd->bqgid', p_c.astype(vc.dtype), vc)
        imp = jnp.einsum('bgiqn,ns->bgqs', p_c, overlap)
        cur = t // NSA_SEL_LEN
        forced = ((sel_blocks[None, :] == 0) | (sel_blocks[None, :] == cur[:, None]) |
                  (sel_blocks[None, :] == cur[:, None] - 1))
        imp = jnp.where(forced, FORCE_SELECT, imp)
        imp = jnp.where(sel_blocks[None, :] <= cur[:, None], imp, NEG_INF)
        _, sel = lax.top_k(imp, k_sel)
        k_g = ks_blk[b_idx, g_idx, sel]
        v_g = vs_blk[b_idx, g_idx, sel]
        kpos = sel[..., None] * NSA_SEL_LEN + jnp.arange(NSA_SEL_LEN)
        mask_s = (kpos <= t[None, None, :, None, None]).reshape(Bsz, G, 1, Q_BLOCK, k_sel * NSA_SEL_LEN)
        s_s = jnp.einsum('bqgid,bgqkld->bgiqkl', qb, k_g).reshape(Bsz, G, I, Q_BLOCK, k_sel * NSA_SEL_LEN) * scale
        p_s = masked_softmax(s_s, mask_s).reshape(Bsz, G, I, Q_BLOCK, k_sel, NSA_SEL_LEN)
        o_s = jnp.einsum('bgiqkl,bgqkld->bqgid', p_s.astype(v_g.dtype), v_g)
        kwb = lax.dynamic_slice_in_dim(kw_pad, t0, Q_BLOCK + NSA_WINDOW, axis=1)
        vwb = lax.dynamic_slice_in_dim(vw_pad, t0, Q_BLOCK + NSA_WINDOW, axis=1)
        wpos = t0 - NSA_WINDOW + jnp.arange(Q_BLOCK + NSA_WINDOW)
        mask_w = ((wpos[None, :] <= t[:, None]) & (wpos[None, :] > t[:, None] - NSA_WINDOW) &
                  (wpos[None, :] >= 0))
        s_w = jnp.einsum('bqgid,bjgd->bgiqj', qb, kwb) * scale
        p_w = masked_softmax(s_w, mask_w)
        o_w = jnp.einsum('bgiqj,bjgd->bqgid', p_w.astype(vwb.dtype), vwb)
        o = (gb[:, :, 0, :, :, None] * o_c + gb[:, :, 1, :, :, None] * o_s +
             gb[:, :, 2, :, :, None] * o_w)
        return o.reshape(Bsz, Q_BLOCK, NSA_Q_W)

    out = lax.map(block, jnp.arange(T // Q_BLOCK))
    return out.transpose(1, 0, 2, 3).reshape(Bsz, T, NSA_Q_W)

def moba_attention(q, k, v):
    Bsz, T, H, D = q.shape
    n_blk = -(-T // MOBA_BLOCK)
    pad = n_blk * MOBA_BLOCK - T
    k_pad = jnp.pad(k, ((0, 0), (0, pad), (0, 0), (0, 0)))
    v_pad = jnp.pad(v, ((0, 0), (0, pad), (0, 0), (0, 0)))
    k_blk = k_pad.reshape(Bsz, n_blk, MOBA_BLOCK, H, D)
    k_mean = jnp.mean(k_blk.astype(jnp.float32), axis=2).astype(k.dtype)
    k_blk = k_blk.transpose(0, 3, 1, 2, 4)
    v_blk = v_pad.reshape(Bsz, n_blk, MOBA_BLOCK, H, D).transpose(0, 3, 1, 2, 4)
    top = max(1, min(MOBA_TOPK, n_blk - 1))
    scale = HEAD_DIM ** -0.5
    b_idx = jnp.arange(Bsz)[:, None, None, None]
    h_idx = jnp.arange(H)[None, :, None, None]
    blocks = jnp.arange(n_blk)

    def block(bi):
        t0 = bi * Q_BLOCK
        t = t0 + jnp.arange(Q_BLOCK)
        cur = t0 // MOBA_BLOCK
        qb = lax.dynamic_slice_in_dim(q, t0, Q_BLOCK, axis=1)
        gate = jnp.einsum('bqhd,bnhd->bhqn', qb, k_mean).astype(jnp.float32)
        gate = jnp.where(blocks < cur, gate, NEG_INF)
        _, sel = lax.top_k(gate, top)
        k_g = k_blk[b_idx, h_idx, sel]
        v_g = v_blk[b_idx, h_idx, sel]
        s_sel = jnp.einsum('bqhd,bhqksd->bhqks', qb, k_g).reshape(Bsz, H, Q_BLOCK, top * MOBA_BLOCK)
        m_sel = jnp.broadcast_to((sel < cur)[..., None],
                                 (Bsz, H, Q_BLOCK, top, MOBA_BLOCK)).reshape(Bsz, H, Q_BLOCK, top * MOBA_BLOCK)
        k_own = lax.dynamic_slice_in_dim(k_pad, cur * MOBA_BLOCK, MOBA_BLOCK, axis=1)
        v_own = lax.dynamic_slice_in_dim(v_pad, cur * MOBA_BLOCK, MOBA_BLOCK, axis=1)
        s_own = jnp.einsum('bqhd,bshd->bhqs', qb, k_own)
        own_pos = cur * MOBA_BLOCK + jnp.arange(MOBA_BLOCK)
        m_own = jnp.broadcast_to(own_pos[None, :] <= t[:, None], (Bsz, H, Q_BLOCK, MOBA_BLOCK))
        p = masked_softmax(jnp.concatenate([s_sel, s_own], axis=-1) * scale,
                           jnp.concatenate([m_sel, m_own], axis=-1)).astype(v.dtype)
        p_sel = p[..., :top * MOBA_BLOCK].reshape(Bsz, H, Q_BLOCK, top, MOBA_BLOCK)
        p_own = p[..., top * MOBA_BLOCK:]
        o = (jnp.einsum('bhqks,bhqksd->bqhd', p_sel, v_g) +
             jnp.einsum('bhqs,bshd->bqhd', p_own, v_own))
        return o.reshape(Bsz, Q_BLOCK, H * D)

    out = lax.map(block, jnp.arange(T // Q_BLOCK))
    return out.transpose(1, 0, 2, 3).reshape(Bsz, T, H * D)

def memory_attention(q, mem_n, w_mem_kv):
    Bsz, T = q.shape[0], q.shape[1]
    k, v = jnp.split(mem_n @ w_mem_kv, 2, axis=-1)
    k = k.reshape(Bsz, -1, MEM_HEADS, HEAD_DIM)
    v = v.reshape(Bsz, -1, MEM_HEADS, HEAD_DIM)
    s = jnp.einsum('bthd,bmhd->bhtm', q, k).astype(jnp.float32) * (HEAD_DIM ** -0.5)
    p = jax.nn.softmax(s, axis=-1).astype(v.dtype)
    return jnp.einsum('bhtm,bmhd->bthd', p, v).reshape(Bsz, T, MEM_W)

def retention(q, k, v):
    Bsz, T, H, _ = q.shape
    C = RET_CHUNK
    NC = T // C
    log_g = jnp.log(1.0 - 2.0 ** (-5.0 - jnp.arange(H, dtype=jnp.float32)))
    i = jnp.arange(C, dtype=jnp.float32)
    diff = i[:, None] - i[None, :]
    decay = jnp.where(diff >= 0, jnp.exp(jnp.maximum(diff, 0.0)[None] * log_g[:, None, None]), 0.0)
    q_decay = jnp.exp((i + 1.0)[None, :] * log_g[:, None])
    k_decay = jnp.exp((C - 1.0 - i)[None, :] * log_g[:, None])
    chunk_decay = jnp.exp(C * log_g)

    def to_chunks(a):
        return a.astype(jnp.float32).reshape(Bsz, NC, C, H, -1).transpose(1, 0, 3, 2, 4)

    def step(state, inp):
        qc, kc, vc = inp
        inner = jnp.einsum('bhid,bhjd->bhij', qc, kc) * decay
        o = (jnp.einsum('bhij,bhjv->bhiv', inner, vc) +
             jnp.einsum('bhid,bhdv->bhiv', qc, state) * q_decay[None, :, :, None])
        state = (state * chunk_decay[None, :, None, None] +
                 jnp.einsum('bhjd,bhjv->bhdv', kc * k_decay[None, :, :, None], vc))
        return state, o

    state0 = jnp.zeros((Bsz, H, q.shape[-1], v.shape[-1]), jnp.float32)
    _, o = lax.scan(step, state0, (to_chunks(q), to_chunks(k), to_chunks(v)))
    return o.transpose(1, 0, 3, 2, 4).reshape(Bsz, T, H, v.shape[-1])

def head_group_norm(o):
    mu = jnp.mean(o, axis=-1, keepdims=True)
    var = jnp.mean(jnp.square(o - mu), axis=-1, keepdims=True)
    return (o - mu) * lax.rsqrt(var + NORM_EPS)

def even_layer(x, mem_n, cos, sin, norm_g, w_in, gate_b, pe_k, w1_k, w2_k, pe_v, w1_v, w2_v, w_mem_kv, w_out):
    Bsz, T, _ = x.shape
    h = rms_norm(x, norm_g)
    (nq, nkc, nvc, nks, nvs, nkw, nvw, ng, nz, mq, mk, mv, mz, eq, ez) = _split(h @ w_in, EVEN_SPLITS)

    def heads(a):
        return a.reshape(Bsz, T, -1, HEAD_DIM)

    def rot(a):
        return apply_rotary(heads(a), cos, sin)

    kc = nsa_compress(rot(nkc), pe_k, w1_k, w2_k)
    vc = nsa_compress(heads(nvc), pe_v, w1_v, w2_v)
    gates = jax.nn.sigmoid(ng + gate_b).reshape(Bsz, T, NSA_BRANCHES, NSA_HEADS)
    a_out = nsa_attention(rot(nq), kc, vc, rot(nks), heads(nvs), rot(nkw), heads(nvw), gates)
    b_out = moba_attention(rot(mq), rot(mk), heads(mv))
    m_out = memory_attention(heads(eq), mem_n, w_mem_kv)
    y = jnp.concatenate([a_out * jax.nn.silu(nz), b_out * jax.nn.silu(mz),
                         m_out * jax.nn.silu(ez)], axis=-1) @ w_out
    return x + y

def odd_layer(x, mem_n, rcos, rsin, norm_g, w_in, w_mem_kv, w_out):
    Bsz, T, _ = x.shape
    h = rms_norm(x, norm_g)
    rq, rk, rv, rz, eq, ez = _split(h @ w_in, ODD_SPLITS)
    q = apply_rotary(rq.reshape(Bsz, T, RET_HEADS, RET_QK_DIM), rcos, rsin)
    k = apply_rotary(rk.reshape(Bsz, T, RET_HEADS, RET_QK_DIM), rcos, rsin) * (RET_QK_DIM ** -0.5)
    v = rv.reshape(Bsz, T, RET_HEADS, RET_V_DIM)
    r_out = head_group_norm(retention(q, k, v)).reshape(Bsz, T, RET_V_W).astype(x.dtype)
    m_out = memory_attention(eq.reshape(Bsz, T, MEM_HEADS, HEAD_DIM), mem_n, w_mem_kv)
    y = jnp.concatenate([r_out * jax.nn.silu(rz), m_out * jax.nn.silu(ez)], axis=-1) @ w_out
    return x + y

def first_inputs(seed: int = 0) -> dict:
    key = jax.random.key(seed)
    ks = jax.random.split(key, 24)

    def nrm(k, shape, scale):
        return jax.random.normal(k, shape, jnp.float32) * scale

    def gain(k):
        return 1.0 + nrm(k, (D_MODEL,), 0.02)

    x = nrm(ks[0], (BATCH, SEQ, D_MODEL), 1.0)
    mem = nrm(ks[1], (BATCH, MEM_LEN, D_MODEL), 1.0)
    positions = jnp.broadcast_to(jnp.arange(SEQ, dtype=jnp.int32)[None, :], (BATCH, SEQ))
    cmp_in = NSA_CMP_LEN * HEAD_DIM
    return {
        'x': x,
        'mem': mem,
        'positions': positions,
        'l0_norm_g': gain(ks[2]),
        'l0_w_in': nrm(ks[3], (D_MODEL, EVEN_IN_W), D_MODEL ** -0.5),
        'l0_nsa_gate_b': nrm(ks[4], (NSA_BRANCHES * NSA_HEADS,), 0.1),
        'l0_cmp_pe_k': nrm(ks[5], (NSA_CMP_LEN, HEAD_DIM), 0.1),
        'l0_cmp_w1_k': nrm(ks[6], (NSA_CMP_LEN, HEAD_DIM, HEAD_DIM), cmp_in ** -0.5),
        'l0_cmp_w2_k': nrm(ks[7], (HEAD_DIM, HEAD_DIM), HEAD_DIM ** -0.5),
        'l0_cmp_pe_v': nrm(ks[8], (NSA_CMP_LEN, HEAD_DIM), 0.1),
        'l0_cmp_w1_v': nrm(ks[9], (NSA_CMP_LEN, HEAD_DIM, HEAD_DIM), cmp_in ** -0.5),
        'l0_cmp_w2_v': nrm(ks[10], (HEAD_DIM, HEAD_DIM), HEAD_DIM ** -0.5),
        'l0_w_mem_kv': nrm(ks[11], (D_MODEL, 2 * MEM_W), D_MODEL ** -0.5),
        'l0_w_out': nrm(ks[12], (EVEN_OUT_W, D_MODEL), EVEN_OUT_W ** -0.5),
        'l1_norm_g': gain(ks[13]),
        'l1_w_in': nrm(ks[14], (D_MODEL, ODD_IN_W), D_MODEL ** -0.5),
        'l1_w_mem_kv': nrm(ks[15], (D_MODEL, 2 * MEM_W), D_MODEL ** -0.5),
        'l1_w_out': nrm(ks[16], (ODD_OUT_W, D_MODEL), ODD_OUT_W ** -0.5),
        'mem_norm_g': gain(ks[17]),
        'final_norm_g': gain(ks[18]),
    }

def first_block(x, mem, positions, l0_norm_g, l0_w_in, l0_nsa_gate_b, l0_cmp_pe_k, l0_cmp_w1_k, l0_cmp_w2_k,
              l0_cmp_pe_v, l0_cmp_w1_v, l0_cmp_w2_v, l0_w_mem_kv, l0_w_out,
              l1_norm_g, l1_w_in, l1_w_mem_kv, l1_w_out, mem_norm_g, final_norm_g):
    attn_inv = 1.0 / (ROPE_THETA ** (jnp.arange(0, HEAD_DIM, 2, dtype=jnp.float32) / HEAD_DIM))
    ret_inv = 1.0 / (ROPE_THETA ** jnp.linspace(0.0, 1.0, RET_QK_DIM // 2, dtype=jnp.float32))
    cos, sin = rotary_tables(positions, attn_inv)
    rcos, rsin = rotary_tables(positions, ret_inv)
    mem_n = rms_norm(mem, mem_norm_g)
    layer_params = (
        (l0_norm_g, l0_w_in, l0_nsa_gate_b, l0_cmp_pe_k, l0_cmp_w1_k, l0_cmp_w2_k,
         l0_cmp_pe_v, l0_cmp_w1_v, l0_cmp_w2_v, l0_w_mem_kv, l0_w_out),
        (l1_norm_g, l1_w_in, l1_w_mem_kv, l1_w_out),
    )
    for layer in range(DEPTH):
        if layer % 2 == 0:
            x = even_layer(x, mem_n, cos, sin, *layer_params[layer])
        else:
            x = odd_layer(x, mem_n, rcos, rsin, *layer_params[layer])
    return rms_norm(x, final_norm_g)


DEPTH_2 = 1

ATT_HEADS = 8
ATT_KV_HEADS = 2
ATT_HEAD_DIM = 64
ATT_GROUP = ATT_HEADS // ATT_KV_HEADS
ATT_Q_DIM = ATT_HEADS * ATT_HEAD_DIM
ATT_KV_DIM = ATT_KV_HEADS * ATT_HEAD_DIM
WINDOW = 128
ATT_BLOCK = 128
ROPE_DIM = ATT_HEAD_DIM // 4
ROPE_THETA_2 = 500000.0

GLA_HEADS = 4
GLA_KEY_DIM = D_MODEL // 2
GLA_VAL_DIM = D_MODEL
GLA_DK = GLA_KEY_DIM // GLA_HEADS
GLA_DV = GLA_VAL_DIM // GLA_HEADS
GLA_GATE_RANK = 16
GLA_GATE_NORM = 16.0
GLA_CHUNK = 64

N_EXPERTS = 16
EXPERT_FF = D_MODEL
CAPACITY_FACTOR = 2

PLE_DIM = 256

EPS = 1e-6

IN_SIZES = (ATT_Q_DIM, ATT_KV_DIM, ATT_KV_DIM,
            GLA_KEY_DIM, GLA_KEY_DIM, GLA_VAL_DIM, GLA_VAL_DIM,
            GLA_GATE_RANK, GLA_GATE_RANK, D_MODEL, D_MODEL)
IN_DIM = ATT_Q_DIM + 2 * ATT_KV_DIM + 2 * GLA_KEY_DIM + 2 * GLA_VAL_DIM + 2 * GLA_GATE_RANK + 2 * D_MODEL


def rmsnorm(x, g):
    xf = x.astype(jnp.float32)
    y = xf * lax.rsqrt(jnp.mean(xf * xf, axis=-1, keepdims=True) + EPS)
    return (y * g.astype(jnp.float32)).astype(x.dtype)

def split_columns(proj):
    parts, start = [], 0
    for size in IN_SIZES:
        parts.append(proj[..., start:start + size])
        start += size
    return parts

def partial_rope(t, positions):
    half = ROPE_DIM // 2
    inv_freq = ROPE_THETA_2 ** (-jnp.arange(0, ROPE_DIM, 2, dtype=jnp.float32) / ROPE_DIM)
    ang = positions.astype(jnp.float32)[..., None] * inv_freq
    cos = jnp.cos(ang)[:, :, None, :].astype(t.dtype)
    sin = jnp.sin(ang)[:, :, None, :].astype(t.dtype)
    t1 = t[..., :half]
    t2 = t[..., half:ROPE_DIM]
    rot = jnp.concatenate([t1 * cos - t2 * sin, t2 * cos + t1 * sin], axis=-1)
    return jnp.concatenate([rot, t[..., ROPE_DIM:]], axis=-1)

def windowed_gqa(q, k, v, sink):
    B, S = q.shape[0], q.shape[1]
    nb = S // ATT_BLOCK
    qb = q.reshape(B, nb, ATT_BLOCK, ATT_KV_HEADS, ATT_GROUP, ATT_HEAD_DIM)

    def band(t):
        tp = jnp.pad(t, ((0, 0), (ATT_BLOCK, ATT_BLOCK), (0, 0), (0, 0)))
        tp = tp.reshape(B, nb + 2, ATT_BLOCK, ATT_KV_HEADS, ATT_HEAD_DIM)
        return jnp.concatenate([tp[:, :-2], tp[:, 1:-1], tp[:, 2:]], axis=2)

    kb, vb = band(k), band(v)
    scores = jnp.einsum('bnqhgd,bnkhd->bnhgqk', qb, kb).astype(jnp.float32) * (ATT_HEAD_DIM ** -0.5)
    blk = jnp.arange(nb)[:, None, None]
    qi = blk * ATT_BLOCK + jnp.arange(ATT_BLOCK)[None, :, None]
    kj = (blk - 1) * ATT_BLOCK + jnp.arange(3 * ATT_BLOCK)[None, None, :]
    valid = (jnp.abs(qi - kj) <= WINDOW) & (kj >= 0) & (kj < S)
    scores = jnp.where(valid[None, :, None, None], scores, -jnp.inf)
    sink_b = sink.astype(jnp.float32).reshape(1, 1, ATT_KV_HEADS, ATT_GROUP, 1, 1)
    m = jnp.maximum(jnp.max(scores, axis=-1, keepdims=True), sink_b)
    e = jnp.exp(scores - m)
    probs = e / (jnp.sum(e, axis=-1, keepdims=True) + jnp.exp(sink_b - m))
    out = jnp.einsum('bnhgqk,bnkhd->bnqhgd', probs.astype(v.dtype), vb)
    return out.reshape(B, S, ATT_Q_DIM)

def gla_chunked(q, k, v, log_a, strict):
    B, S, H, dk = q.shape
    dv = v.shape[-1]
    nc = S // GLA_CHUNK

    def chunk(t):
        return t.reshape(B, nc, GLA_CHUNK, H, t.shape[-1])

    qc, kc, vc, ac = chunk(q), chunk(k), chunk(v), chunk(log_a)
    b = jnp.cumsum(ac, axis=2)
    g = b[:, :, -1]
    q_t = qc * jnp.exp(b)
    k_t = kc * jnp.exp(-b)
    k_end = kc * jnp.exp(g[:, :, None] - b)
    attn = jnp.einsum('bclhd,bcmhd->bchlm', q_t, k_t)
    mask = jnp.tril(jnp.ones((GLA_CHUNK, GLA_CHUNK), dtype=bool), -1 if strict else 0)
    attn = jnp.where(mask, attn, 0.0)
    o_intra = jnp.einsum('bchlm,bcmhe->bclhe', attn, vc)
    kv = jnp.einsum('bclhd,bclhe->bchde', k_end, vc)
    decay = jnp.exp(g)

    def step(state, xs):
        dec, kv_c = xs
        return dec[..., None] * state + kv_c, state

    s0 = jnp.zeros((B, H, dk, dv), dtype=jnp.float32)
    _, s_prev = lax.scan(step, s0, (jnp.moveaxis(decay, 1, 0), jnp.moveaxis(kv, 1, 0)))
    s_prev = jnp.moveaxis(s_prev, 0, 1)
    o_inter = jnp.einsum('bclhd,bchde->bclhe', q_t, s_prev)
    return (o_intra + o_inter).reshape(B, S, H, dv)

def gla_branch(gq, gk, gv, gr, z_f, z_b, up_f, bias_f, up_b, bias_b, norm_gain):
    B, S = gq.shape[0], gq.shape[1]
    f32 = jnp.float32
    q = gq.astype(f32).reshape(B, S, GLA_HEADS, GLA_DK) * (GLA_DK ** -0.5)
    k = gk.astype(f32).reshape(B, S, GLA_HEADS, GLA_DK)
    v = gv.astype(f32).reshape(B, S, GLA_HEADS, GLA_DV)
    la_f = (jax.nn.log_sigmoid(z_f.astype(f32) @ up_f.astype(f32) + bias_f.astype(f32)) / GLA_GATE_NORM).reshape(B, S, GLA_HEADS, GLA_DK)
    la_b = (jax.nn.log_sigmoid(z_b.astype(f32) @ up_b.astype(f32) + bias_b.astype(f32)) / GLA_GATE_NORM).reshape(B, S, GLA_HEADS, GLA_DK)
    o_f = gla_chunked(q, k, v, la_f, strict=False)
    flip = lambda t: jnp.flip(t, axis=1)
    o_b = flip(gla_chunked(flip(q), flip(k), flip(v), flip(la_b), strict=True))
    o = o_f + o_b
    o = o * lax.rsqrt(jnp.mean(o * o, axis=-1, keepdims=True) + EPS) * norm_gain.astype(f32).reshape(GLA_HEADS, GLA_DV)
    o = o.reshape(B, S, GLA_VAL_DIM) * jax.nn.silu(gr.astype(f32))
    return o.astype(gq.dtype)

def expert_choice_ffn(xn, w_router, w_gate, w_up, w_down):
    B, S, D = xn.shape
    cap = CAPACITY_FACTOR * S // N_EXPERTS
    aff = jax.nn.softmax(jnp.einsum('bsd,de->bse', xn, w_router).astype(jnp.float32), axis=-1)
    top_aff, top_idx = lax.top_k(jnp.swapaxes(aff, 1, 2), cap)
    bidx = jnp.arange(B)[:, None, None]
    xg = xn[bidx, top_idx]
    hid = jax.nn.silu(jnp.einsum('becd,edf->becf', xg, w_gate)) * jnp.einsum('becd,edf->becf', xg, w_up)
    y = jnp.einsum('becf,efd->becd', hid, w_down) * top_aff[..., None].astype(xn.dtype)
    return jnp.zeros((B, S, D), dtype=y.dtype).at[bidx, top_idx].add(y)

def second_inputs(seed: int = 0) -> dict:
    key = jax.random.key(seed)
    ks = jax.random.split(key, 32)
    f32 = jnp.float32
    L, D = DEPTH_2, D_MODEL

    def w(k, shape, fan_in):
        return jax.random.normal(k, shape, f32) * (fan_in ** -0.5)

    def gain(k, shape):
        return 1.0 + 0.1 * jax.random.normal(k, shape, f32)

    x = jax.random.normal(ks[0], (BATCH, SEQ, D), f32)
    p = jax.random.normal(ks[1], (L, BATCH, SEQ, PLE_DIM), f32)
    offsets = jax.random.randint(ks[2], (BATCH, 1), 0, 1024, dtype=jnp.int32)
    positions = jnp.arange(SEQ, dtype=jnp.int32)[None, :] + offsets
    return {
        "x": x,
        "p": p,
        "positions": positions,
        "norm_mix": gain(ks[3], (L, D)),
        "w_in": w(ks[4], (L, D, IN_DIM), D),
        "gla_gate_up_fwd": w(ks[5], (L, GLA_GATE_RANK, GLA_KEY_DIM), GLA_GATE_RANK),
        "gla_gate_bias_fwd": 1.0 + 0.5 * jax.random.normal(ks[6], (L, GLA_KEY_DIM), f32),
        "gla_gate_up_bwd": w(ks[7], (L, GLA_GATE_RANK, GLA_KEY_DIM), GLA_GATE_RANK),
        "gla_gate_bias_bwd": 1.0 + 0.5 * jax.random.normal(ks[8], (L, GLA_KEY_DIM), f32),
        "attn_sink": 0.5 * jax.random.normal(ks[9], (L, ATT_HEADS), f32),
        "gla_norm": gain(ks[10], (L, GLA_VAL_DIM)),
        "w_branch_attn": w(ks[11], (L, ATT_Q_DIM, D), ATT_Q_DIM),
        "w_branch_gla": w(ks[12], (L, GLA_VAL_DIM, D), GLA_VAL_DIM),
        "w_out": w(ks[13], (L, D, D), D),
        "norm_ffn": gain(ks[14], (L, D)),
        "w_router": w(ks[15], (L, D, N_EXPERTS), D),
        "w_exp_gate": w(ks[16], (L, N_EXPERTS, D, EXPERT_FF), D),
        "w_exp_up": w(ks[17], (L, N_EXPERTS, D, EXPERT_FF), D),
        "w_exp_down": w(ks[18], (L, N_EXPERTS, EXPERT_FF, D), EXPERT_FF),
        "norm_ple": gain(ks[19], (L, D)),
        "w_ple_gate": w(ks[20], (L, D, D), D),
        "w_ple": w(ks[21], (L, PLE_DIM, D), PLE_DIM),
        "norm_final": gain(ks[22], (D,)),
    }

def second_block(x, p, positions, norm_mix, w_in, gla_gate_up_fwd, gla_gate_bias_fwd,
              gla_gate_up_bwd, gla_gate_bias_bwd, attn_sink, gla_norm, w_branch_attn,
              w_branch_gla, w_out, norm_ffn, w_router, w_exp_gate, w_exp_up, w_exp_down,
              norm_ple, w_ple_gate, w_ple, norm_final):
    B, S, _ = x.shape
    h = x
    for l in range(DEPTH_2):
        a = rmsnorm(h, norm_mix[l])
        proj = a @ w_in[l]
        aq, ak, av, gq, gk, gv, gr, z_f, z_b, g_att, g_gla = split_columns(proj)
        aq = partial_rope(aq.reshape(B, S, ATT_HEADS, ATT_HEAD_DIM), positions)
        ak = partial_rope(ak.reshape(B, S, ATT_KV_HEADS, ATT_HEAD_DIM), positions)
        av = av.reshape(B, S, ATT_KV_HEADS, ATT_HEAD_DIM)
        y_att = windowed_gqa(aq, ak, av, attn_sink[l]) @ w_branch_attn[l]
        y_gla = gla_branch(gq, gk, gv, gr, z_f, z_b,
                           gla_gate_up_fwd[l], gla_gate_bias_fwd[l],
                           gla_gate_up_bwd[l], gla_gate_bias_bwd[l], gla_norm[l]) @ w_branch_gla[l]
        merged = jax.nn.sigmoid(g_att) * y_att + jax.nn.sigmoid(g_gla) * y_gla
        h = h + merged @ w_out[l]
        h = h + expert_choice_ffn(rmsnorm(h, norm_ffn[l]), w_router[l],
                                  w_exp_gate[l], w_exp_up[l], w_exp_down[l])
        ple_gate = jax.nn.sigmoid(rmsnorm(h, norm_ple[l]) @ w_ple_gate[l])
        h = h + ple_gate * (p[l] @ w_ple[l])
    return rmsnorm(h, norm_final)


def setup_inputs(seed=0):
    out = dict(first_inputs(seed))
    for name, value in second_inputs(seed + 1).items():
        if name != "x":
            out[name + "_2"] = value
    return out


def reference(
    x, mem, positions, l0_norm_g, l0_w_in, l0_nsa_gate_b, l0_cmp_pe_k, l0_cmp_w1_k, l0_cmp_w2_k,
    l0_cmp_pe_v, l0_cmp_w1_v, l0_cmp_w2_v, l0_w_mem_kv, l0_w_out, l1_norm_g, l1_w_in,
    l1_w_mem_kv, l1_w_out, mem_norm_g, final_norm_g, p_2, positions_2, norm_mix_2, w_in_2,
    gla_gate_up_fwd_2, gla_gate_bias_fwd_2, gla_gate_up_bwd_2, gla_gate_bias_bwd_2, attn_sink_2,
    gla_norm_2, w_branch_attn_2, w_branch_gla_2, w_out_2, norm_ffn_2, w_router_2, w_exp_gate_2,
    w_exp_up_2, w_exp_down_2, norm_ple_2, w_ple_gate_2, w_ple_2, norm_final_2,
):
    x = first_block(
        x, mem, positions, l0_norm_g, l0_w_in, l0_nsa_gate_b, l0_cmp_pe_k, l0_cmp_w1_k,
        l0_cmp_w2_k, l0_cmp_pe_v, l0_cmp_w1_v, l0_cmp_w2_v, l0_w_mem_kv, l0_w_out, l1_norm_g,
        l1_w_in, l1_w_mem_kv, l1_w_out, mem_norm_g, final_norm_g,
    )
    return second_block(
        x, p_2, positions_2, norm_mix_2, w_in_2, gla_gate_up_fwd_2, gla_gate_bias_fwd_2,
        gla_gate_up_bwd_2, gla_gate_bias_bwd_2, attn_sink_2, gla_norm_2, w_branch_attn_2,
        w_branch_gla_2, w_out_2, norm_ffn_2, w_router_2, w_exp_gate_2, w_exp_up_2, w_exp_down_2,
        norm_ple_2, w_ple_gate_2, w_ple_2, norm_final_2,
    )


_drawn_inputs = setup_inputs


def setup_inputs(seed=0):
    import zlib

    import numpy as np

    out = dict(_drawn_inputs(seed))
    spreads = {}
    factors = {'l0_norm_g': 6.254,
     'l0_nsa_gate_b': 6.514,
     'l0_cmp_pe_k': 8.0,
     'l0_cmp_pe_v': 9.9,
     'mem_norm_g': 8.0,
     'attn_sink_2': 64.0,
     'norm_ple_2': 2.945,
     'l1_norm_g': 8.0}
    for name, (base, spread) in spreads.items():
        noise = np.random.default_rng([zlib.crc32(name.encode()), seed]).standard_normal(out[name].shape)
        drawn = base * np.exp(spread * noise) if base else spread * noise
        out[name] = jnp.asarray(drawn.astype(out[name].dtype))
    for name, factor in factors.items():
        out[name] = (out[name] * factor).astype(out[name].dtype)
    return out
```

```python
from contextlib import ExitStack

import numpy as np
import concourse.bass as bass
from concourse import mybir

F32 = mybir.dt.float32
I32 = mybir.dt.int32
ALU = mybir.AluOpType
ACT = mybir.ActivationFunctionType
AX = mybir.AxisListType

P = 128
T = 512
TT = T // P
D = 1024
KD = D // P
MEM = 256
HD = 64
NEG = -1.0e30
EPS = 1e-6
RING = 3
SLOT = 4096
NE = 16
CAP = 64
RH = 4

CONST = {}
VEC = {}


def _place(table, parts):
    at = 0
    for name, width in parts:
        table[name] = (at, width)
        at += width
    return at


NCONST = _place(CONST, [
    ("ident", P), ("ones", P), ("causal", P), ("behind", P), ("rot", P), ("rot2", P),
    ("inv", 1), ("inv2", 1), ("invr", 1), ("one", 1), ("slot", 1), ("slots", CAP),
    ("cmp01", TT * 32), ("cmpneg", TT * 32), ("scan", T), ("fwd", P), ("bwd", P),
])
NVEC = _place(VEC, [
    ("g_l0", KD), ("g_mem", KD), ("g_l1", KD), ("g_fin", KD), ("g_mix", KD), ("g_ffn", KD), ("g_ple", KD),
    ("g_last", KD), ("g_gla", KD), ("nsa_b", 24), ("sink", 8), ("bias_f", 4), ("bias_b", 4),
    ("pe_k", 32), ("pe_v", 32),
])


def shape_constants():
    f = np.float32
    c = np.zeros((P, NCONST), f)

    def put(name, value):
        at, width = CONST[name]
        c[:, at:at + width] = np.asarray(value, f).reshape(-1, width)

    r, q = np.arange(P)[:, None], np.arange(P)[None, :]
    put("ident", r == q)
    put("ones", np.ones((P, P)))
    put("causal", np.where(q <= r, 0.0, NEG))
    put("behind", np.where(q >= r, 0.0, NEG))
    rot = np.zeros((P, P))
    rot2 = np.zeros((P, P))
    for m in range(P):
        d = m % HD
        rot[m + 32 if d < 32 else m - 32, m] = -1.0 if d < 32 else 1.0
        if d < 16:
            rot2[m + 8 if d < 8 else m - 8, m] = -1.0 if d < 8 else 1.0
    put("rot", rot)
    put("rot2", rot2)
    inv = f(1.0) / (f(10000.0) ** (np.arange(0, HD, 2, dtype=f) / f(HD)))
    put("inv", np.tile(inv, 4)[:, None])
    inv2 = f(500000.0) ** (-np.arange(0, 16, 2, dtype=f) / f(16))
    put("inv2", np.tile(np.concatenate([inv2, inv2, np.zeros(48, f)]), 2)[:, None])
    put("invr", (f(1.0) / (f(10000.0) ** np.linspace(0.0, 1.0, P, dtype=f)))[:, None])
    put("one", np.ones((P, 1)))
    put("slot", (np.arange(P) % CAP + 1)[:, None])
    put("slots", np.tile(np.arange(CAP) + 1, (P, 1)))
    t = np.arange(T)
    seen = (np.arange(32)[None, :] * 16 + 31 <= t[:, None]) & (np.arange(32)[None, :] < 31)
    seen = seen.reshape(TT, P, 32).transpose(1, 0, 2).reshape(P, TT * 32)
    put("cmp01", seen)
    put("cmpneg", np.where(seen, 0.0, NEG))
    put("scan", np.tile(t % 64 != 0, (P, 1)))
    same = r // 64 == q // 64
    put("fwd", same & (q >= r))
    put("bwd", same & (q < r))
    log_g = np.log(1.0 - 2.0 ** (-5.0 - np.arange(RH)))
    diff = t[None, None, :] - np.arange(P)[:, None, None]
    decay = np.where(diff >= 0, np.exp(np.maximum(diff, 0) * log_g[None, :, None]), 0.0) / 16.0

    pick = np.zeros((P, KD, P))
    for k in range(KD):
        for m in range(P):
            pick[2 * k + m // CAP, k, m] = 1.0
    return c, decay.reshape(P, RH * T).astype(f), pick.reshape(P, KD * P).astype(f)[:NE]


def build(nc, a, out):
    es = ExitStack()
    with es:
        live = es


        uses = {}

        def sb(name, shape, dt=F32, ctx=None):
            uses[name] = uses.get(name, 0) + 1
            name = name if uses[name] == 1 else f"{name}_{uses[name]}"
            return (ctx or live).enter_context(nc.sbuf_tensor(name, shape, dt))

        def sem(name):
            return es.enter_context(nc.semaphore(name))

        bank = [es.enter_context(nc.psum_tensor(f"bank{i}", [P, 512], F32)) for i in range(8)]
        cst = sb("cst", [P, NCONST])
        vec = sb("vec", [P, NVEC])
        ring = [sb(f"ring{i}", [P, SLOT]) for i in range(RING)]
        xT = sb("xT", [P, KD, T])

        def con(name, i=None, n=None):
            at, width = CONST[name]
            if i is not None:
                at, width = at + i * n, n
            return cst[:, at:at + width]

        def par(name, i=None):
            at, width = VEC[name]
            return vec[:, at:at + width] if i is None else vec[:, at + i:at + i + 1]

        ident = con("ident")
        ones = con("ones")

        small_loaded = sem("small_loaded")
        stored = sem("stored")
        w_loaded = [sem(f"w_loaded{i}") for i in range(RING)]
        tiles_done = sem("tiles_done")
        act_evac = sem("act_evac")
        dve_evac = sem("dve_evac")
        act_self = sem("act_self")
        dve_self = sem("dve_self")
        pool_self = sem("pool_self")
        pe_self = sem("pe_self")
        counts = {"tiles": 0, "act": 0, "dve": 0}

        class Own:
            def __init__(self, s):
                self.s, self.n = s, 0

            def __call__(self, ins):
                self.n += 1
                ins.then_inc(self.s, 1)
                return self.n

            def wait(self, eng, n=None):
                if (n or self.n) > 0:
                    eng.wait_ge(self.s, n or self.n)

        actq, dveq, poolq, peq = Own(act_self), Own(dve_self), Own(pool_self), Own(pe_self)

        stream = []
        last_tile = {}
        issued = [0]

        def add_block(w, rows, c0, n):
            kt = rows // P
            assert kt * n <= SLOT
            stream.append((w[:, c0:c0 + n].rearrange("(k p) n -> p k n", p=P), kt, n))
            return len(stream) - 1

        def block_ap(j):
            _, kt, n = stream[j]
            return ring[j % RING][:, 0:kt * n].rearrange("p (k n) -> p k n", k=kt)

        EVEN = {}
        w = a["l0_w_in"]
        for name, c0, n in [("nq", 0, 512), ("kv1", 512, 512), ("kv2", 1024, 280), ("nz", 1304, 512),
                            ("mq", 1816, 512), ("mk", 2328, 512), ("mv", 2840, 512), ("mz", 3352, 512),
                            ("e", 3864, 512)]:
            EVEN[name] = add_block(w, D, c0, n)
        MK0 = add_block(a["l0_w_mem_kv"], D, 0, 512)
        MK1 = add_block(a["l1_w_mem_kv"], D, 0, 512)
        w = a["l0_w_out"]
        WO0 = []
        for c in range(4):
            WO0.append(len(stream))
            stream.append((w[:, c * 256:(c + 1) * 256], 10, 256))
        ODD = [add_block(a["l1_w_in"], D, c * 512, 512) for c in range(13)]
        WO1 = [add_block(a["l1_w_out"], 18 * P, c * 128, 128) for c in range(8)]
        W2 = {}
        w = a["w_in_2"][0]
        for name, c0, n in [("aq", 0, 512), ("akv", 512, 256), ("gq", 768, 512), ("gk", 1280, 512),
                            ("gv0", 1792, 512), ("gv1", 2304, 512), ("gr0", 2816, 512), ("gr1", 3328, 512),
                            ("z", 3840, 32), ("ga0", 3872, 512), ("ga1", 4384, 512), ("gg0", 4896, 512),
                            ("gg1", 5408, 512)]:
            W2[name] = add_block(w, D, c0, n)
        WBA = len(stream)
        stream.append((a["w_branch_attn_2"][0], 4, 1024))
        WBG = [add_block(a["w_branch_gla_2"][0], D, c * 512, 512) for c in range(2)]
        WO2 = [add_block(a["w_out_2"][0], D, c * 512, 512) for c in range(2)]
        EXP = []
        for p in range(NE // 2):
            blocks = []
            for n in range(2):
                for w in ("w_exp_gate_2", "w_exp_up_2"):
                    for e in range(2):
                        blocks.append(add_block(a[w][0, 2 * p + e], D, n * 512, 512))
            for n in range(2):
                for e in range(2):
                    blocks.append(add_block(a["w_exp_down_2"][0, 2 * p + e], D, n * 512, 512))
            EXP.append(blocks)
        WPG = [add_block(a["w_ple_gate_2"][0], D, c * 512, 512) for c in range(2)]
        WPL = add_block(a["w_ple_2"][0], 256, 0, 1024)

        def load_special(sp, j):
            dst = block_ap(j)
            view, kt, n = stream[j]
            s = w_loaded[j % RING]
            if j in paired:
                for g in range(2):
                    for k in range(kt):
                        sp.dma_start(dst[:, k, :].rearrange("p (i g d) -> p g i d", g=2, i=4)[:, g],
                                     view[:, k, :].rearrange("p (g i d) -> p g i d", g=2, i=4)[:, g]).then_inc(s, 16)
                return
            pairs = view[0:512, :].rearrange("(g i d) n -> g d i n", g=2, i=4)
            for g in range(2):
                sp.dma_start(dst[g * 64:(g + 1) * 64, 0:4, :], pairs[g]).then_inc(s, 16)
            if kt > 4:
                sp.dma_start(dst[:, 4:kt, :], view[512:kt * P, :].rearrange("(k p) n -> p k n", p=P)).then_inc(s, 16)

        paired = {EVEN["nq"], EVEN["nz"], W2["aq"]}
        special = set(WO0) | {WBA} | paired
        loads_of = {}
        level = [0] * RING
        for j in range(len(stream)):
            level[j % RING] += 16 * (1 if j not in special else (3 if j in WO0 else 16 if j in paired else 2))
            loads_of[j] = level[j % RING]

        def issue_blocks(sp, upto):
            while issued[0] < min(upto, len(stream)):
                j = issued[0]
                if j >= RING:
                    sp.wait_ge(tiles_done, last_tile[j - RING])
                if j in special:
                    load_special(sp, j)
                else:
                    sp.dma_start(block_ap(j), stream[j][0]).then_inc(w_loaded[j % RING], 16)
                issued[0] += 1

        def wait_block(pe, j):
            pe.wait_ge(w_loaded[j % RING], loads_of[j])

        def run_products(jobs, banks=6, extra=None):
            t0, a0, d0 = counts["tiles"], counts["act"], counts["dve"]
            done_at = []
            na, nd = a0, d0
            for n, job in enumerate(jobs):
                if job["eng"] == "act":
                    na += 1
                    done_at.append((act_evac, na))
                else:
                    nd += 1
                    done_at.append((dve_evac, nd))
                if job.get("block") is not None:
                    last_tile[job["block"]] = t0 + n + 1
            used = [j["block"] for j in jobs if j.get("block") is not None]
            with nc.Block() as block:
                @block.sync
                def _(sp):
                    if used:
                        issue_blocks(sp, max(used) + RING + 1)

                @block.tensor
                def _(pe):
                    waited = set()
                    for n, job in enumerate(jobs):
                        if job.get("block") is not None and job["block"] not in waited:
                            waited.add(job["block"])
                            wait_block(pe, job["block"])
                        if n >= banks:
                            pe.wait_ge(*done_at[n - banks])
                        if job.get("after") is not None:
                            pe.wait_ge(*done_at[job["after"]])
                        o = job["out"](bank[n % banks])
                        mats = job["mats"]
                        for i, (l, r) in enumerate(mats):
                            mm = pe.matmul(o, l, r, start=i == 0, stop=i == len(mats) - 1)
                        mm.then_inc(tiles_done, 1)

                def taker(kind, own, s):
                    def body(eng):
                        last = None
                        for n, job in enumerate(jobs):
                            if job["eng"] == kind:
                                if last is not None and kind == "dve":
                                    eng.wait_ge(*last)
                                last = done_at[n]
                                eng.wait_ge(tiles_done, t0 + n + 1)
                                if job.get("with") is not None:
                                    eng.wait_ge(*done_at[job["with"]])
                                job["evac"](eng, job["out"](bank[n % banks]), own).then_inc(s, 1)
                    return body

                block.scalar(taker("act", actq, act_evac))
                block.vector(taker("dve", dveq, dve_evac))
            counts["tiles"] += len(jobs)
            counts["act"], counts["dve"] = na, nd

        def whole(b):
            return b[:, :]

        def to(dst, func=None, scale=1.0):
            def evac(eng, ps, own):
                if eng is nc.scalar or own is actq:
                    return eng.activation(dst, ps, func or ACT.Copy, scale=scale)
                if scale != 1.0:
                    return eng.tensor_scalar(dst, ps, scale, None, ALU.mult)
                return eng.tensor_copy(dst, ps)
            return evac

        def fm_mats(j, c, src, n=P, kt=KD):
            wb = block_ap(j)
            return [(wb[:, k, c:c + n], src[:, k, :]) for k in range(kt)]

        def tm_mats(j, c, n, src, t, kt=KD):
            wb = block_ap(j)
            return [(src[:, k, t * P:(t + 1) * P], wb[:, k, c:c + n]) for k in range(kt)]

        def norm(x, h, gain, n, kt=KD, width=D):
            st = ExitStack()
            with st:
                rs = sb("norm_rs", [P, n], ctx=st)
                ps = bank[0][:, 0:n]
                a1, p1, d1 = actq.n, peq.n, dveq.n
                with nc.Block() as block:
                    @block.scalar
                    def _(act):
                        for k in range(kt):
                            actq(act.activation(h[:, k, :], x[:, k, :], ACT.Square))
                        act.wait_ge(dve_self, d1 + 1)
                        actq(act.activation(rs[:, :], rs[:, :], ACT.Sqrt))

                    @block.tensor
                    def _(pe):
                        for k in range(kt):
                            pe.wait_ge(act_self, a1 + k + 1)
                            mm = pe.matmul(ps, ones, h[:, k, :], start=k == 0, stop=k == kt - 1)
                        peq(mm)

                    @block.vector
                    def _(dve):
                        dve.wait_ge(pe_self, p1 + 1)
                        dveq(dve.tensor_scalar(rs[:, :], ps, 1.0 / width, EPS, ALU.mult, ALU.add))
                        dve.wait_ge(act_self, a1 + kt + 1)
                        dveq(dve.reciprocal(rs[:, :], rs[:, :]))
                        dveq.wait(dve)
                        for k in range(kt):
                            dveq(dve.scalar_tensor_tensor(h[:, k, :], x[:, k, :], par(gain, k), rs[:, :],
                                                          ALU.mult, ALU.mult))

        def tables(angle_pos, inv, cos, sin, ctx):
            u = sb("tab_u", [P, T], ctx=ctx)
            kk = sb("tab_k", [P, T], ctx=ctx)
            ang = angle_pos
            C1, C2 = 6.28125, 0.0019350051879882812
            C3 = float(2 * np.pi - C1 - C2)
            MAGIC = 12582912.0
            with nc.Block() as block:
                d1 = dveq.n
                a1 = actq.n

                @block.vector
                def _(dve):
                    def step(ins):
                        dveq(ins)
                        dveq.wait(dve)
                    step(dve.tensor_scalar(ang, angle_pos, inv, None, ALU.mult))
                    for n, (dst, turn) in enumerate(((cos, 0.25), (sin, 0.0))):
                        step(dve.tensor_scalar(u[:, :], ang, float(1 / (2 * np.pi)), turn, ALU.mult, ALU.add))
                        step(dve.tensor_scalar(kk[:, :], u[:, :], MAGIC, None, ALU.add))
                        step(dve.tensor_scalar(kk[:, :], kk[:, :], MAGIC, None, ALU.subtract))
                        step(dve.scalar_tensor_tensor(u[:, :], kk[:, :], -C1, ang, ALU.mult, ALU.add))
                        step(dve.scalar_tensor_tensor(u[:, :], kk[:, :], -C2, u[:, :], ALU.mult, ALU.add))
                        step(dve.scalar_tensor_tensor(u[:, :], kk[:, :], -C3, u[:, :], ALU.mult, ALU.add))
                        step(dve.tensor_scalar(u[:, :], u[:, :], float(turn * 2 * np.pi), 3.1415925, ALU.add, ALU.min))
                        step(dve.tensor_scalar(dst, u[:, :], -3.1415925, None, ALU.max))
            with nc.Block() as block:
                @block.scalar
                def _(act):
                    actq(act.activation(cos, cos, ACT.Sin))
                    actq(act.activation(sin, sin, ACT.Sin))

        s_ready, m_ready, e_done = sem("s_ready"), sem("m_ready"), sem("e_done")
        t_ready, t_out, o_ready, o_out = sem("t_ready"), sem("t_out"), sem("o_ready"), sem("o_out")
        att = {"u": 0, "g": 0}

        def attention(groups, ctx):
            pr = [sb(f"att_p{i}", [P, T], ctx=ctx) for i in range(2)]
            pt = [sb(f"att_pt{i}", [P, T], ctx=ctx) for i in range(2)]
            nmax = sb("att_nmax", [P, 2, 8], ctx=ctx)
            total = sb("att_sum", [P, 2, 8], ctx=ctx)
            rinv = sb("att_rinv", [P, 8], ctx=ctx)
            esink = sb("att_esink", [P, 8], ctx=ctx)
            units = [(g, i, u) for g, grp in enumerate(groups) for i, u in enumerate(grp["units"])]
            U, u0, g0 = len(units), att["u"], att["g"]
            S, TP, O = bank[0:2], bank[2:4], bank[4:6]
            ends = {}
            for n, (g, i, u) in enumerate(units):
                ends[g] = n
            with nc.Block() as block:
                @block.tensor
                def _(pe):
                    for n in range(U + 2):
                        if n < U:
                            g, i, (q, k, masks, vals) = units[n]
                            if n >= 2:
                                pe.wait_ge(e_done, u0 + n - 1)
                            w = k.shape[-1]
                            pe.matmul(S[n % 2][:, 0:w], q, k, start=True, stop=True).then_inc(s_ready, 1)
                        v = n - 1
                        if 0 <= v < U:
                            pe.wait_ge(e_done, u0 + v + 1)
                            if v >= 2:
                                pe.wait_ge(t_out, u0 + v - 1)
                            nb = len(units[v][2][3])
                            for b in range(nb):
                                mm = pe.transpose(TP[v % 2][:, b * P:(b + 1) * P],
                                                  pr[v % 2][:, b * P:(b + 1) * P], ident)
                            mm.then_inc(t_ready, 1)
                        v = n - 2
                        if 0 <= v < U:
                            g, i, (q, k, masks, vals) = units[v]
                            pe.wait_ge(t_out, u0 + v + 1)
                            if i == 0 and g >= 2:
                                pe.wait_ge(o_out, g0 + g - 1)
                            for b, val in enumerate(vals):
                                mm = pe.matmul(O[g % 2][:, i * HD:(i + 1) * HD], pt[v % 2][:, b * P:(b + 1) * P],
                                               val, start=b == 0, stop=b == len(vals) - 1)
                            mm.then_inc(o_ready, 1)

                @block.vector
                def _(dve):
                    def finish(g):
                        grp = groups[g]
                        nu = len(grp["units"])
                        dve.wait_ge(o_ready, u0 + ends[g] + 1)
                        tot = total[:, g % 2, 0:nu]
                        if grp.get("sink") is not None:
                            dve.wait_ge(act_self, grp["sink_at"])
                            dveq(dve.tensor_tensor(tot, tot, esink[:, 0:nu], ALU.add))
                            dveq.wait(dve)
                        dveq(dve.reciprocal(rinv[:, 0:nu], tot))
                        dveq.wait(dve)
                        grp["evac"](dve, O[g % 2], rinv[:, 0:nu]).then_inc(o_out, 1)
                        dve.wait_ge(o_out, g0 + g + 1)

                    for n in range(U + 3):
                        if n < U:
                            g, i, (q, k, masks, vals) = units[n]
                            w = k.shape[-1]
                            dve.wait_ge(s_ready, u0 + n + 1)
                            for c, mask in masks:
                                dveq(dve.tensor_tensor(S[n % 2][:, c:c + P], S[n % 2][:, c:c + P], mask, ALU.add))
                            if masks:
                                dveq.wait(dve)
                            nm = nmax[:, g % 2, i:i + 1]
                            ins = dve.tensor_reduce(nm, S[n % 2][:, 0:w], AX.X, ALU.max, negate=True)
                            if groups[g].get("sink") is not None:
                                dveq(ins)
                                dveq.wait(dve)
                                ins = dve.tensor_tensor(nm, nm, groups[g]["sink"][:, i:i + 1], ALU.min)
                            ins.then_inc(m_ready, 1)
                        if n - 2 >= 0 and n - 2 < U and ends[units[n - 2][0]] == n - 2:
                            finish(units[n - 2][0])

                @block.scalar
                def _(act):
                    for n in range(U + 1):
                        if n < U:
                            g, i, (q, k, masks, vals) = units[n]
                            w = k.shape[-1]
                            act.wait_ge(m_ready, u0 + n + 1)
                            if n >= 2:
                                act.wait_ge(t_ready, u0 + n - 1)
                            act.activation(pr[n % 2][:, 0:w], S[n % 2][:, 0:w], ACT.Exp,
                                           bias=nmax[:, g % 2, i:i + 1],
                                           accum_out=total[:, g % 2, i:i + 1]).then_inc(e_done, 1)
                        v = n - 1
                        if 0 <= v < U:
                            w = P * len(units[v][2][3])
                            act.wait_ge(t_ready, u0 + v + 1)
                            if v >= 2:
                                act.wait_ge(o_ready, u0 + v - 1)
                            act.activation(pt[v % 2][:, 0:w], TP[v % 2][:, 0:w], ACT.Copy).then_inc(t_out, 1)
                            g, i, _ = units[v]
                            if groups[g].get("sink") is not None and ends[g] == v:
                                nu = len(groups[g]["units"])
                                if g >= 1:
                                    act.wait_ge(o_out, g0 + g)
                                for k2 in range(nu):
                                    actq(act.activation(esink[:, k2:k2 + 1], groups[g]["plus"][:, k2:k2 + 1], ACT.Exp,
                                                        bias=nmax[:, g % 2, k2:k2 + 1]))
            att["u"] += U
            att["g"] += len(groups)

        pos = es.enter_context(nc.sbuf_tensor("pos", [P, 2, T], I32))
        MKV = ExitStack()
        memk = [sb(f"memk{i}", [P, 2, MEM], ctx=MKV) for i in range(2)]
        memv = [sb(f"memv{i}", [P, 2, MEM], ctx=MKV) for i in range(2)]
        with nc.Block() as block:
            @block.scalar
            def _(act):
                act.dma_start(cst[:, :], a["consts"]).then_inc(small_loaded, 16)
                act.dma_start(vec[:, :], a["vecs"]).then_inc(small_loaded, 16)
                act.dma_start(pos[:, :, :], a["pos"]).then_inc(small_loaded, 16)
                act.dma_start(xT[:, :, :], a["xT"].rearrange("(k p) n -> p k n", p=P)).then_inc(small_loaded, 16)
                act.wait_ge(small_loaded, 64)

            @block.sync
            def _(sp):
                issue_blocks(sp, RING)

        L0 = ExitStack()
        with L0:
            live = L0
            gates = sb("nsa_gates", [P, TT, 24])
            proj = sb("proj0", [P, 28, T])
            NQ, NKC, NVC, NKS, NKW, NZ, MQ, MK, MZ, EQ, EZ = 0, 4, 5, 6, 7, 8, 12, 16, 20, 24, 26
            nvs = sb("nvs", [P, TT, P])
            nvw = sb("nvw", [P, TT, P])
            mv = sb("mv", [P, TT, 512])
            PR = ExitStack()
            with PR:
                cos = sb("cos", [P, T], ctx=PR)
                sin = sb("sin", [P, T], ctx=PR)
                TB = ExitStack()
                with TB:
                    posf = sb("posf", [P, T], ctx=TB)
                    with nc.Block() as block:
                        @block.vector
                        def _(dve):
                            dveq(dve.tensor_copy(posf[:, :], pos[:, 0, :]))
                    T1 = ExitStack()
                    with T1:
                        tables(posf[:, :], con("inv"), cos[:, :], sin[:, :], T1)
                MM = ExitStack()
                with MM:
                    memh = sb("memh", [P, KD, MEM], ctx=MM)
                    M2 = ExitStack()
                    memT = sb("memT", [P, KD, MEM], ctx=M2)
                    with nc.Block() as block:
                        @block.scalar
                        def _(act):
                            act.dma_start(memT[:, :, :], a["memT"].rearrange("(k p) n -> p k n", p=P))\
                               .then_inc(small_loaded, 16)
                            act.wait_ge(small_loaded, 80)
                    norm(memT, memh, "g_mem", MEM)
                    M2.close()
                    hT = sb("hT0", [P, KD, T], ctx=MM)
                    norm(xT, hT, "g_l0", T)
                    tmp = sb("rot_tmp", [P, 2, T], ctx=MM)
                    jobs = []

                    def fm(j, c, tile, func=None, scale=1.0, eng=None):
                        mats = fm_mats(j, c, hT)
                        jobs.append(dict(block=j, mats=mats, out=whole, eng=eng or ("act" if len(jobs) % 2 else "dve"),
                                         evac=to(proj[:, tile, :], func, scale)))
                        return len(jobs) - 1

                    def rotary(tile, src, rot, scale=1.0):
                        x = proj[:, tile, :]

                        def evac(dve, ps, own):
                            own(dve.tensor_tensor(tmp[:, 0, :], ps, sin[:, :], ALU.mult))
                            own(dve.tensor_tensor(tmp[:, 1, :], x, cos[:, :], ALU.mult))
                            own.wait(dve)
                            if scale == 1.0:
                                ins = dve.tensor_tensor(x, tmp[:, 0, :], tmp[:, 1, :], ALU.add)
                            else:
                                own(dve.tensor_tensor(tmp[:, 0, :], tmp[:, 0, :], tmp[:, 1, :], ALU.add))
                                own.wait(dve)
                                ins = dve.tensor_scalar(x, tmp[:, 0, :], scale, None, ALU.mult)
                            return ins
                        jobs.append(dict(block=None, mats=[(rot, x)], out=whole, eng="dve", evac=evac, after=src))

                    def tm(j, c, n, dst, t, eng=None, func=None):
                        jobs.append(dict(block=j, mats=tm_mats(j, c, n, hT, t), out=lambda b: b[:, 0:n],
                                         eng=eng or ("act" if len(jobs) % 2 else "dve"), evac=to(dst, func)))
                        return len(jobs) - 1

                    rot = con("rot")
                    wait_rot = []

                    def later(*x):
                        wait_rot.append(x)

                    def flush():
                        for x in wait_rot:
                            rotary(*x)
                        wait_rot.clear()

                    for i in range(4):
                        later(NQ + i, fm(EVEN["nq"], i * P, NQ + i, eng="act"), rot, 0.125)
                    j = EVEN["kv1"]
                    c = fm(j, 0, NKC, eng="act")
                    fm(j, 128, NVC, eng="act")
                    flush()
                    later(NKC, c, rot)
                    later(NKS, fm(j, 256, NKS, eng="act"), rot)
                    for t in range(TT):
                        tm(j, 384, 128, nvs[:, t, :], t, eng="act")
                    flush()
                    j = EVEN["kv2"]
                    later(NKW, fm(j, 0, NKW, eng="act"), rot)
                    for t in range(TT):
                        tm(j, 128, 128, nvw[:, t, :], t, eng="act")

                    def gate_evac(t):
                        def evac(dve, ps, own):
                            return dve.tensor_tensor(gates[:, t, :], ps, par("nsa_b"), ALU.add)
                        return evac
                    for t in range(TT):
                        jobs.append(dict(block=j, mats=tm_mats(j, 256, 24, hT, t), out=lambda b: b[:, 0:24], eng="dve",
                                         evac=gate_evac(t)))
                    flush()
                    for i in range(4):
                        fm(EVEN["nz"], i * P, NZ + i, ACT.Silu, eng="act")
                    for i in range(4):
                        later(MQ + i, fm(EVEN["mq"], i * P, MQ + i, eng="act"), rot, 0.125)
                    c = [fm(EVEN["mk"], i * P, MK + i, eng="act") for i in range(2)]
                    flush()
                    c += [fm(EVEN["mk"], i * P, MK + i, eng="act") for i in range(2, 4)]
                    for i in range(4):
                        later(MK + i, c[i], rot)
                    for t in range(TT):
                        tm(EVEN["mv"], 0, 512, mv[:, t, :], t, eng="act")
                    flush()
                    for i in range(4):
                        fm(EVEN["mz"], i * P, MZ + i, ACT.Silu, eng="act")
                    for i in range(2):
                        fm(EVEN["e"], i * P, EQ + i, scale=0.125, eng="dve")
                    for i in range(2):
                        fm(EVEN["e"], 256 + i * P, EZ + i, ACT.Silu, eng="act")
                    for l, j in enumerate((MK0, MK1)):
                        for i in range(2):
                            jobs.append(dict(block=j, mats=[(block_ap(j)[:, k, i * P:(i + 1) * P], memh[:, k, :])
                                                            for k in range(KD)],
                                             out=lambda b: b[:, 0:MEM], eng="dve", evac=to(memk[l][:, i, :])))
                        for t in range(2):
                            jobs.append(dict(block=j, mats=[(memh[:, k, t * P:(t + 1) * P], block_ap(j)[:, k, 256:512])
                                                            for k in range(KD)],
                                             out=lambda b: b[:, 0:MEM], eng="act", evac=to(memv[l][:, t, :])))
                    run_products(jobs)

            CM = ExitStack()
            with CM:
                kc = sb("kc", [P, 32], ctx=CM)
                vcd = sb("vcd", [P, 2, 4, HD], ctx=CM)
                CA = ExitStack()
                with CA:
                    w1 = sb("cmp_w1", [P, 2, 32, HD], ctx=CA)
                    w2 = sb("cmp_w2", [P, 2, HD], ctx=CA)
                    blocks = sb("cmp_blocks", [P, 2, 32, 31], ctx=CA)
                    hid = sb("cmp_hid", [P, 2, 31], ctx=CA)
                    cmp_loaded = sem("cmp_loaded")
                    d1, p1, a1, g1 = dveq.n, peq.n, actq.n, poolq.n
                    with nc.Block() as block:
                        @block.sync
                        def _(sp):
                            for i, kv in enumerate("kv"):
                                for g in range(2):
                                    sp.dma_start(w1[g * 64:(g + 1) * 64, i], a[f"l0_cmp_w1_{kv}"]
                                                 .rearrange("l d e -> d l e")).then_inc(cmp_loaded, 16)
                                    sp.dma_start(w2[g * 64:(g + 1) * 64, i], a[f"l0_cmp_w2_{kv}"]).then_inc(cmp_loaded, 16)

                        @block.vector
                        def _(dve):
                            for i, tile in enumerate((NKC, NVC)):
                                src = proj[:, tile, :]
                                for half in range(2):
                                    at = src[:, 16 * half:16 * half + 496].rearrange("p (n l) -> p l n", l=16)
                                    pe_ = par("pe_k" if i == 0 else "pe_v")[:, 16 * half:16 * half + 16]
                                    dveq(dve.tensor_tensor(blocks[:, i, 16 * half:16 * half + 16, :], at,
                                                           pe_.unsqueeze(2).to_broadcast([P, 16, 31]), ALU.add))
                            dveq(dve.memset(kc[:, :], 0.0))
                            dveq(dve.memset(vcd[:, :, :, :], 0.0))

                        @block.scalar
                        def _(act):
                            act.wait_ge(pe_self, p1 + 1)
                            actq(act.activation(hid[:, :, :], bank[0][:, 0:64].rearrange("p (i n) -> p i n", i=2)[:, :, 0:31],
                                                ACT.Silu))
                            act.wait_ge(pe_self, p1 + 2)
                            act.wait_ge(dve_self, d1 + 6)
                            actq(act.activation(kc[:, 0:31], bank[1][:, 0:31], ACT.Copy))
                            for g in range(2):
                                for i in range(4):
                                    actq(act.activation(vcd[32 * i:32 * i + 31, g, i, :],
                                                        bank[2 + g][0:31, 0:HD], ACT.Copy))
                            for t in range(TT):
                                actq(act.activation(gates[:, t, :], gates[:, t, :], ACT.Sigmoid))

                        @block.tensor
                        def _(pe):
                            pe.wait_ge(cmp_loaded, 128)
                            pe.wait_ge(dve_self, d1 + 4)
                            for g in range(2):
                                r = slice(g * 64, (g + 1) * 64)
                                for i in range(2):
                                    for l in range(32):
                                        mm = pe.matmul(bank[0][r, 32 * i:32 * i + 31], w1[r, i, l, :], blocks[r, i, l, :],
                                                       start=l == 0, stop=l == 31)
                            peq(mm)
                            pe.wait_ge(act_self, a1 + 1)
                            for g in range(2):
                                r = slice(g * 64, (g + 1) * 64)
                                pe.matmul(bank[1][r, 0:31], w2[r, 0, :], hid[r, 0, :], start=True, stop=True)
                            for g in range(2):
                                r = slice(g * 64, (g + 1) * 64)
                                mm = pe.matmul(bank[2 + g][0:31, 0:HD], hid[r, 1, :], w2[r, 1, :],
                                               start=True, stop=True)
                            peq(mm)

                oacc = sb("nsa_out", [P, TT, 8, HD], ctx=CM)
                sc = sb("cmp_s", [P, 8, 32], ctx=CM)
                mx = sb("cmp_m", [P, 8], ctx=CM)
                sm = sb("cmp_sum", [P, 8], ctx=CM)
                pT = sb("cmp_pt", [P, 2, P], ctx=CM)
                for t in range(TT):
                    d1, p1, a1 = dveq.n, peq.n, actq.n
                    with nc.Block() as block:
                        @block.tensor
                        def _(pe):
                            for h in range(8):
                                g, i = h // 4, h % 4
                                r = slice(g * 64, (g + 1) * 64)
                                mm = pe.matmul(bank[0 if g == 0 else 1][:, i * 32:(i + 1) * 32],
                                               proj[r, NQ + i, t * P:(t + 1) * P], kc[r, :], start=True, stop=True)
                            peq(mm)
                            pe.wait_ge(dve_self, d1 + 8)
                            for g in range(2):
                                mm = pe.transpose(bank[2][:, g * P:(g + 1) * P],
                                                  sc[:, 4 * g:4 * g + 4, :].rearrange("p i n -> p (i n)"), ident)
                            peq(mm)
                            pe.wait_ge(act_self, a1 + 2)
                            for g in range(2):
                                mm = pe.matmul(bank[3][:, g * 256:(g + 1) * 256], pT[:, g, :],
                                               vcd[:, g, :, :].rearrange("p i d -> p (i d)"), start=True, stop=True)
                            peq(mm)

                        @block.vector
                        def _(dve):
                            def step(ins):
                                dveq(ins)
                                dveq.wait(dve)
                            m01 = con("cmp01", t, 32).unsqueeze(1)
                            neg = con("cmpneg", t, 32).unsqueeze(1)
                            dve.wait_ge(pe_self, p1 + 1)
                            for g in range(2):
                                dveq(dve.tensor_tensor(sc[:, 4 * g:4 * g + 4, :],
                                                       bank[g][:, 0:128].rearrange("p (i n) -> p i n", i=4),
                                                       m01.to_broadcast([P, 4, 32]), ALU.mult))
                            dveq.wait(dve)
                            step(dve.tensor_tensor(sc[:, :, :], sc[:, :, :], neg.to_broadcast([P, 8, 32]), ALU.add))
                            step(dve.tensor_reduce(mx[:, :], sc[:, :, :], AX.X, ALU.max))
                            step(dve.tensor_tensor(sc[:, :, :], sc[:, :, :],
                                                   mx[:, :].unsqueeze(2).to_broadcast([P, 8, 32]), ALU.subtract))
                            dve.wait_ge(act_self, a1 + 1)
                            step(dve.tensor_tensor(sc[:, :, :], sc[:, :, :], m01.to_broadcast([P, 8, 32]), ALU.mult))
                            step(dve.tensor_reduce(sm[:, :], sc[:, :, :], AX.X, ALU.add))
                            step(dve.tensor_scalar(sm[:, :], sm[:, :], 1e-30, None, ALU.max))
                            step(dve.reciprocal(sm[:, :], sm[:, :]))
                            step(dve.tensor_tensor(sm[:, :], sm[:, :], gates[:, t, 0:8], ALU.mult))
                            dve.wait_ge(pe_self, p1 + 3)
                            dveq(dve.tensor_tensor(oacc[:, t, :, :], bank[3][:, :].rearrange("p (h d) -> p h d", d=HD),
                                                   sm[:, :].unsqueeze(2).to_broadcast([P, 8, HD]), ALU.mult))

                        @block.scalar
                        def _(act):
                            act.wait_ge(dve_self, d1 + 5)
                            actq(act.activation(sc[:, :, :], sc[:, :, :], ACT.Exp))
                            act.wait_ge(pe_self, p1 + 2)
                            actq(act.activation(pT[:, :, :], bank[2][:, 0:256].rearrange("p (g n) -> p g n", g=2), ACT.Copy))

                causal = con("causal")
                tmpo = sb("att_tmpo", [P, 8, HD], ctx=CM)

                def units_of(t, qs, ks, vs):
                    return [(q[:, t * P:(t + 1) * P], k[:, 0:(t + 1) * P], [(t * P, causal)],
                             [v(b) for b in range(t + 1)]) for q, k, v in zip(qs, ks, vs)]

                def head(tile, h):
                    return proj[h * 64:(h + 1) * 64, tile, :]

                def values(v, h):
                    return lambda b: v[:, b, h * HD:(h + 1) * HD]

                def add_evac(t, branch):
                    def evac(dve, ps, r):
                        dveq(dve.tensor_tensor(r, r, gates[:, t, 8 * branch:8 * branch + 8], ALU.mult))
                        dveq.wait(dve)
                        dveq(dve.tensor_tensor(tmpo[:, :, :], ps[:, :].rearrange("p (h d) -> p h d", d=HD),
                                               r.unsqueeze(2).to_broadcast([P, 8, HD]), ALU.mult))
                        dveq.wait(dve)
                        return dve.tensor_tensor(oacc[:, t, :, :], oacc[:, t, :, :], tmpo[:, :, :], ALU.add)
                    return evac

                def set_evac(dst, n):
                    def evac(dve, ps, r):
                        return dve.tensor_tensor(dst, ps[:, 0:n * HD].rearrange("p (h d) -> p h d", d=HD),
                                                 r.unsqueeze(2).to_broadcast([P, n, HD]), ALU.mult)
                    return evac

                groups = []
                for branch, kt_, v in ((1, NKS, nvs), (2, NKW, nvw)):
                    for t in range(TT):
                        groups.append(dict(units=units_of(t, [head(NQ + h % 4, h // 4) for h in range(8)],
                                                          [head(kt_, h // 4) for h in range(8)],
                                                          [values(v, h // 4) for h in range(8)]),
                                           evac=add_evac(t, branch)))
                moba = sb("moba_out", [P, TT, 8, HD], ctx=CM)
                for t in range(TT):
                    groups.append(dict(units=units_of(t, [head(MQ + h // 2, h % 2) for h in range(8)],
                                                      [head(MK + h // 2, h % 2) for h in range(8)],
                                                      [values(mv, h) for h in range(8)]),
                                       evac=set_evac(moba[:, t, :, :], 8)))
                memo = sb("mem_out", [P, TT, 4, HD], ctx=CM)
                for t in range(TT):
                    groups.append(dict(units=[(head(EQ + h // 2, h % 2)[:, t * P:(t + 1) * P],
                                               memk[0][(h % 2) * 64:(h % 2) * 64 + 64, h // 2, :], [],
                                               [memv[0][:, b, h * HD:(h + 1) * HD] for b in range(2)]) for h in range(4)],
                                       evac=set_evac(memo[:, t, :, :], 4)))
                AT = ExitStack()
                with AT:
                    attention(groups, AT)

                def gate_back(src, gate0, pairs, npair):
                    for t in range(TT):
                        for i in range(npair):
                            s = src[:, t, :, :]
                            l = (s.rearrange("p (g i) d -> p i g d", g=2)[:, i] if pairs else s[:, 2 * i:2 * i + 2, :])
                            yield t, gate0 + i, l
                items = [*gate_back(oacc, NZ, True, 4), *gate_back(moba, MZ, False, 4), *gate_back(memo, EZ, False, 2)]
                stage = sb("back", [P, 2, P], ctx=CM)
                back_in, back_t, back_out = sem("back_in"), sem("back_t"), sem("back_out")
                with nc.Block() as block:
                    @block.scalar
                    def _(act):
                        for n, (t, tile, l) in enumerate(items):
                            if n >= 2:
                                act.wait_ge(back_t, n - 1)
                            act.activation(stage[:, n % 2, :].rearrange("p (g d) -> p g d", g=2), l, ACT.Copy)\
                               .then_inc(back_in, 1)

                    @block.tensor
                    def _(pe):
                        for n, (t, tile, l) in enumerate(items):
                            pe.wait_ge(back_in, n + 1)
                            if n >= 2:
                                pe.wait_ge(back_out, n - 1)
                            pe.transpose(bank[n % 2][:, 0:P], stage[:, n % 2, :], ident).then_inc(back_t, 1)

                    @block.vector
                    def _(dve):
                        for n, (t, tile, l) in enumerate(items):
                            dve.wait_ge(back_t, n + 1)
                            y = proj[:, tile, t * P:(t + 1) * P]
                            dve.tensor_tensor(y, bank[n % 2][:, 0:P], y, ALU.mult).then_inc(back_out, 1)

            yt = [NZ, NZ + 1, NZ + 2, NZ + 3, MZ, MZ + 1, MZ + 2, MZ + 3, EZ, EZ + 1]
            jobs = []

            def add_to(m):
                def evac(dve, ps, own):
                    return dve.tensor_tensor(xT[:, m, :], ps, xT[:, m, :], ALU.add)
                return evac
            for c, j in enumerate(WO0):
                for m in range(2):
                    jobs.append(dict(block=j, mats=[(block_ap(j)[:, k, m * P:(m + 1) * P], proj[:, yt[k], :])
                                                    for k in range(10)],
                                     out=whole, eng="dve", evac=add_to(2 * c + m)))
            run_products(jobs)

        L1 = ExitStack()
        with L1:
            live = L1
            RQ, RK, RZ, EQ, EZ = 0, 8, 16, 32, 34
            proj = sb("proj1", [P, 36, T])
            rv = sb("rv", [P, TT, 2048])
            H1 = ExitStack()
            with H1:
                hT = sb("hT1", [P, KD, T], ctx=H1)
                norm(xT, hT, "g_l1", T)
                jobs = []

                def fm1(j, c, tile, func=None, scale=1.0, eng=None):
                    jobs.append(dict(block=j, mats=fm_mats(j, c, hT), out=whole,
                                     eng=eng or ("act" if func or len(jobs) % 2 else "dve"),
                                     evac=to(proj[:, tile, :], func, scale)))
                for i in range(16):
                    fm1(ODD[i // 4], (i % 4) * P, RQ + i)
                for c in range(4):
                    for t in range(TT):
                        j = ODD[4 + c]
                        jobs.append(dict(block=j, mats=tm_mats(j, 0, 512, hT, t), out=whole,
                                         eng="act" if t % 2 else "dve", evac=to(rv[:, t, c * 512:(c + 1) * 512])))
                for i in range(16):
                    fm1(ODD[8 + i // 4], (i % 4) * P, RZ + i, ACT.Silu)
                for i in range(2):
                    fm1(ODD[12], i * P, EQ + i, scale=0.125, eng="dve")
                for i in range(2):
                    fm1(ODD[12], 256 + i * P, EZ + i, ACT.Silu)
                run_products(jobs)
            RO = ExitStack()
            with RO:
                cosr = sb("cosr", [P, T], ctx=RO)
                sinr = sb("sinr", [P, T], ctx=RO)
                posf = sb("posf1", [P, T], ctx=RO)
                with nc.Block() as block:
                    @block.vector
                    def _(dve):
                        dveq(dve.tensor_copy(posf[:, :], pos[:, 0, :]))
                T1 = ExitStack()
                with T1:
                    tables(posf[:, :], con("invr"), cosr[:, :], sinr[:, :], T1)
                ra = sb("ra", [P, 2, T], ctx=RO)
                rb = sb("rb", [P, 2, T], ctx=RO)
                for part in range(8):
                    x1, x2 = proj[:, 2 * part, :], proj[:, 2 * part + 1, :]
                    d1, g1 = dveq.n, poolq.n
                    with nc.Block() as block:
                        @block.vector
                        def _(dve):
                            dveq(dve.tensor_tensor(ra[:, 0, :], x1, cosr[:, :], ALU.mult))
                            dveq(dve.tensor_tensor(ra[:, 1, :], x2, sinr[:, :], ALU.mult))
                            dveq.wait(dve)
                            dve.wait_ge(pool_self, g1 + 2)
                            dveq(dve.tensor_tensor(x1, ra[:, 0, :], ra[:, 1, :], ALU.subtract))

                        @block.gpsimd
                        def _(pool):
                            poolq(pool.tensor_tensor(rb[:, 0, :], x1, sinr[:, :], ALU.mult))
                            poolq(pool.tensor_tensor(rb[:, 1, :], x2, cosr[:, :], ALU.mult))
                            poolq.wait(pool)
                            pool.wait_ge(dve_self, d1 + 2)
                            poolq(pool.tensor_tensor(x2, rb[:, 0, :], rb[:, 1, :], ALU.add))

            MA = ExitStack()
            with MA:
                memo = sb("mem_out1", [P, TT, 4, HD], ctx=MA)
                groups = [dict(units=[(proj[(h % 2) * 64:(h % 2) * 64 + 64, EQ + h // 2, t * P:(t + 1) * P],
                                       memk[1][(h % 2) * 64:(h % 2) * 64 + 64, h // 2, :], [],
                                       [memv[1][:, b, h * HD:(h + 1) * HD] for b in range(2)]) for h in range(4)],
                               evac=set_evac(memo[:, t, :, :], 4)) for t in range(TT)]
                AT = ExitStack()
                with AT:
                    attention(groups, AT)
                p1 = peq.n
                with nc.Block() as block:
                    @block.tensor
                    def _(pe):
                        for i in range(2):
                            for t in range(TT):
                                mm = pe.transpose(bank[i][:, t * P:(t + 1) * P],
                                                  memo[:, t, 2 * i:2 * i + 2, :].rearrange("p h d -> p (h d)"), ident)
                            peq(mm)

                    @block.vector
                    def _(dve):
                        for i in range(2):
                            dve.wait_ge(pe_self, p1 + i + 1)
                            dveq(dve.tensor_tensor(proj[:, EZ + i, :], bank[i][:, :], proj[:, EZ + i, :], ALU.mult))

            RT = ExitStack()
            with RT:
                decay = sb("decay", [P, T], ctx=RT)
                decay_loaded = sem("decay_loaded")
                with nc.Block() as block:
                    @block.scalar
                    def _(act):
                        act.dma_start(decay[:, :], a["decay"][:, 0:T]).then_inc(decay_loaded, 16)
                sT = sb("ret_s", [P, TT, T], ctx=RT)
                ro = sb("ret_o", [P, 4, T], ctx=RT)
                rq2, mu, rs = sT[:, 0:2, :], sT[:, 2, :], sT[:, 3, :]
                for h in range(RH):
                    d1, p1, a1 = dveq.n, peq.n, actq.n
                    with nc.Block() as block:
                        @block.tensor
                        def _(pe):
                            for b in range(TT):
                                n = T - b * P
                                for k in range(2):
                                    mm = pe.matmul(bank[b][:, 0:n], proj[:, RK + 2 * h + k, b * P:(b + 1) * P],
                                                   proj[:, RQ + 2 * h + k, b * P:T], start=k == 0, stop=k == 1)
                                peq(mm)
                            for m in range(4):
                                for b in range(TT):
                                    if m == 0:
                                        pe.wait_ge(dve_self, d1 + b + 1)
                                    mm = pe.matmul(bank[4 + m][:, b * P:T], rv[:, b, h * 512 + m * P:h * 512 + (m + 1) * P],
                                                   sT[:, b, 0:T - b * P], start=b == 0, stop=b == TT - 1)
                                peq(mm)
                            for m in range(4):
                                pe.wait_ge(act_self, a1 + m + 1)
                                mm = pe.matmul(bank[0][:, :], ones, ro[:, m, :], start=m == 0, stop=m == 3)
                            peq(mm)
                            for m in range(4):
                                pe.wait_ge(act_self, a1 + 4 + m + 1)
                                mm = pe.matmul(bank[1][:, :], ones, rq2[:, m % 2, :], start=m == 0, stop=m == 3)
                                peq(mm)

                        @block.vector
                        def _(dve):
                            dec = decay
                            dve.wait_ge(decay_loaded, 16 * (h + 1))
                            for b in range(TT):
                                n = T - b * P
                                dve.wait_ge(pe_self, p1 + b + 1)
                                dveq(dve.tensor_tensor(sT[:, b, 0:n], bank[b][:, 0:n], dec[:, 0:n], ALU.mult))
                            dve.wait_ge(pe_self, p1 + 9)
                            dveq(dve.tensor_scalar(mu, bank[0][:, :], 1.0 / 512, None, ALU.mult))
                            dveq.wait(dve)
                            for m in range(4):
                                dveq(dve.tensor_tensor(ro[:, m, :], ro[:, m, :], mu, ALU.subtract))
                            dve.wait_ge(pe_self, p1 + 13)
                            dveq(dve.tensor_scalar(rs, bank[1][:, :], 1.0 / 512, EPS, ALU.mult, ALU.add))
                            dve.wait_ge(act_self, a1 + 9)
                            dveq(dve.reciprocal(rs, rs))
                            dveq.wait(dve)
                            for m in range(4):
                                dveq(dve.tensor_tensor(ro[:, m, :], ro[:, m, :], rs, ALU.mult))
                            dveq.wait(dve)
                            for m in range(4):
                                y = proj[:, RZ + 4 * h + m, :]
                                dveq(dve.tensor_tensor(y, y, ro[:, m, :], ALU.mult))

                        @block.scalar
                        def _(act):
                            if h + 1 < RH:
                                act.wait_ge(dve_self, d1 + TT)
                                act.dma_start(decay[:, :], a["decay"][:, (h + 1) * T:(h + 2) * T])\
                                   .then_inc(decay_loaded, 16)
                            for m in range(4):
                                act.wait_ge(pe_self, p1 + 4 + m + 1)
                                actq(act.activation(ro[:, m, :], bank[4 + m][:, :], ACT.Copy))
                            for m in range(4):
                                act.wait_ge(dve_self, d1 + 6 + m)
                                if m >= 2:
                                    act.wait_ge(pe_self, p1 + 10 + m - 2)
                                actq(act.activation(rq2[:, m % 2, :], ro[:, m, :], ACT.Square))
                            act.wait_ge(dve_self, d1 + 10)
                            actq(act.activation(rs, rs, ACT.Sqrt))
            yt1 = [RZ + i for i in range(16)] + [EZ, EZ + 1]
            jobs = [dict(block=j, mats=[(block_ap(j)[:, k, :], proj[:, yt1[k], :]) for k in range(18)],
                         out=whole, eng="dve", evac=add_to(m)) for m, j in enumerate(WO1)]
            run_products(jobs)

        MKV.close()
        norm(xT, xT2 := es.enter_context(nc.sbuf_tensor("xT2", [P, KD, T], F32)), "g_fin", T)
        res = xT2
        B2 = ExitStack()
        with B2:
            live = B2
            AQ, AK, GQ, GK, GR, GA, GG = 0, 4, 5, 9, 13, 21, 29
            proj = sb("proj2", [P, 37, T])
            av = sb("av", [P, TT, P])
            gv = sb("gv", [P, TT, D])
            z = sb("z", [16, 2, T])
            hT = xT
            norm(res, hT, "g_mix", T)
            jobs = []
            R2 = ExitStack()
            with R2:
                cos2 = sb("cos2", [P, T], ctx=R2)
                sin2 = sb("sin2", [P, T], ctx=R2)
                T1 = ExitStack()
                with T1:
                    posf = sb("posf2", [P, T], ctx=T1)
                    with nc.Block() as block:
                        @block.vector
                        def _(dve):
                            dveq(dve.tensor_copy(posf[:, :], pos[:, 1, :]))
                    tables(posf[:, :], con("inv2"), cos2[:, :], sin2[:, :], T1)
                tmp = sb("rot_tmp2", [P, 2, T], ctx=R2)

                def fm2(j, c, tile, func=None, scale=1.0, eng="act"):
                    mats = fm_mats(j, c, hT)
                    jobs.append(dict(block=j, mats=mats, out=whole, eng=eng, evac=to(proj[:, tile, :], func, scale)))
                    return len(jobs) - 1

                def rotary2(tile, src, scale):
                    x = proj[:, tile, :]

                    def evac(dve, ps, own):
                        own(dve.tensor_tensor(tmp[:, 0, :], ps, sin2[:, :], ALU.mult))
                        own(dve.tensor_tensor(tmp[:, 1, :], x, cos2[:, :], ALU.mult))
                        own.wait(dve)
                        own(dve.tensor_tensor(tmp[:, 0, :], tmp[:, 0, :], tmp[:, 1, :], ALU.add))
                        own.wait(dve)
                        return dve.tensor_scalar(x, tmp[:, 0, :], scale, None, ALU.mult)
                    jobs.append(dict(block=None, mats=[(con("rot2"), x)], out=whole, eng="dve", evac=evac, after=src))

                c = [fm2(W2["aq"], i * P, AQ + i) for i in range(4)]
                c.append(fm2(W2["akv"], 0, AK))
                for t in range(TT):
                    jobs.append(dict(block=W2["akv"], mats=tm_mats(W2["akv"], 128, 128, hT, t),
                                     out=lambda b: b[:, 0:128], eng="act", evac=to(av[:, t, :])))
                for i in range(4):
                    rotary2(AQ + i, c[i], 0.125)
                rotary2(AK, c[4], 1.0)
                for i in range(4):
                    fm2(W2["gq"], i * P, GQ + i, scale=float(P) ** -0.5)
                for i in range(4):
                    fm2(W2["gk"], i * P, GK + i, eng="dve")
                for c in range(2):
                    for t in range(TT):
                        j = W2[f"gv{c}"]
                        jobs.append(dict(block=j, mats=tm_mats(j, 0, 512, hT, t), out=whole, eng="dve",
                                         evac=to(gv[:, t, c * 512:(c + 1) * 512])))
                for i in range(8):
                    fm2(W2[f"gr{i // 4}"], (i % 4) * P, GR + i, ACT.Silu)
                for i in range(2):
                    j = W2["z"]
                    jobs.append(dict(block=j, mats=fm_mats(j, 16 * i, hT, 16), out=lambda b: b[0:16, :], eng="dve",
                                     evac=to(z[:, i, :])))
                for i in range(8):
                    fm2(W2[f"ga{i // 4}"], (i % 4) * P, GA + i, ACT.Sigmoid)
                for i in range(8):
                    fm2(W2[f"gg{i // 4}"], (i % 4) * P, GG + i, ACT.Sigmoid)
                run_products(jobs)

            ybr = xT[:, 4:8, :]
            WA = ExitStack()
            with WA:
                ao = xT[:, 0:4, :].rearrange("p t (h d) -> p t h d", d=HD)
                nsink = sb("nsink", [P, 8], ctx=WA)
                with nc.Block() as block:
                    @block.vector
                    def _(dve):
                        dveq(dve.tensor_scalar(nsink[:, :], par("sink"), -1.0, None, ALU.mult))
                groups = []
                a1 = actq.n
                for t in range(TT):
                    lo, hi = max(t - 1, 0), min(t + 1, TT - 1)
                    masks = []
                    if t > 0:
                        masks.append((0, con("behind")))
                    if t < TT - 1:
                        masks.append(((t + 1 - lo) * P, con("causal")))
                    a1 += 8
                    groups.append(dict(units=[(proj[(h // 4) * 64:(h // 4) * 64 + 64, AQ + h % 4, t * P:(t + 1) * P],
                                               proj[(h // 4) * 64:(h // 4) * 64 + 64, AK, lo * P:(hi + 1) * P], masks,
                                               [av[:, b, (h // 4) * HD:(h // 4 + 1) * HD] for b in range(lo, hi + 1)])
                                              for h in range(8)],
                                       sink=nsink, plus=par("sink"), sink_at=a1, evac=set_evac(ao[:, t, :, :], 8)))
                AT = ExitStack()
                with AT:
                    attention(groups, AT)
                stage = sb("back2", [P, 2, P], ctx=WA)
                b0 = len(items)
                with nc.Block() as block:
                    its = [(t, i) for t in range(TT) for i in range(4)]

                    @block.scalar
                    def _(act):
                        for n, (t, i) in enumerate(its):
                            if n >= 2:
                                act.wait_ge(back_t, b0 + n - 1)
                            act.activation(stage[:, n % 2, :].rearrange("p (g d) -> p g d", g=2),
                                           ao[:, t, :, :].rearrange("p (g i) d -> p i g d", g=2)[:, i], ACT.Copy)\
                               .then_inc(back_in, 1)

                    @block.tensor
                    def _(pe):
                        for n, (t, i) in enumerate(its):
                            pe.wait_ge(back_in, b0 + n + 1)
                            if n >= 2:
                                pe.wait_ge(back_out, b0 + n - 1)
                            pe.transpose(bank[n % 2][:, 0:P], stage[:, n % 2, :], ident).then_inc(back_t, 1)

                    @block.vector
                    def _(dve):
                        for n, (t, i) in enumerate(its):
                            dve.wait_ge(back_t, b0 + n + 1)
                            dve.tensor_copy(ybr[:, i, t * P:(t + 1) * P], bank[n % 2][:, 0:P]).then_inc(back_out, 1)

            GL = ExitStack()
            with GL:
                up = sb("gla_up", [16, 2, 512], ctx=GL)
                up_loaded = sem("up_loaded")
                with nc.Block() as block:
                    @block.sync
                    def _(sp):
                        sp.dma_start(up[:, 0, :], a["gla_gate_up_fwd_2"][0]).then_inc(up_loaded, 16)
                        sp.dma_start(up[:, 1, :], a["gla_gate_up_bwd_2"][0]).then_inc(up_loaded, 16)
                        sp.wait_ge(up_loaded, 32)
                la, t1, t2, cum = (proj[:, i, :] for i in range(AQ, AQ + 4))
                qt, kt_, ke = (xT[:, i, :] for i in range(3))
                am = xT[:, 3, :].rearrange("p (t l) -> p t l", t=TT)
                dec = sb("gla_dec", [P, 8], ctx=GL)
                ket = proj[:, AK, :].rearrange("p (t n) -> p t n", t=TT)
                st_ = sb("gla_state", [P, 8, 256], ctx=GL)
                for h in range(4):
                    for d in range(2):
                        d1, p1, a1 = dveq.n, peq.n, actq.n
                        cum3 = cum.rearrange("p (c l) -> p c l", l=64)
                        g3 = cum3[:, :, 63:64].to_broadcast([P, 8, 64])

                        def c3(x):
                            return x.rearrange("p (c l) -> p c l", l=64)
                        with nc.Block() as block:
                            @block.tensor
                            def _(pe):
                                pe.matmul(bank[0][:, :], up[:, d, h * P:(h + 1) * P], z[:, d, :], start=True, stop=True)\
                                  .then_inc(pe_self, 1)
                                peq.n += 1

                            @block.scalar
                            def _(act):
                                b = par("bias_f" if d == 0 else "bias_b", h)
                                act.wait_ge(pe_self, p1 + 1)
                                actq(act.activation(t1, bank[0][:, :], ACT.Abs, bias=b))
                                actq.wait(act)
                                actq(act.activation(t1, t1, ACT.Exp, scale=-1.0))
                                actq.wait(act)
                                actq(act.activation(t1, t1, ACT.Ln, bias=con("one")))

                            @block.vector
                            def _(dve):
                                dve.wait_ge(act_self, a1 + 1)
                                b = par("bias_f" if d == 0 else "bias_b", h)
                                dveq(dve.tensor_scalar(t2, bank[0][:, :], b, 0.0, ALU.add, ALU.min))
                                dveq.wait(dve)
                                dve.wait_ge(act_self, a1 + 3)
                                dveq(dve.tensor_tensor(la, t2, t1, ALU.subtract))
                                dveq.wait(dve)
                                dveq(dve.tensor_tensor_scan(cum, con("scan"), la, 0.0, ALU.mult, ALU.add))
                                dveq.wait(dve)
                                if d == 0:
                                    dveq(dve.tensor_copy(t1, cum))
                                    dveq(dve.tensor_tensor(c3(t2), g3, cum3, ALU.subtract))
                                else:
                                    dveq(dve.tensor_tensor(c3(t1), g3, cum3, ALU.subtract))
                                    dveq.wait(dve)
                                    dveq(dve.tensor_tensor(t1, t1, la, ALU.add))
                                    dveq(dve.tensor_tensor(t2, cum, la, ALU.subtract))
                        with nc.Block() as block:
                            @block.scalar
                            def _(act):
                                actq(act.activation(qt, t1, ACT.Exp, scale=1.0 / 16))
                                actq(act.activation(kt_, t1, ACT.Exp, scale=-1.0 / 16))
                                actq(act.activation(ke, t2, ACT.Exp, scale=1.0 / 16))
                                actq(act.activation(dec[:, :], cum3[:, :, 63], ACT.Exp, scale=1.0 / 16))
                        d1, p1, a1 = dveq.n, peq.n, actq.n
                        kvs = [bank[2 + c % 2 + 2 * (c // 4)][:, (c // 2 % 2) * 256:(c // 2 % 2) * 256 + 256]
                               for c in range(8)]
                        order = list(range(8)) if d == 0 else list(range(7, -1, -1))
                        with nc.Block() as block:
                            @block.vector
                            def _(dve):
                                dveq(dve.tensor_tensor(qt, qt, proj[:, GQ + h, :], ALU.mult))
                                dveq(dve.tensor_tensor(kt_, kt_, proj[:, GK + h, :], ALU.mult))
                                dveq(dve.tensor_tensor(ke, ke, proj[:, GK + h, :], ALU.mult))
                                dveq(dve.memset(st_[:, order[0], :], 0.0))
                                dve.wait_ge(pe_self, p1 + 1)
                                m = con("fwd" if d == 0 else "bwd").unsqueeze(1).to_broadcast([P, TT, P])
                                dveq(dve.tensor_tensor(am[:, :, :], bank[0][:, :].rearrange("p (t l) -> p t l", t=TT), m,
                                                       ALU.mult))
                                dve.wait_ge(pe_self, p1 + 3)
                                for n in range(7):
                                    c = order[n]
                                    kv = kvs[c]
                                    dveq.wait(dve)
                                    dveq(dve.scalar_tensor_tensor(st_[:, order[n + 1], :], st_[:, c, :], dec[:, c:c + 1], kv,
                                                                  ALU.mult, ALU.add))

                            @block.tensor
                            def _(pe):
                                pe.wait_ge(dve_self, d1 + 2)
                                for t in range(TT):
                                    s = slice(t * P, (t + 1) * P)
                                    mm = pe.matmul(bank[0][:, s], kt_[:, s], qt[:, s], start=True, stop=True)
                                peq(mm)
                                pe.wait_ge(dve_self, d1 + 3)
                                for t in range(TT):
                                    s = slice(t * P, (t + 1) * P)
                                    mm = pe.transpose(bank[1][:, s], ke[:, s], ident)
                                peq(mm)
                                pe.wait_ge(act_self, a1 + 1)
                                for c in range(8):
                                    r = slice((c % 2) * 64, (c % 2) * 64 + 64)
                                    mm = pe.matmul(kvs[c], ket[r, c // 2, :],
                                                   gv[r, c // 2, h * 256:(h + 1) * 256], start=True, stop=True)
                                peq(mm)
                                pe.wait_ge(dve_self, d1 + 5)
                                for v in range(2):
                                    for t in range(TT):
                                        s = slice(t * P, (t + 1) * P)
                                        pe.matmul(bank[6 + v][:, s], gv[:, t, h * 256 + v * P:h * 256 + (v + 1) * P],
                                                  am[:, t, :], start=(d == 0 and t == 0), stop=False, skip_group_check=True)
                                for n in range(1, 8):
                                    c = order[n]
                                    pe.wait_ge(dve_self, d1 + 5 + n)
                                    for v in range(2):
                                        mm = pe.matmul(bank[6 + v][:, c * 64:(c + 1) * 64], st_[:, c, v * P:(v + 1) * P],
                                                       qt[:, c * 64:(c + 1) * 64], start=False, stop=(n == 7 and d == 1),
                                                       skip_group_check=True)
                                peq(mm)

                            @block.scalar
                            def _(act):
                                act.wait_ge(pe_self, p1 + 2)
                                actq(act.activation(ket[:, :, :].rearrange("p t n -> p (t n)"), bank[1][:, :], ACT.Copy))
                    d1, p1, a1 = dveq.n, peq.n, actq.n
                    with nc.Block() as block:
                        @block.scalar
                        def _(act):
                            for v in range(2):
                                actq(act.activation((t1, t2)[v], bank[6 + v][:, :], ACT.Square))
                            act.wait_ge(dve_self, d1 + 1)
                            actq(act.activation(cum, cum, ACT.Sqrt))

                        @block.tensor
                        def _(pe):
                            for v in range(2):
                                pe.wait_ge(act_self, a1 + v + 1)
                                mm = pe.matmul(bank[0][:, :], ones, (t1, t2)[v], start=v == 0, stop=v == 1)
                            peq(mm)

                        @block.vector
                        def _(dve):
                            dve.wait_ge(pe_self, p1 + 1)
                            dveq(dve.tensor_scalar(cum, bank[0][:, :], 1.0 / 256, EPS, ALU.mult, ALU.add))
                            dve.wait_ge(act_self, a1 + 3)
                            dveq(dve.reciprocal(cum, cum))
                            dveq.wait(dve)
                            for v in range(2):
                                i = 2 * h + v
                                dveq(dve.scalar_tensor_tensor((qt, kt_)[v], bank[6 + v][:, :], par("g_gla", i),
                                                              cum, ALU.mult, ALU.mult))
                            dveq.wait(dve)
                            for v in range(2):
                                y = proj[:, GR + 2 * h + v, :]
                                dveq(dve.tensor_tensor(y, y, (qt, kt_)[v], ALU.mult))

            jobs = []

            def times_gate(tile, into=None):
                def evac(dve, ps, own):
                    g = proj[:, tile, :]
                    if into is None:
                        return dve.tensor_tensor(g, ps, g, ALU.mult)
                    own(dve.tensor_tensor(g, ps, g, ALU.mult))
                    own.wait(dve)
                    d = proj[:, into, :]
                    return dve.tensor_tensor(d, d, g, ALU.add)
                return evac
            for m in range(8):
                jobs.append(dict(block=WBA, mats=[(block_ap(WBA)[:, k, m * P:(m + 1) * P], ybr[:, k, :]) for k in range(4)],
                                 out=whole, eng="dve", evac=times_gate(GA + m)))
            for m in range(8):
                j = WBG[m // 4]
                jobs.append(dict(block=j, mats=[(block_ap(j)[:, k, (m % 4) * P:(m % 4 + 1) * P], proj[:, GR + k, :])
                                                for k in range(8)],
                                 out=whole, eng="dve", evac=times_gate(GG + m, GA + m)))
            run_products(jobs)
            jobs = []

            def add_res(m):
                def evac(dve, ps, own):
                    return dve.tensor_tensor(res[:, m, :], ps, res[:, m, :], ALU.add)
                return evac
            for m in range(8):
                j = WO2[m // 4]
                jobs.append(dict(block=j, mats=[(block_ap(j)[:, k, (m % 4) * P:(m % 4 + 1) * P], proj[:, GA + k, :])
                                                for k in range(8)],
                                 out=whole, eng="dve", evac=add_res(m)))
            run_products(jobs)

        ME = ExitStack()
        with ME:
            live = ME
            xn = xT
            norm(res, xn, "g_ffn", T)
            xg = sb("xg", [P, KD, NE * CAP])
            rankT = sb("rankT", [NE, T])
            affT = sb("affT", [NE, T])
            R1 = ExitStack()
            with R1:
                wr = sb("w_router", [P, KD, NE], ctx=R1)
                aff = sb("aff", [P, TT, NE], ctx=R1)
                st1 = sb("aff_m", [P, 2, TT], ctx=R1)
                rank = sb("rank", [P, TT, NE], ctx=R1)
                work = sb("topk", [NE, T], ctx=R1)
                top = sb("top8", [NE, 8], ctx=R1)
                onesT = sb("ones_row", [NE, T], ctx=R1)
                xnt = sb("xn_tm", [P, TT, D], ctx=R1)
                hot = sb("hot", [P, TT, NE, CAP], ctx=R1)
                router_loaded = sem("router_loaded")
                d1, p1, a1 = dveq.n, peq.n, actq.n
                with nc.Block() as block:
                    @block.sync
                    def _(sp):
                        sp.dma_start(wr[:, :, :], a["w_router_2"][0].rearrange("(k p) e -> p k e", p=P))\
                          .then_inc(router_loaded, 16)

                    @block.tensor
                    def _(pe):
                        pe.wait_ge(router_loaded, 16)
                        for t in range(TT):
                            for k in range(KD):
                                mm = pe.matmul(bank[0][:, t * NE:(t + 1) * NE], xn[:, k, t * P:(t + 1) * P], wr[:, k, :],
                                               start=k == 0, stop=k == KD - 1)
                        peq(mm)
                        for t in range(TT):
                            for half in range(2):
                                n = 2 * t + half
                                if n >= 4:
                                    pe.wait_ge(act_self, a1 + n - 3)
                                for k in range(4):
                                    mm = pe.transpose(bank[1 + n % 4][:, k * P:(k + 1) * P],
                                                      xn[:, 4 * half + k, t * P:(t + 1) * P], ident)
                                peq(mm)
                        pe.wait_ge(dve_self, d1 + 5)
                        for t in range(TT):
                            mm = pe.transpose(bank[5][0:NE, t * P:(t + 1) * P], aff[:, t, :], ident)
                        peq(mm)

                    @block.scalar
                    def _(act):
                        for n in range(8):
                            act.wait_ge(pe_self, p1 + 2 + n)
                            actq(act.activation(xnt[:, n // 2, (n % 2) * 512:(n % 2 + 1) * 512], bank[1 + n % 4][:, :],
                                                ACT.Copy))
                        act.wait_ge(dve_self, d1 + 2)
                        actq(act.activation(aff[:, :, :], aff[:, :, :], ACT.Exp))

                    @block.vector
                    def _(dve):
                        def step(ins):
                            dveq(ins)
                            dveq.wait(dve)
                        dve.wait_ge(pe_self, p1 + 1)
                        lg = bank[0][:, 0:TT * NE].rearrange("p (t e) -> p t e", t=TT)
                        step(dve.tensor_reduce(st1[:, 0, :], lg, AX.X, ALU.max))
                        step(dve.tensor_tensor(aff[:, :, :], lg, st1[:, 0, :].unsqueeze(2).to_broadcast([P, TT, NE]),
                                               ALU.subtract))
                        dve.wait_ge(act_self, a1 + 9)
                        step(dve.tensor_reduce(st1[:, 1, :], aff[:, :, :], AX.X, ALU.add))
                        step(dve.reciprocal(st1[:, 1, :], st1[:, 1, :]))
                        step(dve.tensor_tensor(aff[:, :, :], aff[:, :, :],
                                               st1[:, 1, :].unsqueeze(2).to_broadcast([P, TT, NE]), ALU.mult))
                        dve.wait_ge(pe_self, p1 + 10)
                        dveq(dve.memset(onesT[:, :], 1.0))
                        dveq(dve.tensor_copy(affT[:, :], bank[5][0:NE, :]))
                        step(dve.tensor_copy(work[:, :], bank[5][0:NE, :]))
                        for _ in range(CAP // 8):
                            step(dve.max(top[:, :], work[:, :]))
                            step(dve.match_replace(work[:, :], top[:, :], work[:, :], -1.0))
                        step(dve.tensor_scalar(work[:, :], work[:, :], 0.0, None, ALU.is_lt))
                        step(dve.tensor_tensor_scan(rankT[:, :], onesT[:, :], work[:, :], 0.0, ALU.mult, ALU.add))
                        step(dve.tensor_tensor(rankT[:, :], rankT[:, :], work[:, :], ALU.mult))
                d1, p1, a1 = dveq.n, peq.n, actq.n
                with nc.Block() as block:
                    @block.tensor
                    def _(pe):
                        for t in range(TT):
                            mm = pe.transpose(bank[0][:, t * NE:(t + 1) * NE], rankT[:, t * P:(t + 1) * P],
                                              ident[0:NE, 0:NE])
                        peq(mm)
                        n = 0
                        for half in range(2):
                            for k in range(KD):
                                if n >= 4:
                                    pe.wait_ge(act_self, a1 + n - 3)
                                for t in range(TT):
                                    if n == 0:
                                        pe.wait_ge(dve_self, d1 + 2 + t)
                                    mm = pe.matmul(bank[1 + n % 4][:, :], xnt[:, t, k * P:(k + 1) * P],
                                                   hot[:, t, 8 * half:8 * half + 8, :].rearrange("p e s -> p (e s)"),
                                                   start=t == 0, stop=t == TT - 1)
                                peq(mm)
                                n += 1

                    @block.vector
                    def _(dve):
                        dve.wait_ge(pe_self, p1 + 1)
                        dveq(dve.tensor_copy(rank[:, :, :], bank[0][:, 0:TT * NE].rearrange("p (t e) -> p t e", t=TT)))
                        dveq.wait(dve)
                        for t in range(TT):
                            dveq(dve.tensor_tensor(hot[:, t, :, :], con("slots").unsqueeze(1).to_broadcast([P, NE, CAP]),
                                                   rank[:, t, :].unsqueeze(2).to_broadcast([P, NE, CAP]), ALU.is_equal))

                    @block.scalar
                    def _(act):
                        for n in range(16):
                            act.wait_ge(pe_self, p1 + 2 + n)
                            half, k = n // 8, n % 8
                            actq(act.activation(xg[:, k, half * 512:(half + 1) * 512], bank[1 + n % 4][:, :], ACT.Copy))
            ye = sb("ye", [P, KD, D])
            put = sb("put", [P, KD, T])
            bc = sb("bc", [P, T])
            pick = sb("pick", [NE, KD * P])
            pick_loaded = sem("pick_loaded")
            with nc.Block() as block:
                @block.scalar
                def _(act):
                    act.dma_start(pick[:, :], a["pick"]).then_inc(pick_loaded, 16)
                    act.wait_ge(pick_loaded, 16)
            d1, p1, a1 = dveq.n, peq.n, actq.n
            with nc.Block() as block:
                @block.tensor
                def _(pe):
                    for k in range(KD):
                        if k >= 2:
                            pe.wait_ge(dve_self, d1 + k - 1)
                        row = pick[:, k * P:(k + 1) * P]
                        pe.matmul(bank[2 * (k % 2)][:, :], row, rankT[:, :], start=True, stop=True)
                        peq(pe.matmul(bank[2 * (k % 2) + 1][:, :], row, affT[:, :], start=True, stop=True))

                @block.scalar
                def _(act):
                    for k in range(KD):
                        act.wait_ge(pe_self, p1 + k + 1)
                        if k >= 1:
                            act.wait_ge(dve_self, d1 + k)
                        actq(act.activation(bc[:, :], bank[2 * (k % 2) + 1][:, :], ACT.Copy))

                @block.vector
                def _(dve):
                    for k in range(KD):
                        dve.wait_ge(act_self, a1 + k + 1)
                        dveq(dve.scalar_tensor_tensor(put[:, k, :], bank[2 * (k % 2)][:, :], con("slot"), bc[:, :],
                                                      ALU.is_equal, ALU.mult))
            sg = sb("sg", [P, T])
            hid = sb("hid", [P, D])
            hidT = sb("hidT", [P, KD, P])
            act_hid, dve_hid, hid_t, hid_out, ye_out = (sem("act_hid"), sem("dve_hid"), sem("hid_t"), sem("hid_out"),
                                                        sem("ye_out"))
            t0 = counts["tiles"]
            for p in range(NE // 2):
                for i in range(12):
                    last_tile[EXP[p][i]] = t0 + 12 * p + i + 1
            with nc.Block() as block:
                @block.sync
                def _(sp):
                    issue_blocks(sp, EXP[-1][-1] + RING + 1)

                @block.tensor
                def _(pe):
                    for p in range(NE // 2):
                        base = t0 + 12 * p
                        for i in range(8):
                            n, which, e = i // 4, (i // 2) % 2, i % 2
                            j = EXP[p][i]
                            wait_block(pe, j)
                            if e == 0 and p + n > 0:
                                pe.wait_ge(dve_hid, 2 * p + n)
                            if e == 0 and n == 1:
                                pe.wait_ge(dve_hid, 2 * p + 1)
                            for k in range(KD):
                                mm = pe.matmul(bank[which][e * 64:(e + 1) * 64, :],
                                               xg[:, k, (2 * p + e) * CAP:(2 * p + e + 1) * CAP], block_ap(j)[:, k, :],
                                               start=k == 0, stop=k == KD - 1)
                            mm.then_inc(tiles_done, 1)
                        for n in range(2):
                            pe.wait_ge(dve_hid, 2 * p + n + 1)
                            if p + n > 0:
                                pe.wait_ge(hid_out, 2 * p + n)
                            for k in range(4):
                                mm = pe.transpose(bank[2][:, k * P:(k + 1) * P],
                                                  hid[:, n * 512 + k * P:n * 512 + (k + 1) * P], ident)
                            mm.then_inc(hid_t, 1)
                        pe.wait_ge(hid_out, 2 * p + 2)
                        for i in range(8, 12):
                            n, e = (i - 8) // 2, i % 2
                            j = EXP[p][i]
                            wait_block(pe, j)
                            if e == 0 and p > 0:
                                pe.wait_ge(ye_out, 2 * p - 1 + n)
                            for k in range(KD):
                                mm = pe.matmul(bank[3 + n][e * 64:(e + 1) * 64, :], hidT[:, k, e * CAP:(e + 1) * CAP],
                                               block_ap(j)[:, k, :], start=k == 0, stop=k == KD - 1)
                            mm.then_inc(tiles_done, 1)

                @block.scalar
                def _(act):
                    for p in range(NE // 2):
                        base = t0 + 12 * p
                        for n in range(2):
                            act.wait_ge(tiles_done, base + 4 * n + 2)
                            if p + n > 0:
                                act.wait_ge(dve_hid, 2 * p + n)
                            act.activation(sg[:, :], bank[0][:, :], ACT.Silu).then_inc(act_hid, 1)
                        for n in range(2):
                            act.wait_ge(hid_t, 2 * p + n + 1)
                            act.activation(hidT[:, 4 * n:4 * n + 4, :].rearrange("p k s -> p (k s)"), bank[2][:, :],
                                           ACT.Copy).then_inc(hid_out, 1)

                @block.vector
                def _(dve):
                    for p in range(NE // 2):
                        base = t0 + 12 * p
                        for n in range(2):
                            dve.wait_ge(act_hid, 2 * p + n + 1)
                            dve.wait_ge(tiles_done, base + 4 * n + 4)
                            if p > 0:
                                dve.wait_ge(hid_t, 2 * p)
                            dve.tensor_tensor(hid[:, n * 512:(n + 1) * 512], bank[1][:, :], sg[:, :], ALU.mult)\
                               .then_inc(dve_hid, 1)
                        for n in range(2):
                            dve.wait_ge(tiles_done, base + 8 + 2 * n + 2)
                            dve.tensor_copy(ye[:, p, n * 512:(n + 1) * 512], bank[3 + n][:, :]).then_inc(ye_out, 1)
            counts["tiles"] += 96
            jobs = [dict(block=None, mats=[(ye[:, k, m * P:(m + 1) * P], put[:, k, :]) for k in range(KD)],
                         out=whole, eng="dve", evac=add_res(m)) for m in range(KD)]
            run_products(jobs)

        PL = ExitStack()
        with PL:
            live = PL
            hT = xT
            norm(res, hT, "g_ple", T)
            gate = sb("ple_gate", [P, KD, T])
            pT_ = sb("pleT", [P, 2, T])
            ple_loaded = sem("ple_loaded")
            with nc.Block() as block:
                @block.scalar
                def _(act):
                    act.dma_start(pT_[:, :, :], a["pT"].rearrange("(k p) n -> p k n", p=P)).then_inc(ple_loaded, 16)
                    act.wait_ge(ple_loaded, 16)
            jobs = [dict(block=WPG[m // 4], mats=fm_mats(WPG[m // 4], (m % 4) * P, hT), out=whole, eng="act",
                         evac=to(gate[:, m, :], ACT.Sigmoid)) for m in range(8)]

            def ple_evac(m):
                def evac(dve, ps, own):
                    own(dve.tensor_tensor(gate[:, m, :], ps, gate[:, m, :], ALU.mult))
                    own.wait(dve)
                    return dve.tensor_tensor(res[:, m, :], res[:, m, :], gate[:, m, :], ALU.add)
                return evac
            jobs += [dict(block=WPL, mats=[(block_ap(WPL)[:, k, m * P:(m + 1) * P], pT_[:, k, :]) for k in range(2)],
                          out=whole, eng="dve", evac=ple_evac(m), **{"with": m}) for m in range(8)]
            run_products(jobs)
            norm(res, hT, "g_last", T)
            with nc.Block() as block:
                @block.sync
                def _(sp):
                    sp.dma_start(out.rearrange("(k p) n -> p k n", p=P), hT[:, :, :]).then_inc(stored, 16)
                    sp.wait_ge(stored, 16)


WEIGHTS = ["l0_w_in", "l0_w_mem_kv", "l0_w_out", "l1_w_in", "l1_w_mem_kv", "l1_w_out", "l0_cmp_w1_k", "l0_cmp_w1_v",
           "l0_cmp_w2_k", "l0_cmp_w2_v", "w_in_2", "gla_gate_up_fwd_2", "gla_gate_up_bwd_2", "w_branch_attn_2",
           "w_branch_gla_2", "w_out_2", "w_router_2", "w_exp_gate_2", "w_exp_up_2", "w_exp_down_2", "w_ple_gate_2",
           "w_ple_2"]


def kernel(**inputs):
    import concourse.bacc as _bacc
    from concourse.bass_utils import run_bass_kernel_spmd as _run

    x = {k: np.asarray(v) for k, v in inputs.items()}

    def columns(v, k):
        return v.reshape(k, P).T

    def rows(v):
        return np.broadcast_to(v.reshape(1, -1), (P, v.size))

    parts = {
        "g_l0": columns(x["l0_norm_g"], KD), "g_mem": columns(x["mem_norm_g"], KD), "g_l1": columns(x["l1_norm_g"], KD),
        "g_fin": columns(x["final_norm_g"], KD), "g_mix": columns(x["norm_mix_2"], KD),
        "g_ffn": columns(x["norm_ffn_2"], KD), "g_ple": columns(x["norm_ple_2"], KD),
        "g_last": columns(x["norm_final_2"], KD), "g_gla": columns(x["gla_norm_2"], KD),
        "nsa_b": rows(x["l0_nsa_gate_b"]), "sink": rows(x["attn_sink_2"]),
        "bias_f": columns(x["gla_gate_bias_fwd_2"], 4), "bias_b": columns(x["gla_gate_bias_bwd_2"], 4),
        "pe_k": np.tile(x["l0_cmp_pe_k"].T, (2, 1)), "pe_v": np.tile(x["l0_cmp_pe_v"].T, (2, 1)),
    }
    consts, decay, pick = shape_constants()
    arrays = {
        "consts": consts, "decay": decay, "pick": pick,
        "vecs": np.ascontiguousarray(np.concatenate([parts[name] for name in VEC], axis=1)),
        "pos": np.ascontiguousarray(np.broadcast_to(np.stack([x["positions"][0], x["positions_2"][0]])[None], (P, 2, T))),
        "xT": np.ascontiguousarray(x["x"][0].T),
        "memT": np.ascontiguousarray(x["mem"][0].T),
        "pT": np.ascontiguousarray(x["p_2"][0, 0].T),
    }
    for name in WEIGHTS:
        arrays[name] = np.ascontiguousarray(x[name])
    nc = _bacc.Bacc("TRN2", target_bir_lowering=False, num_devices=1)
    aps = {n: nc.dram_tensor(f"in_{n}", v.shape, mybir.dt.from_np(v.dtype), kind="ExternalInput").ap()
           for n, v in arrays.items()}
    out = nc.dram_tensor("out_0", (D, T), F32, kind="ExternalOutput").ap()
    build(nc, aps, out)
    r = _run(nc, [{f"in_{n}": v for n, v in arrays.items()}], core_ids=[0])
    return np.ascontiguousarray(r.results[0]["out_0"].T)[None]
```

```python
from contextlib import ExitStack

import numpy as np
import concourse.bass as bass
from concourse import mybir

F32 = mybir.dt.float32
I32 = mybir.dt.int32
ALU = mybir.AluOpType
ACT = mybir.ActivationFunctionType
AX = mybir.AxisListType

P = 128
T = 512
TT = T // P
D = 1024
KD = D // P
MEM = 256
HD = 64
NEG = -1.0e30
EPS = 1e-6
RING = 3
WIDE = 5
SLOT = 4096
NE = 16
CAP = 64
RH = 4

CONST = {}
VEC = {}


def _place(table, parts):
    at = 0
    for name, width in parts:
        table[name] = (at, width)
        at += width
    return at


NCONST = _place(CONST, [
    ("ident", P), ("ones", P), ("causal", P), ("behind", P), ("rot", P), ("rot2", P),
    ("inv", 1), ("inv2", 1), ("invr", 1), ("one", 1), ("slot", 1), ("slots", CAP),
    ("cmp01", TT * 32), ("cmpneg", TT * 32), ("scan", T), ("fwd", P), ("bwd", P),
])
NVEC = _place(VEC, [
    ("g_l0", KD), ("g_mem", KD), ("g_l1", KD), ("g_fin", KD), ("g_mix", KD), ("g_ffn", KD), ("g_ple", KD),
    ("g_last", KD), ("g_gla", KD), ("nsa_b", 24), ("sink", 8), ("bias_f", 4), ("bias_b", 4),
    ("pe_k", 32), ("pe_v", 32),
])


def shape_constants():
    f = np.float32
    c = np.zeros((P, NCONST), f)

    def put(name, value):
        at, width = CONST[name]
        c[:, at:at + width] = np.asarray(value, f).reshape(-1, width)

    r, q = np.arange(P)[:, None], np.arange(P)[None, :]
    put("ident", r == q)
    put("ones", np.ones((P, P)))
    put("causal", np.where(q <= r, 0.0, NEG))
    put("behind", np.where(q >= r, 0.0, NEG))
    rot = np.zeros((P, P))
    rot2 = np.zeros((P, P))
    for m in range(P):
        d = m % HD
        rot[m + 32 if d < 32 else m - 32, m] = -1.0 if d < 32 else 1.0
        if d < 16:
            rot2[m + 8 if d < 8 else m - 8, m] = -1.0 if d < 8 else 1.0
    put("rot", rot)
    put("rot2", rot2)
    inv = f(1.0) / (f(10000.0) ** (np.arange(0, HD, 2, dtype=f) / f(HD)))
    put("inv", np.tile(inv, 4)[:, None])
    inv2 = f(500000.0) ** (-np.arange(0, 16, 2, dtype=f) / f(16))
    put("inv2", np.tile(np.concatenate([inv2, inv2, np.zeros(48, f)]), 2)[:, None])
    put("invr", (f(1.0) / (f(10000.0) ** np.linspace(0.0, 1.0, P, dtype=f)))[:, None])
    put("one", np.ones((P, 1)))
    put("slot", (np.arange(P) % CAP + 1)[:, None])
    put("slots", np.tile(np.arange(CAP) + 1, (P, 1)))
    t = np.arange(T)
    seen = (np.arange(32)[None, :] * 16 + 31 <= t[:, None]) & (np.arange(32)[None, :] < 31)
    seen = seen.reshape(TT, P, 32).transpose(1, 0, 2).reshape(P, TT * 32)
    put("cmp01", seen)
    put("cmpneg", np.where(seen, 0.0, NEG))
    put("scan", np.tile(t % 64 != 0, (P, 1)))
    same = r // 64 == q // 64
    put("fwd", same & (q >= r))
    put("bwd", same & (q < r))
    log_g = np.log(1.0 - 2.0 ** (-5.0 - np.arange(RH)))
    diff = t[None, None, :] - np.arange(P)[:, None, None]
    decay = np.where(diff >= 0, np.exp(np.maximum(diff, 0) * log_g[None, :, None]), 0.0) / 16.0

    pick = np.zeros((P, KD, P))
    for k in range(KD):
        for m in range(P):
            pick[2 * k + m // CAP, k, m] = 1.0
    return c, decay.reshape(P, RH * T).astype(f), pick.reshape(P, KD * P).astype(f)[:NE]


def build(nc, a, out):
    es = ExitStack()
    with es:
        live = es


        uses = {}

        def sb(name, shape, dt=F32, ctx=None):
            uses[name] = uses.get(name, 0) + 1
            name = name if uses[name] == 1 else f"{name}_{uses[name]}"
            return (ctx or live).enter_context(nc.sbuf_tensor(name, shape, dt))

        def sem(name):
            return es.enter_context(nc.semaphore(name))

        bank = [es.enter_context(nc.psum_tensor(f"bank{i}", [P, 512], F32)) for i in range(8)]
        cst = sb("cst", [P, NCONST])
        vec = sb("vec", [P, NVEC])
        ring = [sb(f"ring{i}", [P, SLOT]) for i in range(RING)]
        xT = sb("xT", [P, KD, T])

        def con(name, i=None, n=None):
            at, width = CONST[name]
            if i is not None:
                at, width = at + i * n, n
            return cst[:, at:at + width]

        def par(name, i=None):
            at, width = VEC[name]
            return vec[:, at:at + width] if i is None else vec[:, at + i:at + i + 1]

        ident = con("ident")
        ones = con("ones")

        small_loaded = sem("small_loaded")
        stored = sem("stored")
        w_loaded = [sem(f"w_loaded{i}") for i in range(WIDE)]
        tiles_done = sem("tiles_done")
        act_evac = sem("act_evac")
        dve_evac = sem("dve_evac")
        act_self = sem("act_self")
        dve_self = sem("dve_self")
        pool_self = sem("pool_self")
        pe_self = sem("pe_self")
        counts = {"tiles": 0, "act": 0, "dve": 0}

        class Own:
            def __init__(self, s):
                self.s, self.n = s, 0

            def __call__(self, ins):
                self.n += 1
                ins.then_inc(self.s, 1)
                return self.n

            def wait(self, eng, n=None):
                if (n or self.n) > 0:
                    eng.wait_ge(self.s, n or self.n)

        actq, dveq, poolq, peq = Own(act_self), Own(dve_self), Own(pool_self), Own(pe_self)

        stream = []
        last_tile = {}
        issued = [0]

        def add_block(w, rows, c0, n):
            kt = rows // P
            assert kt * n <= SLOT
            stream.append((w[:, c0:c0 + n].rearrange("(k p) n -> p k n", p=P), kt, n))
            return len(stream) - 1

        def slot(j):
            e = j - EXP[0][0]
            if e < 0:
                return j % RING
            return RING + e % WIDE if e % WIDE < WIDE - RING else (EXP[0][0] + e % WIDE - (WIDE - RING)) % RING

        def block_ap(j):
            _, kt, n = stream[j]
            return ring[slot(j)][:, 0:kt * n].rearrange("p (k n) -> p k n", k=kt)

        EVEN = {}
        w = a["l0_w_in"]
        for name, c0, n in [("nq", 0, 512), ("kv1", 512, 512), ("kv2", 1024, 280), ("nz", 1304, 512),
                            ("mq", 1816, 512), ("mk", 2328, 512), ("mv", 2840, 512), ("mz", 3352, 512),
                            ("e", 3864, 512)]:
            EVEN[name] = add_block(w, D, c0, n)
        MK0 = add_block(a["l0_w_mem_kv"], D, 0, 512)
        MK1 = add_block(a["l1_w_mem_kv"], D, 0, 512)
        w = a["l0_w_out"]
        WO0 = []
        for c in range(4):
            WO0.append(len(stream))
            stream.append((w[:, c * 256:(c + 1) * 256], 10, 256))
        ODD = [add_block(a["l1_w_in"], D, c * 512, 512) for c in range(13)]
        WO1 = [add_block(a["l1_w_out"], 18 * P, c * 128, 128) for c in range(8)]
        W2 = {}
        w = a["w_in_2"][0]
        for name, c0, n in [("aq", 0, 512), ("akv", 512, 256), ("gq", 768, 512), ("gk", 1280, 512),
                            ("gv0", 1792, 512), ("gv1", 2304, 512), ("gr0", 2816, 512), ("gr1", 3328, 512),
                            ("z", 3840, 32), ("ga0", 3872, 512), ("ga1", 4384, 512), ("gg0", 4896, 512),
                            ("gg1", 5408, 512)]:
            W2[name] = add_block(w, D, c0, n)
        WBA = len(stream)
        stream.append((a["w_branch_attn_2"][0], 4, 1024))
        WBG = [add_block(a["w_branch_gla_2"][0], D, c * 512, 512) for c in range(2)]
        WO2 = [add_block(a["w_out_2"][0], D, c * 512, 512) for c in range(2)]
        EXP = []
        for p in range(NE // 2):
            blocks = []
            for n in range(2):
                for w in ("w_exp_gate_2", "w_exp_up_2"):
                    for e in range(2):
                        blocks.append(add_block(a[w][0, 2 * p + e], D, n * 512, 512))
            for n in range(2):
                for e in range(2):
                    blocks.append(add_block(a["w_exp_down_2"][0, 2 * p + e], D, n * 512, 512))
            EXP.append(blocks)
        WPG = [add_block(a["w_ple_gate_2"][0], D, c * 512, 512) for c in range(2)]
        WPL = add_block(a["w_ple_2"][0], 256, 0, 1024)

        def load_special(sp, j):
            dst = block_ap(j)
            view, kt, n = stream[j]
            s = w_loaded[slot(j)]
            if j in paired:
                for g in range(2):
                    for k in range(kt):
                        sp.dma_start(dst[:, k, :].rearrange("p (i g d) -> p g i d", g=2, i=4)[:, g],
                                     view[:, k, :].rearrange("p (g i d) -> p g i d", g=2, i=4)[:, g]).then_inc(s, 16)
                return
            pairs = view[0:512, :].rearrange("(g i d) n -> g d i n", g=2, i=4)
            for g in range(2):
                sp.dma_start(dst[g * 64:(g + 1) * 64, 0:4, :], pairs[g]).then_inc(s, 16)
            if kt > 4:
                sp.dma_start(dst[:, 4:kt, :], view[512:kt * P, :].rearrange("(k p) n -> p k n", p=P)).then_inc(s, 16)

        paired = {EVEN["nq"], EVEN["nz"], W2["aq"]}
        special = set(WO0) | {WBA} | paired
        loads_of = {}
        level = [0] * WIDE
        for j in range(len(stream)):
            level[slot(j)] += 16 * (1 if j not in special else (3 if j in WO0 else 16 if j in paired else 2))
            loads_of[j] = level[slot(j)]

        def issue_blocks(sp, upto):
            while issued[0] < min(upto, len(stream)):
                j = issued[0]
                last = j - (RING if j < EXP[0][0] else WIDE)
                if last >= 0 and j not in EXP[0][0:WIDE - RING]:
                    sp.wait_ge(tiles_done, last_tile[last])
                if j in special:
                    load_special(sp, j)
                else:
                    sp.dma_start(block_ap(j), stream[j][0]).then_inc(w_loaded[slot(j)], 16)
                issued[0] += 1

        def wait_block(pe, j):
            pe.wait_ge(w_loaded[slot(j)], loads_of[j])

        def run_products(jobs, banks=6, first=None, last=None):
            t0, a0, d0 = counts["tiles"], counts["act"], counts["dve"]
            done_at = []
            na, nd = a0, d0
            for n, job in enumerate(jobs):
                if job["eng"] == "act":
                    na += 1
                    done_at.append((act_evac, na))
                else:
                    nd += 1
                    done_at.append((dve_evac, nd))
                if job.get("block") is not None:
                    last_tile[job["block"]] = t0 + n + 1
            used = [j["block"] for j in jobs if j.get("block") is not None]
            if last is not None:
                last["tiles"].extend(done_at[n] for n in last["of"])
            with nc.Block() as block:
                @block.sync
                def _(sp):
                    if used:
                        m = max(used)
                        issue_blocks(sp, min(m + RING + 1, EXP[0][0]) if m < EXP[0][0] else m + WIDE + 1)
                    if last is not None and "sync" in last:
                        last["sync"](sp)

                @block.tensor
                def _(pe):
                    waited = set()
                    if first is not None:
                        first["pe"](pe)
                    for n, job in enumerate(jobs):
                        if job.get("block") is not None and job["block"] not in waited:
                            waited.add(job["block"])
                            wait_block(pe, job["block"])
                        if n >= banks:
                            pe.wait_ge(*done_at[n - banks])
                        if job.get("after") is not None:
                            pe.wait_ge(*done_at[job["after"]])
                        o = job["out"](bank[n % banks])
                        mats = job["mats"]
                        for i, (l, r) in enumerate(mats):
                            if n == 0 and first is not None:
                                pe.wait_ge(dve_self, first["ready"][i])
                            mm = pe.matmul(o, l, r, start=i == 0, stop=i == len(mats) - 1)
                        mm.then_inc(tiles_done, 1)
                    if last is not None:
                        last["pe"](pe)

                def taker(kind, own, s):
                    def body(eng):
                        if first is not None:
                            first[kind](eng)
                        mine = None
                        for n, job in enumerate(jobs):
                            if job["eng"] == kind:
                                if mine is not None and kind == "dve":
                                    eng.wait_ge(*mine)
                                mine = done_at[n]
                                eng.wait_ge(tiles_done, t0 + n + 1)
                                if job.get("with") is not None:
                                    eng.wait_ge(*done_at[job["with"]])
                                job["evac"](eng, job["out"](bank[n % banks]), own).then_inc(s, 1)
                        if last is not None:
                            last[kind](eng)
                    return body

                block.scalar(taker("act", actq, act_evac))
                block.vector(taker("dve", dveq, dve_evac))
            counts["tiles"] += len(jobs)
            counts["act"], counts["dve"] = na, nd

        def whole(b):
            return b[:, :]

        def to(dst, func=None, scale=1.0):
            def evac(eng, ps, own):
                if eng is nc.scalar or own is actq:
                    return eng.activation(dst, ps, func or ACT.Copy, scale=scale)
                if scale != 1.0:
                    return eng.tensor_scalar(dst, ps, scale, None, ALU.mult)
                return eng.tensor_copy(dst, ps)
            return evac

        def fm_mats(j, c, src, n=P, kt=KD):
            wb = block_ap(j)
            return [(wb[:, k, c:c + n], src[:, k, :]) for k in range(kt)]

        def tm_mats(j, c, n, src, t, kt=KD):
            wb = block_ap(j)
            return [(src[:, k, t * P:(t + 1) * P], wb[:, k, c:c + n]) for k in range(kt)]

        def norm_parts(x, h, gain, rs, kt=KD, width=D, behind=(0, 0, 0), of=None, sq=None):
            ps = bank[6][:, 0:rs.shape[-1]]
            a1, p1, d1 = actq.n + behind[0], peq.n + behind[1], dveq.n + behind[2]
            tiles = []
            sq = h if sq is None else sq

            def on_act(act):
                for k in range(kt):
                    if tiles:
                        act.wait_ge(*tiles[k])
                    actq(act.activation(sq[:, k, :], x[:, k, :], ACT.Square))
                act.wait_ge(dve_self, d1 + 1)
                actq(act.activation(rs, rs, ACT.Sqrt))

            def on_pe(pe):
                for k in range(kt):
                    pe.wait_ge(act_self, a1 + k + 1)
                    mm = pe.matmul(ps, ones, sq[:, k, :], start=k == 0, stop=k == kt - 1)
                peq(mm)

            def on_dve(dve):
                dve.wait_ge(pe_self, p1 + 1)
                dveq(dve.tensor_scalar(rs, ps, 1.0 / width, EPS, ALU.mult, ALU.add))
                dve.wait_ge(act_self, a1 + kt + 1)
                dveq(dve.reciprocal(rs, rs))
                dveq.wait(dve)
                for k in range(kt):
                    dveq(dve.scalar_tensor_tensor(h[:, k, :], x[:, k, :], par(gain, k), rs, ALU.mult, ALU.mult))
            return dict(act=on_act, pe=on_pe, dve=on_dve, ready=[d1 + 3 + k for k in range(kt)], acts=kt + 1,
                        of=of, tiles=tiles)

        def norm(x, h, gain, n, kt=KD, width=D):
            st = ExitStack()
            with st:
                parts = norm_parts(x, h, gain, sb("norm_rs", [P, n], ctx=st)[:, :], kt, width)
                with nc.Block() as block:
                    block.scalar(parts["act"])
                    block.tensor(parts["pe"])
                    block.vector(parts["dve"])

        def tables(position, inv, cos, sin, ang, u, kk, before):
            C1, C2 = 6.28125, 0.0019350051879882812
            C3 = float(2 * np.pi - C1 - C2)
            MAGIC = 12582912.0
            reduced = dveq.n + len(before["ready"]) + 2 + 2 + 2 * 8
            sines = actq.n + before["acts"] + 2

            def on_dve(dve):
                before["dve"](dve)

                def step(ins):
                    dveq(ins)
                    dveq.wait(dve)
                step(dve.tensor_copy(ang, position))
                step(dve.tensor_scalar(ang, ang, inv, None, ALU.mult))
                for dst, turn in ((cos, 0.25), (sin, 0.0)):
                    step(dve.tensor_scalar(u, ang, float(1 / (2 * np.pi)), turn, ALU.mult, ALU.add))
                    step(dve.tensor_scalar(kk, u, MAGIC, None, ALU.add))
                    step(dve.tensor_scalar(kk, kk, MAGIC, None, ALU.subtract))
                    step(dve.scalar_tensor_tensor(u, kk, -C1, ang, ALU.mult, ALU.add))
                    step(dve.scalar_tensor_tensor(u, kk, -C2, u, ALU.mult, ALU.add))
                    step(dve.scalar_tensor_tensor(u, kk, -C3, u, ALU.mult, ALU.add))
                    step(dve.tensor_scalar(u, u, float(turn * 2 * np.pi), 3.1415925, ALU.add, ALU.min))
                    step(dve.tensor_scalar(dst, u, -3.1415925, None, ALU.max))
                dve.wait_ge(act_self, sines)

            def on_act(act):
                before["act"](act)
                act.wait_ge(dve_self, reduced)
                actq(act.activation(cos, cos, ACT.Sin))
                actq(act.activation(sin, sin, ACT.Sin))
            return dict(dve=on_dve, act=on_act, pe=before["pe"], ready=before["ready"])

        s_ready, m_ready, e_done = sem("s_ready"), sem("m_ready"), sem("e_done")
        t_ready, t_out, o_ready, o_out = sem("t_ready"), sem("t_out"), sem("o_ready"), sem("o_out")
        att = {"u": 0, "g": 0}

        def attention(groups, ctx):
            wk = max(u[1].shape[-1] for grp in groups for u in grp["units"])
            wv = max(P * len(u[3]) for grp in groups for u in grp["units"])
            pr = [sb(f"att_p{i}", [P, max(wk, wv)], ctx=ctx) for i in range(4)]
            pt = [sb(f"att_pt{i}", [P, wv], ctx=ctx) for i in range(4)]
            nmax = sb("att_nmax", [P, 4, 8], ctx=ctx)
            total = sb("att_sum", [P, 4, 8], ctx=ctx)
            rinv = sb("att_rinv", [P, 8], ctx=ctx)
            esink = sb("att_esink", [P, 8], ctx=ctx)
            units = [(g, i, u) for g, grp in enumerate(groups) for i, u in [(i, grp["units"][i]) for i in grp.get("order", range(len(grp["units"])))]]
            U, u0, g0 = len(units), att["u"], att["g"]
            S, TP, O = bank[0:4], bank[4:6], bank[6:8]
            ends, starts = {}, {}
            for n, (g, i, u) in enumerate(units):
                ends[g] = n
                starts.setdefault(g, n)
            with nc.Block() as block:
                @block.tensor
                def _(pe):
                    for m in range(0, U + 4, 2):
                        for n in range(m, min(m + 2, U)):
                            g, i, (q, k, masks, vals) = units[n]
                            if n >= 4:
                                pe.wait_ge(e_done, u0 + n - 3)
                            w = k.shape[-1]
                            pe.matmul(S[n % 4][:, 0:w], q, k, start=True, stop=True).then_inc(s_ready, 1)
                        for v in range(max(m - 2, 0), min(m, U)):
                            pe.wait_ge(e_done, u0 + v + 1)
                            if v >= 2:
                                pe.wait_ge(t_out, u0 + v - 1)
                            nb = len(units[v][2][3])
                            for b in range(nb):
                                mm = pe.transpose(TP[v % 2][:, b * P:(b + 1) * P],
                                                  pr[v % 4][:, b * P:(b + 1) * P], ident)
                            mm.then_inc(t_ready, 1)
                        for v in range(max(m - 4, 0), min(m - 2, U)):
                            g, i, (q, k, masks, vals) = units[v]
                            pe.wait_ge(t_out, u0 + v + 1)
                            if v == starts[g] and g >= 2:
                                pe.wait_ge(o_out, g0 + g - 1)
                            for b, val in enumerate(vals):
                                mm = pe.matmul(O[g % 2][:, i * HD:(i + 1) * HD], pt[v % 4][:, b * P:(b + 1) * P],
                                               val, start=b == 0, stop=b == len(vals) - 1)
                            mm.then_inc(o_ready, 1)

                @block.vector
                def _(dve):
                    def finish(g):
                        grp = groups[g]
                        nu = len(grp["units"])
                        dve.wait_ge(o_ready, u0 + ends[g] + 1)
                        tot = total[:, g % 4, 0:nu]
                        if grp.get("sink") is not None:
                            dve.wait_ge(act_self, grp["sink_at"])
                            dveq(dve.tensor_tensor(tot, tot, esink[:, 0:nu], ALU.add))
                            dveq.wait(dve)
                        dveq(dve.reciprocal(rinv[:, 0:nu], tot))
                        dveq.wait(dve)
                        grp["evac"](dve, O[g % 2], rinv[:, 0:nu]).then_inc(o_out, 1)
                        dve.wait_ge(o_out, g0 + g + 1)

                    for m in range(0, U + 6, 2):
                        for n in range(m, min(m + 2, U)):
                            g, i, (q, k, masks, vals) = units[n]
                            dve.wait_ge(s_ready, u0 + n + 1)
                            for c, mask in masks:
                                dveq(dve.tensor_tensor(S[n % 4][:, c:c + P], S[n % 4][:, c:c + P], mask, ALU.add))
                        for n in range(m, min(m + 2, U)):
                            g, i, (q, k, masks, vals) = units[n]
                            if masks:
                                dveq.wait(dve)
                            nm = nmax[:, g % 4, i:i + 1]
                            ins = dve.tensor_reduce(nm, S[n % 4][:, 0:k.shape[-1]], AX.X, ALU.max, negate=True)
                            if groups[g].get("sink") is not None:
                                dveq(ins)
                                dveq.wait(dve)
                                ins = dve.tensor_tensor(nm, nm, groups[g]["sink"][:, i:i + 1], ALU.min)
                            ins.then_inc(m_ready, 1)
                        for v in range(max(m - 6, 0), min(m - 4, U)):
                            if ends[units[v][0]] == v:
                                finish(units[v][0])

                @block.scalar
                def _(act):
                    for m in range(0, U + 2, 2):
                        for n in range(m, min(m + 2, U)):
                            g, i, (q, k, masks, vals) = units[n]
                            w = k.shape[-1]
                            act.wait_ge(m_ready, u0 + n + 1)
                            if n >= 4:
                                act.wait_ge(t_ready, u0 + n - 3)
                            act.activation(pr[n % 4][:, 0:w], S[n % 4][:, 0:w], ACT.Exp,
                                           bias=nmax[:, g % 4, i:i + 1],
                                           accum_out=total[:, g % 4, i:i + 1]).then_inc(e_done, 1)
                        for v in range(max(m - 2, 0), min(m, U)):
                            w = P * len(units[v][2][3])
                            act.wait_ge(t_ready, u0 + v + 1)
                            if v >= 4:
                                act.wait_ge(o_ready, u0 + v - 3)
                            act.activation(pt[v % 4][:, 0:w], TP[v % 2][:, 0:w], ACT.Copy).then_inc(t_out, 1)
                            g, i, _ = units[v]
                            if groups[g].get("sink") is not None and ends[g] == v:
                                nu = len(groups[g]["units"])
                                if g >= 1:
                                    act.wait_ge(o_out, g0 + g)
                                for k2 in range(nu):
                                    actq(act.activation(esink[:, k2:k2 + 1], groups[g]["plus"][:, k2:k2 + 1], ACT.Exp,
                                                        bias=nmax[:, g % 4, k2:k2 + 1]))
            att["u"] += U
            att["g"] += len(groups)

        pos = es.enter_context(nc.sbuf_tensor("pos", [P, 2, T], I32))
        MKV = ExitStack()
        memk = [sb(f"memk{i}", [P, 2, MEM], ctx=MKV) for i in range(2)]
        memv = [sb(f"memv{i}", [P, 2, MEM], ctx=MKV) for i in range(2)]
        L0 = ExitStack()
        proj = sb("proj0", [P, 28, T], ctx=L0)
        memT = proj[:, 24:28, :].rearrange("p a (b n) -> p (a b) n", n=MEM)
        memory_loaded = sem("memory_loaded")
        with nc.Block() as block:
            @block.scalar
            def _(act):
                act.dma_start(cst[:, :], a["consts"]).then_inc(small_loaded, 16)
                act.dma_start(vec[:, :], a["vecs"]).then_inc(small_loaded, 16)
                act.dma_start(pos[:, :, :], a["pos"]).then_inc(small_loaded, 16)
                act.dma_start(xT[:, :, :], a["xT"].rearrange("(k p) n -> p k n", p=P)).then_inc(small_loaded, 16)
                act.dma_start(memT, a["memT"].rearrange("(k p) n -> p k n", p=P)).then_inc(memory_loaded, 16)
                act.wait_ge(small_loaded, 64)

            @block.sync
            def _(sp):
                issue_blocks(sp, RING)

        with L0:
            live = L0
            gates = sb("nsa_gates", [P, TT, 24])
            NQ, NKC, NVC, NKS, NKW, NZ, MQ, MK, MZ, EQ, EZ = 0, 4, 5, 6, 7, 8, 12, 16, 20, 24, 26
            nvs = sb("nvs", [P, TT, P])
            nvw = sb("nvw", [P, TT, P])
            mv = sb("mv", [P, TT, 512])
            kc = sb("kc", [P, 32])
            vcd = sb("vcd", [P, 2, 4, HD])
            CW = ExitStack()
            w1 = sb("cmp_w1", [P, 2, 32, HD], ctx=CW)
            w2 = sb("cmp_w2", [P, 2, HD], ctx=CW)
            cmp_loaded = sem("cmp_loaded")
            PR = ExitStack()
            with PR:
                cos = sb("cos", [P, T], ctx=PR)
                sin = sb("sin", [P, T], ctx=PR)
                MM = ExitStack()
                with MM:
                    memh = sb("memh", [P, KD, MEM], ctx=MM)
                    with nc.Block() as block:
                        @block.scalar
                        def _(act):
                            for i, kv in enumerate("kv"):
                                for g in range(2):
                                    act.dma_start(w1[g * 64:(g + 1) * 64, i], a[f"l0_cmp_w1_{kv}"]
                                                  .rearrange("l d e -> d l e")).then_inc(cmp_loaded, 16)
                                    act.dma_start(w2[g * 64:(g + 1) * 64, i], a[f"l0_cmp_w2_{kv}"]).then_inc(cmp_loaded, 16)
                            act.wait_ge(memory_loaded, 16)
                    norm(memT, memh, "g_mem", MEM)
                    hT = sb("hT0", [P, KD, T], ctx=MM)
                    normed = norm_parts(xT, hT, "g_l0", proj[:, MZ + 3, :])
                    tmp = sb("rot_tmp", [P, 2, T], ctx=MM)
                    jobs = []

                    def fm(j, c, tile, func=None, scale=1.0, eng=None):
                        mats = fm_mats(j, c, hT)
                        jobs.append(dict(block=j, mats=mats, out=whole, eng=eng or ("act" if len(jobs) % 2 else "dve"),
                                         evac=to(proj[:, tile, :], func, scale)))
                        return len(jobs) - 1

                    def rotary(tile, src, rot, scale=1.0):
                        x = proj[:, tile, :]

                        def evac(dve, ps, own):
                            own(dve.tensor_tensor(tmp[:, 0, :], ps, sin[:, :], ALU.mult))
                            own(dve.tensor_tensor(tmp[:, 1, :], x, cos[:, :], ALU.mult))
                            own.wait(dve)
                            if scale == 1.0:
                                ins = dve.tensor_tensor(x, tmp[:, 0, :], tmp[:, 1, :], ALU.add)
                            else:
                                own(dve.tensor_tensor(tmp[:, 0, :], tmp[:, 0, :], tmp[:, 1, :], ALU.add))
                                own.wait(dve)
                                ins = dve.tensor_scalar(x, tmp[:, 0, :], scale, None, ALU.mult)
                            return ins
                        jobs.append(dict(block=None, mats=[(rot, x)], out=whole, eng="dve", evac=evac, after=src))

                    def tm(j, c, n, dst, t, eng=None, func=None):
                        jobs.append(dict(block=j, mats=tm_mats(j, c, n, hT, t), out=lambda b: b[:, 0:n],
                                         eng=eng or ("act" if len(jobs) % 2 else "dve"), evac=to(dst, func)))
                        return len(jobs) - 1

                    rot = con("rot")
                    wait_rot = []

                    def later(*x):
                        wait_rot.append(x)

                    def flush():
                        for x in wait_rot:
                            rotary(*x)
                        wait_rot.clear()

                    for i in range(4):
                        later(NQ + i, fm(EVEN["nq"], i * P, NQ + i, eng="act"), rot, 0.125)
                    j = EVEN["kv1"]
                    c = fm(j, 0, NKC, eng="act")
                    fm(j, 128, NVC, eng="act")
                    flush()
                    later(NKC, c, rot)
                    later(NKS, fm(j, 256, NKS, eng="act"), rot)
                    for t in range(TT):
                        tm(j, 384, 128, nvs[:, t, :], t, eng="act")
                    flush()
                    j = EVEN["kv2"]
                    later(NKW, fm(j, 0, NKW, eng="act"), rot)
                    for t in range(TT):
                        tm(j, 128, 128, nvw[:, t, :], t, eng="act")

                    def gate_evac(t):
                        def evac(dve, ps, own):
                            return dve.tensor_tensor(gates[:, t, :], ps, par("nsa_b"), ALU.add)
                        return evac
                    for t in range(TT):
                        jobs.append(dict(block=j, mats=tm_mats(j, 256, 24, hT, t), out=lambda b: b[:, 0:24], eng="dve",
                                         evac=gate_evac(t)))
                    flush()
                    for i in range(4):
                        fm(EVEN["nz"], i * P, NZ + i, ACT.Silu, eng="act")
                    for i in range(4):
                        later(MQ + i, fm(EVEN["mq"], i * P, MQ + i, eng="act"), rot, 0.125)
                    c = [fm(EVEN["mk"], i * P, MK + i, eng="act") for i in range(2)]
                    flush()
                    c += [fm(EVEN["mk"], i * P, MK + i, eng="act") for i in range(2, 4)]
                    for i in range(4):
                        later(MK + i, c[i], rot)
                    for t in range(TT):
                        tm(EVEN["mv"], 0, 512, mv[:, t, :], t, eng="act")
                    flush()
                    for i in range(4):
                        fm(EVEN["mz"], i * P, MZ + i, ACT.Silu, eng="act")
                    for i in range(2):
                        fm(EVEN["e"], i * P, EQ + i, scale=0.125, eng="dve")
                    for i in range(2):
                        fm(EVEN["e"], 256 + i * P, EZ + i, ACT.Silu, eng="act")
                    for l, j in enumerate((MK0, MK1)):
                        for i in range(2):
                            jobs.append(dict(block=j, mats=[(block_ap(j)[:, k, i * P:(i + 1) * P], memh[:, k, :])
                                                            for k in range(KD)],
                                             out=lambda b: b[:, 0:MEM], eng="dve", evac=to(memk[l][:, i, :])))
                        for t in range(2):
                            jobs.append(dict(block=j, mats=[(memh[:, k, t * P:(t + 1) * P], block_ap(j)[:, k, 256:512])
                                                            for k in range(KD)],
                                             out=lambda b: b[:, 0:MEM], eng="act", evac=to(memv[l][:, t, :])))
                    run_products(jobs, first=tables(pos[:, 0, :], con("inv"), cos[:, :], sin[:, :],
                                                    *[proj[:, MZ + i, :] for i in range(3)], normed))

            CM = ExitStack()
            with CM:
                CA = ExitStack()
                with CA:
                    blocks = sb("cmp_blocks", [P, 2, 32, 31], ctx=CA)
                    hid = sb("cmp_hid", [P, 2, 31], ctx=CA)
                    d1, p1, a1, g1 = dveq.n, peq.n, actq.n, poolq.n
                    with nc.Block() as block:
                        @block.vector
                        def _(dve):
                            for i, tile in enumerate((NKC, NVC)):
                                src = proj[:, tile, :]
                                for half in range(2):
                                    at = src[:, 16 * half:16 * half + 496].rearrange("p (n l) -> p l n", l=16)
                                    pe_ = par("pe_k" if i == 0 else "pe_v")[:, 16 * half:16 * half + 16]
                                    dveq(dve.tensor_tensor(blocks[:, i, 16 * half:16 * half + 16, :], at,
                                                           pe_.unsqueeze(2).to_broadcast([P, 16, 31]), ALU.add))
                            dveq(dve.memset(kc[:, :], 0.0))
                            dveq(dve.memset(vcd[:, :, :, :], 0.0))

                        @block.scalar
                        def _(act):
                            act.wait_ge(pe_self, p1 + 1)
                            actq(act.activation(hid[:, :, :], bank[0][:, 0:64].rearrange("p (i n) -> p i n", i=2)[:, :, 0:31],
                                                ACT.Silu))
                            act.wait_ge(pe_self, p1 + 2)
                            act.wait_ge(dve_self, d1 + 6)
                            actq(act.activation(kc[:, 0:31], bank[1][:, 0:31], ACT.Copy))
                            for g in range(2):
                                for i in range(4):
                                    actq(act.activation(vcd[32 * i:32 * i + 31, g, i, :],
                                                        bank[2 + g][0:31, 0:HD], ACT.Copy))
                            for t in range(TT):
                                actq(act.activation(gates[:, t, :], gates[:, t, :], ACT.Sigmoid))

                        @block.tensor
                        def _(pe):
                            pe.wait_ge(cmp_loaded, 128)
                            pe.wait_ge(dve_self, d1 + 4)
                            for g in range(2):
                                r = slice(g * 64, (g + 1) * 64)
                                for i in range(2):
                                    for l in range(32):
                                        mm = pe.matmul(bank[0][r, 32 * i:32 * i + 31], w1[r, i, l, :], blocks[r, i, l, :],
                                                       start=l == 0, stop=l == 31)
                            peq(mm)
                            pe.wait_ge(act_self, a1 + 1)
                            for g in range(2):
                                r = slice(g * 64, (g + 1) * 64)
                                pe.matmul(bank[1][r, 0:31], w2[r, 0, :], hid[r, 0, :], start=True, stop=True)
                            for g in range(2):
                                r = slice(g * 64, (g + 1) * 64)
                                mm = pe.matmul(bank[2 + g][0:31, 0:HD], hid[r, 1, :], w2[r, 1, :],
                                               start=True, stop=True)
                            peq(mm)

                CW.close()
                oacc = sb("nsa_out", [P, TT, 8, HD], ctx=CM)
                C2 = ExitStack()
                with C2:
                    sc = sb("cmp_s", [P, TT, 8, 32], ctx=C2)
                    mx = sb("cmp_m", [P, TT, 8], ctx=C2)
                    sm = sb("cmp_sum", [P, TT, 8], ctx=C2)
                    pT = sb("cmp_pt", [P, TT, 2, P], ctx=C2)
                    m01 = con("cmp01").rearrange("p (t n) -> p t n", t=TT).unsqueeze(2)
                    neg = con("cmpneg").rearrange("p (t n) -> p t n", t=TT).unsqueeze(2)
                    d1, p1, a1 = dveq.n, peq.n, actq.n
                    with nc.Block() as block:
                        @block.tensor
                        def _(pe):
                            for t in range(TT):
                                for h in range(8):
                                    g, i = h // 4, h % 4
                                    r = slice(g * 64, (g + 1) * 64)
                                    mm = pe.matmul(bank[g][:, t * P + i * 32:t * P + (i + 1) * 32],
                                                   proj[r, NQ + i, t * P:(t + 1) * P], kc[r, :], start=True, stop=True)
                            peq(mm)
                            pe.wait_ge(dve_self, d1 + 6)
                            for t in range(TT):
                                for g in range(2):
                                    c = (t % 2) * 256 + g * P
                                    mm = pe.transpose(bank[2 + t // 2][:, c:c + P],
                                                      sc[:, t, 4 * g:4 * g + 4, :].rearrange("p i n -> p (i n)"), ident)
                                if t % 2 == 1:
                                    peq(mm)
                            for t in range(TT):
                                pe.wait_ge(act_self, a1 + 2 + t // 2)
                                for g in range(2):
                                    mm = pe.matmul(bank[4 + t][:, g * 256:(g + 1) * 256], pT[:, t, g, :],
                                                   vcd[:, g, :, :].rearrange("p i d -> p (i d)"), start=True, stop=True)
                                peq(mm)

                        @block.vector
                        def _(dve):
                            def step(ins):
                                dveq(ins)
                                dveq.wait(dve)
                            dve.wait_ge(pe_self, p1 + 1)
                            for g in range(2):
                                dveq(dve.tensor_tensor(sc[:, :, 4 * g:4 * g + 4, :],
                                                       bank[g][:, :].rearrange("p (t i n) -> p t i n", t=TT, i=4),
                                                       m01.to_broadcast([P, TT, 4, 32]), ALU.mult))
                            dveq.wait(dve)
                            step(dve.tensor_tensor(sc[:, :, :, :], sc[:, :, :, :], neg.to_broadcast([P, TT, 8, 32]), ALU.add))
                            step(dve.tensor_reduce(mx[:, :, :], sc[:, :, :, :], AX.X, ALU.max))
                            step(dve.tensor_tensor(sc[:, :, :, :], sc[:, :, :, :],
                                                   mx[:, :, :].unsqueeze(3).to_broadcast([P, TT, 8, 32]), ALU.subtract))
                            dve.wait_ge(act_self, a1 + 1)
                            step(dve.tensor_tensor(sc[:, :, :, :], sc[:, :, :, :], m01.to_broadcast([P, TT, 8, 32]), ALU.mult))
                            step(dve.tensor_reduce(sm[:, :, :], sc[:, :, :, :], AX.X, ALU.add))
                            step(dve.tensor_scalar(sm[:, :, :], sm[:, :, :], 1e-30, None, ALU.max))
                            step(dve.reciprocal(sm[:, :, :], sm[:, :, :]))
                            step(dve.tensor_tensor(sm[:, :, :], sm[:, :, :], gates[:, :, 0:8], ALU.mult))
                            for t in range(TT):
                                dve.wait_ge(pe_self, p1 + 4 + t)
                                dveq(dve.tensor_tensor(oacc[:, t, :, :], bank[4 + t][:, :].rearrange("p (h d) -> p h d", d=HD),
                                                       sm[:, t, :].unsqueeze(2).to_broadcast([P, 8, HD]), ALU.mult))

                        @block.scalar
                        def _(act):
                            act.wait_ge(dve_self, d1 + 5)
                            actq(act.activation(sc[:, :, :, :], sc[:, :, :, :], ACT.Exp))
                            for i in range(2):
                                act.wait_ge(pe_self, p1 + 2 + i)
                                actq(act.activation(pT[:, 2 * i:2 * i + 2, :, :],
                                                    bank[2 + i][:, :].rearrange("p (t g n) -> p t g n", t=2, g=2), ACT.Copy))

                causal = con("causal")
                tmpo = sb("att_tmpo", [P, 8, HD], ctx=CM)

                def units_of(t, qs, ks, vs):
                    return [(q[:, t * P:(t + 1) * P], k[:, 0:(t + 1) * P], [(t * P, causal)],
                             [v(b) for b in range(t + 1)]) for q, k, v in zip(qs, ks, vs)]

                def head(tile, h):
                    return proj[h * 64:(h + 1) * 64, tile, :]

                def values(v, h):
                    return lambda b: v[:, b, h * HD:(h + 1) * HD]

                def add_evac(t, branch):
                    def evac(dve, ps, r):
                        dveq(dve.tensor_tensor(r, r, gates[:, t, 8 * branch:8 * branch + 8], ALU.mult))
                        dveq.wait(dve)
                        dveq(dve.tensor_tensor(tmpo[:, :, :], ps[:, :].rearrange("p (h d) -> p h d", d=HD),
                                               r.unsqueeze(2).to_broadcast([P, 8, HD]), ALU.mult))
                        dveq.wait(dve)
                        return dve.tensor_tensor(oacc[:, t, :, :], oacc[:, t, :, :], tmpo[:, :, :], ALU.add)
                    return evac

                def set_evac(dst, n):
                    def evac(dve, ps, r):
                        return dve.tensor_tensor(dst, ps[:, 0:n * HD].rearrange("p (h d) -> p h d", d=HD),
                                                 r.unsqueeze(2).to_broadcast([P, n, HD]), ALU.mult)
                    return evac

                groups = []
                for branch, kt_, v in ((1, NKS, nvs), (2, NKW, nvw)):
                    for t in range(TT):
                        groups.append(dict(units=units_of(t, [head(NQ + h % 4, h // 4) for h in range(8)],
                                                          [head(kt_, h // 4) for h in range(8)],
                                                          [values(v, h // 4) for h in range(8)]),
                                           evac=add_evac(t, branch), order=[0, 4, 1, 5, 2, 6, 3, 7]))
                moba = sb("moba_out", [P, TT, 8, HD], ctx=CM)
                for t in range(TT):
                    groups.append(dict(units=units_of(t, [head(MQ + h // 2, h % 2) for h in range(8)],
                                                      [head(MK + h // 2, h % 2) for h in range(8)],
                                                      [values(mv, h) for h in range(8)]),
                                       evac=set_evac(moba[:, t, :, :], 8)))
                memo = sb("mem_out", [P, TT, 4, HD], ctx=CM)
                for t in range(TT):
                    groups.append(dict(units=[(head(EQ + h // 2, h % 2)[:, t * P:(t + 1) * P],
                                               memk[0][(h % 2) * 64:(h % 2) * 64 + 64, h // 2, :], [],
                                               [memv[0][:, b, h * HD:(h + 1) * HD] for b in range(2)]) for h in range(4)],
                                       evac=set_evac(memo[:, t, :, :], 4)))
                AT = ExitStack()
                with AT:
                    attention(groups, AT)

                def gate_back(src, gate0, pairs, npair):
                    for t in range(TT):
                        for i in range(npair):
                            s = src[:, t, :, :]
                            l = (s.rearrange("p (g i) d -> p i g d", g=2)[:, i] if pairs else s[:, 2 * i:2 * i + 2, :])
                            yield t, gate0 + i, l
                items = [*gate_back(oacc, NZ, True, 4), *gate_back(moba, MZ, False, 4), *gate_back(memo, EZ, False, 2)]
                stage = sb("back", [P, 2, P], ctx=CM)
                back_in, back_t, back_out = sem("back_in"), sem("back_t"), sem("back_out")
                with nc.Block() as block:
                    @block.scalar
                    def _(act):
                        for n, (t, tile, l) in enumerate(items):
                            if n >= 2:
                                act.wait_ge(back_t, n - 1)
                            act.activation(stage[:, n % 2, :].rearrange("p (g d) -> p g d", g=2), l, ACT.Copy)\
                               .then_inc(back_in, 1)

                    @block.tensor
                    def _(pe):
                        for n, (t, tile, l) in enumerate(items):
                            pe.wait_ge(back_in, n + 1)
                            if n >= 2:
                                pe.wait_ge(back_out, n - 1)
                            pe.transpose(bank[n % 2][:, 0:P], stage[:, n % 2, :], ident).then_inc(back_t, 1)

                    @block.vector
                    def _(dve):
                        for n, (t, tile, l) in enumerate(items):
                            dve.wait_ge(back_t, n + 1)
                            y = proj[:, tile, t * P:(t + 1) * P]
                            dve.tensor_tensor(y, bank[n % 2][:, 0:P], y, ALU.mult).then_inc(back_out, 1)

            yt = [NZ, NZ + 1, NZ + 2, NZ + 3, MZ, MZ + 1, MZ + 2, MZ + 3, EZ, EZ + 1]
            jobs = []

            def add_to(m):
                def evac(dve, ps, own):
                    return dve.tensor_tensor(xT[:, m, :], ps, xT[:, m, :], ALU.add)
                return evac
            for c, j in enumerate(WO0):
                for m in range(2):
                    jobs.append(dict(block=j, mats=[(block_ap(j)[:, k, m * P:(m + 1) * P], proj[:, yt[k], :])
                                                    for k in range(10)],
                                     out=whole, eng="dve", evac=add_to(2 * c + m)))
            run_products(jobs)

        L1 = ExitStack()
        with L1:
            live = L1
            RQ, RK, RZ, EQ, EZ = 0, 8, 16, 32, 34
            proj = sb("proj1", [P, 36, T])
            rv = sb("rv", [P, TT, 2048])
            H1 = ExitStack()
            with H1:
                hT = sb("hT1", [P, KD, T], ctx=H1)
                normed = norm_parts(xT, hT, "g_l1", proj[:, RZ + 6, :])
                jobs = []

                def fm1(j, c, tile, func=None, scale=1.0, eng=None):
                    jobs.append(dict(block=j, mats=fm_mats(j, c, hT), out=whole,
                                     eng=eng or ("act" if func or len(jobs) % 2 else "dve"),
                                     evac=to(proj[:, tile, :], func, scale)))
                cosr, sinr = proj[:, RZ, :], proj[:, RZ + 1, :]
                ra = proj[:, RZ + 2:RZ + 4, :]
                rb = proj[:, RZ + 4:RZ + 6, :]

                def turn(x1, x2):
                    def evac(dve, ps, own):
                        own(dve.tensor_tensor(ra[:, 0, :], x1, cosr, ALU.mult))
                        own(dve.tensor_tensor(ra[:, 1, :], ps, sinr, ALU.mult))
                        own(dve.tensor_tensor(rb[:, 0, :], x1, sinr, ALU.mult))
                        own(dve.tensor_tensor(rb[:, 1, :], ps, cosr, ALU.mult))
                        own.wait(dve)
                        own(dve.tensor_tensor(x1, ra[:, 0, :], ra[:, 1, :], ALU.subtract))
                        return dve.tensor_tensor(x2, rb[:, 0, :], rb[:, 1, :], ALU.add)
                    return evac
                for i in range(0, 16, 2):
                    fm1(ODD[i // 4], (i % 4) * P, RQ + i, eng="act")
                    jobs.append(dict(block=ODD[i // 4], mats=fm_mats(ODD[i // 4], (i % 4 + 1) * P, hT), out=whole,
                                     eng="dve", evac=turn(proj[:, RQ + i, :], proj[:, RQ + i + 1, :]),
                                     **{"with": len(jobs) - 1}))
                turned = len(jobs) - 1
                for c in range(4):
                    for t in range(TT):
                        j = ODD[4 + c]
                        jobs.append(dict(block=j, mats=tm_mats(j, 0, 512, hT, t), out=whole,
                                         eng="act" if t % 2 else "dve", evac=to(rv[:, t, c * 512:(c + 1) * 512])))
                for i in range(16):
                    fm1(ODD[8 + i // 4], (i % 4) * P, RZ + i, ACT.Silu)
                    if i == 0:
                        jobs[-1]["with"] = turned
                for i in range(2):
                    fm1(ODD[12], i * P, EQ + i, scale=0.125, eng="dve")
                for i in range(2):
                    fm1(ODD[12], 256 + i * P, EZ + i, ACT.Silu)
                run_products(jobs, first=tables(pos[:, 0, :], con("invr"), cosr, sinr,
                                                *[proj[:, RZ + i, :] for i in (2, 3, 4)], normed))
            MA = ExitStack()
            with MA:
                memo = sb("mem_out1", [P, TT, 4, HD], ctx=MA)
                groups = [dict(units=[(proj[(h % 2) * 64:(h % 2) * 64 + 64, EQ + h // 2, t * P:(t + 1) * P],
                                       memk[1][(h % 2) * 64:(h % 2) * 64 + 64, h // 2, :], [],
                                       [memv[1][:, b, h * HD:(h + 1) * HD] for b in range(2)]) for h in range(4)],
                               evac=set_evac(memo[:, t, :, :], 4)) for t in range(TT)]
                AT = ExitStack()
                with AT:
                    attention(groups, AT)
                p1 = peq.n
                with nc.Block() as block:
                    @block.tensor
                    def _(pe):
                        for i in range(2):
                            for t in range(TT):
                                mm = pe.transpose(bank[i][:, t * P:(t + 1) * P],
                                                  memo[:, t, 2 * i:2 * i + 2, :].rearrange("p h d -> p (h d)"), ident)
                            peq(mm)

                    @block.vector
                    def _(dve):
                        for i in range(2):
                            dve.wait_ge(pe_self, p1 + i + 1)
                            dveq(dve.tensor_tensor(proj[:, EZ + i, :], bank[i][:, :], proj[:, EZ + i, :], ALU.mult))

            RT = ExitStack()
            with RT:
                decay = sb("decay", [P, T], ctx=RT)
                decay_loaded = sem("decay_loaded")
                with nc.Block() as block:
                    @block.scalar
                    def _(act):
                        act.dma_start(decay[:, :], a["decay"][:, 0:T]).then_inc(decay_loaded, 16)
                sT = sb("ret_s", [P, TT, T], ctx=RT)
                ro = sb("ret_o", [P, 4, T], ctx=RT)
                rq2 = sT[:, 0:2, :]
                st = proj[:, EQ, :]
                LAST = 8
                d0, p0, a0 = dveq.n, peq.n, actq.n
                first_of = [d0 + (h * 11 + (h - 1) * LAST if h else 0) for h in range(RH)]
                mean_of = [first_of[h] + TT + (LAST if h else 0) + 1 for h in range(RH)]
                order = [0, 2, 3, 1]
                with nc.Block() as block:
                    @block.tensor
                    def _(pe):
                        for h in range(RH):
                            d1, a1 = first_of[h], a0 + 9 * h
                            for b in order:
                                n = T - b * P
                                if h > 0 and b == 0:
                                    pe.wait_ge(dve_self, mean_of[h - 1])
                                if h > 0 and b == 1:
                                    pe.wait_ge(dve_self, mean_of[h - 1] + 5)
                                for k in range(2):
                                    mm = pe.matmul(bank[b][:, 0:n], proj[:, RK + 2 * h + k, b * P:(b + 1) * P],
                                                   proj[:, RQ + 2 * h + k, b * P:T], start=k == 0, stop=k == 1)
                                peq(mm)
                            for m in range(4):
                                for i, b in enumerate(order):
                                    if m == 0:
                                        pe.wait_ge(dve_self, d1 + i + 1)
                                    mm = pe.matmul(bank[4 + m][:, b * P:T], rv[:, b, h * 512 + m * P:h * 512 + (m + 1) * P],
                                                   sT[:, b, 0:T - b * P], start=i == 0, stop=i == TT - 1)
                                peq(mm)
                            for m in range(4):
                                pe.wait_ge(act_self, a1 + m + 1)
                                mm = pe.matmul(bank[0][:, :], ones, ro[:, m, :], start=m == 0, stop=m == 3)
                            peq(mm)
                            for m in range(4):
                                pe.wait_ge(act_self, a1 + 4 + m + 1)
                                mm = pe.matmul(bank[1][:, :], ones, rq2[:, m % 2, :], start=m == 0, stop=m == 3)
                                peq(mm)

                    @block.vector
                    def _(dve):
                        def last_steps(h):
                            dve.wait_ge(dve_self, mean_of[h] + 6)
                            for m in range(4):
                                dveq(dve.tensor_tensor(ro[:, m, :], ro[:, m, :], st, ALU.mult))
                            dveq.wait(dve)
                            for m in range(4):
                                y = proj[:, RZ + 4 * h + m, :]
                                dveq(dve.tensor_tensor(y, y, ro[:, m, :], ALU.mult))
                        for h in range(RH):
                            p1, a1 = p0 + 13 * h, a0 + 9 * h
                            dve.wait_ge(decay_loaded, 16 * (h + 1))
                            for i, b in enumerate(order):
                                n = T - b * P
                                dve.wait_ge(pe_self, p1 + i + 1)
                                dveq(dve.tensor_tensor(sT[:, b, 0:n], bank[b][:, 0:n], decay[:, 0:n], ALU.mult))
                            if h > 0:
                                last_steps(h - 1)
                            dve.wait_ge(pe_self, p1 + 9)
                            dveq(dve.tensor_scalar(st, bank[0][:, :], 1.0 / 512, None, ALU.mult))
                            dveq.wait(dve)
                            for m in range(4):
                                dveq(dve.tensor_tensor(ro[:, m, :], ro[:, m, :], st, ALU.subtract))
                            dve.wait_ge(pe_self, p1 + 13)
                            dveq(dve.tensor_scalar(st, bank[1][:, :], 1.0 / 512, EPS, ALU.mult, ALU.add))
                            dve.wait_ge(act_self, a1 + 9)
                            dveq(dve.reciprocal(st, st))
                        last_steps(RH - 1)

                    @block.scalar
                    def _(act):
                        for h in range(RH):
                            d1, p1 = first_of[h], p0 + 13 * h
                            if h + 1 < RH:
                                act.wait_ge(dve_self, d1 + TT)
                                act.dma_start(decay[:, :], a["decay"][:, (h + 1) * T:(h + 2) * T])\
                                   .then_inc(decay_loaded, 16)
                            for m in range(4):
                                if h > 0:
                                    act.wait_ge(dve_self, d1 + TT + 4 + m + 1)
                                act.wait_ge(pe_self, p1 + 4 + m + 1)
                                actq(act.activation(ro[:, m, :], bank[4 + m][:, :], ACT.Copy))
                            for m in range(4):
                                act.wait_ge(dve_self, mean_of[h] + 1 + m)
                                if m >= 2:
                                    act.wait_ge(pe_self, p1 + 10 + m - 2)
                                actq(act.activation(rq2[:, m % 2, :], ro[:, m, :], ACT.Square))
                            act.wait_ge(dve_self, mean_of[h] + 5)
                            actq(act.activation(st, st, ACT.Sqrt))
            yt1 = [RZ + i for i in range(16)] + [EZ, EZ + 1]
            jobs = [dict(block=j, mats=[(block_ap(j)[:, k, :], proj[:, yt1[k], :]) for k in range(18)],
                         out=whole, eng="dve", evac=add_to(m)) for m, j in enumerate(WO1)]
            run_products(jobs, last=norm_parts(xT, xT, "g_fin", proj[:, RK, :], of=range(8), sq=proj[:, RQ:RQ + 8, :]))

        MKV.close()
        res = xT
        xT = sb("normed", [P, KD, T], ctx=es)
        B2 = ExitStack()
        with B2:
            live = B2
            AQ, AK, GQ, GK, GR, GA, GG = 0, 4, 5, 9, 13, 21, 29
            proj = sb("proj2", [P, 37, T])
            av = sb("av", [P, TT, P])
            gv = sb("gv", [P, TT, D])
            z = sb("z", [16, 2, T])
            hT = xT
            normed = norm_parts(res, hT, "g_mix", proj[:, GG + 3, :])
            jobs = []
            R2 = ExitStack()
            with R2:
                cos2 = sb("cos2", [P, T], ctx=R2)
                sin2 = sb("sin2", [P, T], ctx=R2)
                tmp = sb("rot_tmp2", [P, 2, T], ctx=R2)

                def fm2(j, c, tile, func=None, scale=1.0, eng="act"):
                    mats = fm_mats(j, c, hT)
                    jobs.append(dict(block=j, mats=mats, out=whole, eng=eng, evac=to(proj[:, tile, :], func, scale)))
                    return len(jobs) - 1

                def rotary2(tile, src, scale):
                    x = proj[:, tile, :]

                    def evac(dve, ps, own):
                        own(dve.tensor_tensor(tmp[:, 0, :], ps, sin2[:, :], ALU.mult))
                        own(dve.tensor_tensor(tmp[:, 1, :], x, cos2[:, :], ALU.mult))
                        own.wait(dve)
                        own(dve.tensor_tensor(tmp[:, 0, :], tmp[:, 0, :], tmp[:, 1, :], ALU.add))
                        own.wait(dve)
                        return dve.tensor_scalar(x, tmp[:, 0, :], scale, None, ALU.mult)
                    jobs.append(dict(block=None, mats=[(con("rot2"), x)], out=whole, eng="dve", evac=evac, after=src))

                c = [fm2(W2["aq"], i * P, AQ + i) for i in range(4)]
                c.append(fm2(W2["akv"], 0, AK))
                for t in range(TT):
                    jobs.append(dict(block=W2["akv"], mats=tm_mats(W2["akv"], 128, 128, hT, t),
                                     out=lambda b: b[:, 0:128], eng="act", evac=to(av[:, t, :])))
                for i in range(4):
                    rotary2(AQ + i, c[i], 0.125)
                rotary2(AK, c[4], 1.0)
                for i in range(4):
                    fm2(W2["gq"], i * P, GQ + i, scale=float(P) ** -0.5)
                for i in range(4):
                    fm2(W2["gk"], i * P, GK + i, eng="dve")
                for c in range(2):
                    for t in range(TT):
                        j = W2[f"gv{c}"]
                        jobs.append(dict(block=j, mats=tm_mats(j, 0, 512, hT, t), out=whole, eng="dve",
                                         evac=to(gv[:, t, c * 512:(c + 1) * 512])))
                for i in range(8):
                    fm2(W2[f"gr{i // 4}"], (i % 4) * P, GR + i, ACT.Silu)
                for i in range(2):
                    j = W2["z"]
                    jobs.append(dict(block=j, mats=fm_mats(j, 16 * i, hT, 16), out=lambda b: b[0:16, :], eng="dve",
                                     evac=to(z[:, i, :])))
                for i in range(8):
                    fm2(W2[f"ga{i // 4}"], (i % 4) * P, GA + i, ACT.Sigmoid)
                for i in range(8):
                    fm2(W2[f"gg{i // 4}"], (i % 4) * P, GG + i, ACT.Sigmoid)
                run_products(jobs, first=tables(pos[:, 1, :], con("inv2"), cos2[:, :], sin2[:, :],
                                                *[proj[:, GG + i, :] for i in range(3)], normed))

            ybr = xT[:, 4:8, :]
            WA = ExitStack()
            with WA:
                ao = xT[:, 0:4, :].rearrange("p t (h d) -> p t h d", d=HD)
                nsink = sb("nsink", [P, 8], ctx=WA)
                with nc.Block() as block:
                    @block.vector
                    def _(dve):
                        dveq(dve.tensor_scalar(nsink[:, :], par("sink"), -1.0, None, ALU.mult))
                groups = []
                a1 = actq.n
                for t in range(TT):
                    lo, hi = max(t - 1, 0), min(t + 1, TT - 1)
                    masks = []
                    if t > 0:
                        masks.append((0, con("behind")))
                    if t < TT - 1:
                        masks.append(((t + 1 - lo) * P, con("causal")))
                    a1 += 8
                    groups.append(dict(units=[(proj[(h // 4) * 64:(h // 4) * 64 + 64, AQ + h % 4, t * P:(t + 1) * P],
                                               proj[(h // 4) * 64:(h // 4) * 64 + 64, AK, lo * P:(hi + 1) * P], masks,
                                               [av[:, b, (h // 4) * HD:(h // 4 + 1) * HD] for b in range(lo, hi + 1)])
                                              for h in range(8)],
                                       sink=nsink, plus=par("sink"), sink_at=a1, evac=set_evac(ao[:, t, :, :], 8),
                                       order=[0, 4, 1, 5, 2, 6, 3, 7]))
                AT = ExitStack()
                with AT:
                    attention(groups, AT)
                stage = sb("back2", [P, 2, P], ctx=WA)
                b0 = len(items)
                with nc.Block() as block:
                    its = [(t, i) for t in range(TT) for i in range(4)]

                    @block.scalar
                    def _(act):
                        for n, (t, i) in enumerate(its):
                            if n >= 2:
                                act.wait_ge(back_t, b0 + n - 1)
                            act.activation(stage[:, n % 2, :].rearrange("p (g d) -> p g d", g=2),
                                           ao[:, t, :, :].rearrange("p (g i) d -> p i g d", g=2)[:, i], ACT.Copy)\
                               .then_inc(back_in, 1)

                    @block.tensor
                    def _(pe):
                        for n, (t, i) in enumerate(its):
                            pe.wait_ge(back_in, b0 + n + 1)
                            if n >= 2:
                                pe.wait_ge(back_out, b0 + n - 1)
                            pe.transpose(bank[n % 2][:, 0:P], stage[:, n % 2, :], ident).then_inc(back_t, 1)

                    @block.vector
                    def _(dve):
                        for n, (t, i) in enumerate(its):
                            dve.wait_ge(back_t, b0 + n + 1)
                            dve.tensor_copy(ybr[:, i, t * P:(t + 1) * P], bank[n % 2][:, 0:P]).then_inc(back_out, 1)

            GL = ExitStack()
            with GL:
                up = sb("gla_up", [16, 2, 512], ctx=GL)
                up_loaded = sem("up_loaded")
                with nc.Block() as block:
                    @block.sync
                    def _(sp):
                        sp.dma_start(up[:, 0, :], a["gla_gate_up_fwd_2"][0]).then_inc(up_loaded, 16)
                        sp.dma_start(up[:, 1, :], a["gla_gate_up_bwd_2"][0]).then_inc(up_loaded, 16)
                        sp.wait_ge(up_loaded, 32)
                la, t1, t2, cum = (proj[:, i, :] for i in range(AQ, AQ + 4))
                qt, kt_, ke = (xT[:, i, :] for i in range(3))
                am = xT[:, 3, :].rearrange("p (t l) -> p t l", t=TT)
                dec = sb("gla_dec", [P, 8], ctx=GL)
                ket = proj[:, AK, :].rearrange("p (t n) -> p t n", t=TT)
                st_ = sb("gla_state", [P, 8, 256], ctx=GL)
                turns = [(h, d) for h in range(4) for d in range(2)]
                spare = sb("gla_ke2", [P, T], ctx=GL)
                sets = [(qt, kt_, ke), (pos[:, 0, :].bitcast(F32), pos[:, 1, :].bitcast(F32), spare[:, :])]
                decs = [dec, sb("gla_dec2", [P, 8], ctx=GL)]
                cum3 = cum.rearrange("p (c l) -> p c l", l=64)
                g3 = cum3[:, :, 63:64].to_broadcast([P, 8, 64])
                zs, lns, mins, sums, decayed = sem("zs"), sem("lns"), sem("mins"), sem("sums"), sem("decayed")
                read = sem("z_read")

                def c3(x):
                    return x.rearrange("p (c l) -> p c l", l=64)

                def bias(n):
                    h, d = turns[n]
                    return par("bias_f" if d == 0 else "bias_b", h)

                def decay_pe(pe, n):
                    h, d = turns[n]
                    pe.matmul(bank[1][:, :], up[:, d, h * P:(h + 1) * P], z[:, d, :], start=True, stop=True)\
                      .then_inc(zs, 1)

                def decay_act1(act, n):
                    act.wait_ge(zs, n + 1)
                    if n > 0:
                        act.wait_ge(decayed, 4 * n)
                    act.activation(t1, bank[1][:, :], ACT.Abs, bias=bias(n)).then_inc(read, 1)
                    act.wait_ge(read, 2 * n + 1)
                    actq(act.activation(t1, t1, ACT.Exp, scale=-1.0))
                    actq.wait(act)
                    act.activation(t1, t1, ACT.Ln, bias=con("one")).then_inc(lns, 1)

                def decay_dve1(dve, n):
                    dve.wait_ge(read, 2 * n + 1)
                    if n > 0:
                        dve.wait_ge(decayed, 4 * n)
                    dve.tensor_scalar(t2, bank[1][:, :], bias(n), 0.0, ALU.add, ALU.min).then_inc(read, 1)

                def decay_dve2(dve, n):
                    dve.wait_ge(read, 2 * n + 2)
                    dve.wait_ge(lns, n + 1)
                    dveq(dve.tensor_tensor(la, t2, t1, ALU.subtract))
                    dveq.wait(dve)
                    dveq(dve.tensor_tensor_scan(cum, con("scan"), la, 0.0, ALU.mult, ALU.add))
                    dveq.wait(dve)
                    if turns[n][1] == 0:
                        dveq(dve.tensor_copy(t1, cum))
                        dve.tensor_tensor(c3(t2), g3, cum3, ALU.subtract).then_inc(sums, 1)
                    else:
                        dveq(dve.tensor_tensor(c3(t1), g3, cum3, ALU.subtract))
                        dveq.wait(dve)
                        dveq(dve.tensor_tensor(t1, t1, la, ALU.add))
                        dve.tensor_tensor(t2, cum, la, ALU.subtract).then_inc(sums, 1)

                def decay_act2(act, n):
                    q_, k_, e_ = sets[n % 2]
                    act.wait_ge(sums, n + 1)
                    act.activation(q_, t1, ACT.Exp, scale=1.0 / 16).then_inc(decayed, 1)
                    act.activation(k_, t1, ACT.Exp, scale=-1.0 / 16).then_inc(decayed, 1)
                    act.activation(e_, t2, ACT.Exp, scale=1.0 / 16).then_inc(decayed, 1)
                    act.activation(decs[n % 2][:, :], cum3[:, :, 63], ACT.Exp, scale=1.0 / 16).then_inc(decayed, 1)

                with nc.Block() as block:
                    @block.tensor
                    def _(pe):
                        decay_pe(pe, 0)

                    @block.scalar
                    def _(act):
                        decay_act1(act, 0)
                        decay_act2(act, 0)

                    @block.vector
                    def _(dve):
                        decay_dve1(dve, 0)
                        decay_dve2(dve, 0)

                for h in range(4):
                    for d in range(2):
                        turn = 2 * h + d
                        more = turn + 1 < len(turns)
                        qt, kt_, ke = sets[turn % 2]
                        dec = decs[turn % 2]
                        d1, p1, a1 = dveq.n, peq.n, actq.n
                        kvs = [bank[2 + c % 2 + 2 * (c // 4)][:, (c // 2 % 2) * 256:(c // 2 % 2) * 256 + 256]
                               for c in range(8)]
                        order = list(range(8)) if d == 0 else list(range(7, -1, -1))
                        chain_at = d1 + 5 + ((3 if turns[turn + 1][1] == 0 else 4) if more else 0)
                        a_ket = a1 + (2 if more else 1)
                        with nc.Block() as block:
                            @block.vector
                            def _(dve):
                                dveq(dve.tensor_tensor(qt, qt, proj[:, GQ + h, :], ALU.mult))
                                dveq(dve.tensor_tensor(kt_, kt_, proj[:, GK + h, :], ALU.mult))
                                dveq(dve.tensor_tensor(ke, ke, proj[:, GK + h, :], ALU.mult))
                                dveq(dve.memset(st_[:, order[0], :], 0.0))
                                if more:
                                    decay_dve1(dve, turn + 1)
                                dve.wait_ge(pe_self, p1 + 1)
                                m = con("fwd" if d == 0 else "bwd").unsqueeze(1).to_broadcast([P, TT, P])
                                dveq(dve.tensor_tensor(am[:, :, :], bank[0][:, :].rearrange("p (t l) -> p t l", t=TT), m,
                                                       ALU.mult))
                                if more:
                                    decay_dve2(dve, turn + 1)
                                dve.wait_ge(pe_self, p1 + 3)
                                for n in range(7):
                                    c = order[n]
                                    dveq.wait(dve)
                                    dveq(dve.scalar_tensor_tensor(st_[:, order[n + 1], :], st_[:, c, :], dec[:, c:c + 1],
                                                                  kvs[c], ALU.mult, ALU.add))

                            @block.tensor
                            def _(pe):
                                if more:
                                    decay_pe(pe, turn + 1)
                                pe.wait_ge(dve_self, d1 + 2)
                                for t in range(TT):
                                    s = slice(t * P, (t + 1) * P)
                                    mm = pe.matmul(bank[0][:, s], kt_[:, s], qt[:, s], start=True, stop=True)
                                peq(mm)
                                pe.wait_ge(dve_self, d1 + 3)
                                if more:
                                    pe.wait_ge(read, 2 * (turn + 1) + 2)
                                for t in range(TT):
                                    s = slice(t * P, (t + 1) * P)
                                    mm = pe.transpose(bank[1][:, s], ke[:, s], ident)
                                peq(mm)
                                pe.wait_ge(act_self, a_ket)
                                for c in range(8):
                                    r = slice((c % 2) * 64, (c % 2) * 64 + 64)
                                    mm = pe.matmul(kvs[c], ket[r, c // 2, :],
                                                   gv[r, c // 2, h * 256:(h + 1) * 256], start=True, stop=True)
                                peq(mm)
                                pe.wait_ge(dve_self, d1 + 5)
                                for v in range(2):
                                    for t in range(TT):
                                        s = slice(t * P, (t + 1) * P)
                                        pe.matmul(bank[6 + v][:, s], gv[:, t, h * 256 + v * P:h * 256 + (v + 1) * P],
                                                  am[:, t, :], start=(d == 0 and t == 0), stop=False, skip_group_check=True)
                                for n in range(1, 8):
                                    c = order[n]
                                    pe.wait_ge(dve_self, chain_at + n)
                                    for v in range(2):
                                        mm = pe.matmul(bank[6 + v][:, c * 64:(c + 1) * 64], st_[:, c, v * P:(v + 1) * P],
                                                       qt[:, c * 64:(c + 1) * 64], start=False, stop=(n == 7 and d == 1),
                                                       skip_group_check=True)
                                peq(mm)

                            @block.scalar
                            def _(act):
                                if more:
                                    decay_act1(act, turn + 1)
                                act.wait_ge(pe_self, p1 + 2)
                                actq(act.activation(ket[:, :, :].rearrange("p t n -> p (t n)"), bank[1][:, :], ACT.Copy))
                                if more:
                                    decay_act2(act, turn + 1)
                    am2, ke_, rs_ = kt_, ke, qt
                    d1, p1, a1 = dveq.n, peq.n, actq.n
                    with nc.Block() as block:
                        @block.scalar
                        def _(act):
                            for v in range(2):
                                actq(act.activation((am2, ke_)[v], bank[6 + v][:, :], ACT.Square))
                            act.wait_ge(dve_self, d1 + 1)
                            actq(act.activation(rs_, rs_, ACT.Sqrt))

                        @block.tensor
                        def _(pe):
                            for v in range(2):
                                pe.wait_ge(act_self, a1 + v + 1)
                                mm = pe.matmul(bank[0][:, :], ones, (am2, ke_)[v], start=v == 0, stop=v == 1)
                            peq(mm)

                        @block.vector
                        def _(dve):
                            dve.wait_ge(pe_self, p1 + 1)
                            dveq(dve.tensor_scalar(rs_, bank[0][:, :], 1.0 / 256, EPS, ALU.mult, ALU.add))
                            dve.wait_ge(act_self, a1 + 3)
                            dveq(dve.reciprocal(rs_, rs_))
                            dveq.wait(dve)
                            for v in range(2):
                                i = 2 * h + v
                                dveq(dve.scalar_tensor_tensor((am2, ke_)[v], bank[6 + v][:, :], par("g_gla", i),
                                                              rs_, ALU.mult, ALU.mult))
                            dveq.wait(dve)
                            for v in range(2):
                                y = proj[:, GR + 2 * h + v, :]
                                dveq(dve.tensor_tensor(y, y, (am2, ke_)[v], ALU.mult))

            jobs = []

            def times_gate(tile, into=None):
                def evac(dve, ps, own):
                    g = proj[:, tile, :]
                    if into is None:
                        return dve.tensor_tensor(g, ps, g, ALU.mult)
                    own(dve.tensor_tensor(g, ps, g, ALU.mult))
                    own.wait(dve)
                    d = proj[:, into, :]
                    return dve.tensor_tensor(d, d, g, ALU.add)
                return evac
            for m in range(8):
                jobs.append(dict(block=WBA, mats=[(block_ap(WBA)[:, k, m * P:(m + 1) * P], ybr[:, k, :]) for k in range(4)],
                                 out=whole, eng="dve", evac=times_gate(GA + m)))
            for m in range(8):
                j = WBG[m // 4]
                jobs.append(dict(block=j, mats=[(block_ap(j)[:, k, (m % 4) * P:(m % 4 + 1) * P], proj[:, GR + k, :])
                                                for k in range(8)],
                                 out=whole, eng="dve", evac=times_gate(GG + m, GA + m)))
            run_products(jobs)
            jobs = []

            def add_res(m):
                def evac(dve, ps, own):
                    return dve.tensor_tensor(res[:, m, :], ps, res[:, m, :], ALU.add)
                return evac
            for m in range(8):
                j = WO2[m // 4]
                jobs.append(dict(block=j, mats=[(block_ap(j)[:, k, (m % 4) * P:(m % 4 + 1) * P], proj[:, GA + k, :])
                                                for k in range(8)],
                                 out=whole, eng="dve", evac=add_res(m)))
            run_products(jobs, last=norm_parts(res, xT, "g_ffn", proj[:, GG, :], of=range(8)))

        ME = ExitStack()
        with ME:
            live = ME
            xn = xT
            ring.extend(sb(f"ring{i}", [P, SLOT], ctx=es) for i in range(RING, WIDE))
            xg = sb("xg", [P, KD, NE * CAP])
            wr = xg[:, 0, 0:KD * NE].rearrange("p (k e) -> p k e", k=KD)
            router_loaded = sem("router_loaded")
            with nc.Block() as block:
                @block.sync
                def _(sp):
                    sp.dma_start(wr[:, :, :], a["w_router_2"][0].rearrange("(k p) e -> p k e", p=P))\
                      .then_inc(router_loaded, 16)
                    issue_blocks(sp, EXP[0][0] + WIDE)
            rankT = sb("rankT", [NE, T])
            affT = sb("affT", [NE, T])
            R1 = ExitStack()
            with R1:
                aff = sb("aff", [P, TT, NE], ctx=R1)
                st1 = sb("aff_m", [P, 2, TT], ctx=R1)
                rank = sb("rank", [P, TT, NE], ctx=R1)
                work = sb("topk", [NE, T], ctx=R1)
                top = sb("top8", [NE, 8], ctx=R1)
                onesT = sb("ones_row", [NE, T], ctx=R1)
                xnt = sb("xn_tm", [P, TT, D], ctx=R1)
                hot = sb("hot", [P, TT, NE, CAP], ctx=R1)
                d1, p1, a1 = dveq.n, peq.n, actq.n
                with nc.Block() as block:
                    @block.tensor
                    def _(pe):
                        pe.wait_ge(router_loaded, 16)
                        for t in range(TT):
                            for k in range(KD):
                                mm = pe.matmul(bank[0][:, t * NE:(t + 1) * NE], xn[:, k, t * P:(t + 1) * P], wr[:, k, :],
                                               start=k == 0, stop=k == KD - 1)
                        peq(mm)
                        for t in range(TT):
                            for half in range(2):
                                n = 2 * t + half
                                if n >= 4:
                                    pe.wait_ge(act_self, a1 + n - 3)
                                for k in range(4):
                                    mm = pe.transpose(bank[1 + n % 4][:, k * P:(k + 1) * P],
                                                      xn[:, 4 * half + k, t * P:(t + 1) * P], ident)
                                peq(mm)
                        pe.wait_ge(dve_self, d1 + 5)
                        for t in range(TT):
                            mm = pe.transpose(bank[5][0:NE, t * P:(t + 1) * P], aff[:, t, :], ident)
                        peq(mm)

                    @block.scalar
                    def _(act):
                        for n in range(8):
                            act.wait_ge(pe_self, p1 + 2 + n)
                            actq(act.activation(xnt[:, n // 2, (n % 2) * 512:(n % 2 + 1) * 512], bank[1 + n % 4][:, :],
                                                ACT.Copy))
                        act.wait_ge(dve_self, d1 + 2)
                        actq(act.activation(aff[:, :, :], aff[:, :, :], ACT.Exp))

                    @block.vector
                    def _(dve):
                        def step(ins):
                            dveq(ins)
                            dveq.wait(dve)
                        dve.wait_ge(pe_self, p1 + 1)
                        lg = bank[0][:, 0:TT * NE].rearrange("p (t e) -> p t e", t=TT)
                        step(dve.tensor_reduce(st1[:, 0, :], lg, AX.X, ALU.max))
                        step(dve.tensor_tensor(aff[:, :, :], lg, st1[:, 0, :].unsqueeze(2).to_broadcast([P, TT, NE]),
                                               ALU.subtract))
                        dve.wait_ge(act_self, a1 + 9)
                        step(dve.tensor_reduce(st1[:, 1, :], aff[:, :, :], AX.X, ALU.add))
                        step(dve.reciprocal(st1[:, 1, :], st1[:, 1, :]))
                        step(dve.tensor_tensor(aff[:, :, :], aff[:, :, :],
                                               st1[:, 1, :].unsqueeze(2).to_broadcast([P, TT, NE]), ALU.mult))
                        dve.wait_ge(pe_self, p1 + 10)
                        dveq(dve.memset(onesT[:, :], 1.0))
                        dveq(dve.tensor_copy(affT[:, :], bank[5][0:NE, :]))
                        step(dve.tensor_copy(work[:, :], bank[5][0:NE, :]))
                        for _ in range(CAP // 8):
                            step(dve.max(top[:, :], work[:, :]))
                            step(dve.match_replace(work[:, :], top[:, :], work[:, :], -1.0))
                        step(dve.tensor_scalar(work[:, :], work[:, :], 0.0, None, ALU.is_lt))
                        step(dve.tensor_tensor_scan(rankT[:, :], onesT[:, :], work[:, :], 0.0, ALU.mult, ALU.add))
                        step(dve.tensor_tensor(rankT[:, :], rankT[:, :], work[:, :], ALU.mult))
                d1, p1, a1 = dveq.n, peq.n, actq.n
                with nc.Block() as block:
                    @block.tensor
                    def _(pe):
                        for t in range(TT):
                            mm = pe.transpose(bank[0][:, t * NE:(t + 1) * NE], rankT[:, t * P:(t + 1) * P],
                                              ident[0:NE, 0:NE])
                        peq(mm)
                        n = 0
                        for half in range(2):
                            for k in range(KD):
                                if n >= 4:
                                    pe.wait_ge(act_self, a1 + n - 3)
                                for t in range(TT):
                                    if n == 0:
                                        pe.wait_ge(dve_self, d1 + 2 + t)
                                    mm = pe.matmul(bank[1 + n % 4][:, :], xnt[:, t, k * P:(k + 1) * P],
                                                   hot[:, t, 8 * half:8 * half + 8, :].rearrange("p e s -> p (e s)"),
                                                   start=t == 0, stop=t == TT - 1)
                                peq(mm)
                                n += 1

                    @block.vector
                    def _(dve):
                        dve.wait_ge(pe_self, p1 + 1)
                        dveq(dve.tensor_copy(rank[:, :, :], bank[0][:, 0:TT * NE].rearrange("p (t e) -> p t e", t=TT)))
                        dveq.wait(dve)
                        for t in range(TT):
                            dveq(dve.tensor_tensor(hot[:, t, :, :], con("slots").unsqueeze(1).to_broadcast([P, NE, CAP]),
                                                   rank[:, t, :].unsqueeze(2).to_broadcast([P, NE, CAP]), ALU.is_equal))

                    @block.scalar
                    def _(act):
                        for n in range(16):
                            act.wait_ge(pe_self, p1 + 2 + n)
                            half, k = n // 8, n % 8
                            actq(act.activation(xg[:, k, half * 512:(half + 1) * 512], bank[1 + n % 4][:, :], ACT.Copy))
            ye = sb("ye", [P, KD, D])
            put = xT
            bc = sb("bc", [P, T])
            pick = sb("pick", [NE, KD * P])
            pick_loaded = sem("pick_loaded")
            with nc.Block() as block:
                @block.scalar
                def _(act):
                    act.dma_start(pick[:, :], a["pick"]).then_inc(pick_loaded, 16)
                    act.wait_ge(pick_loaded, 16)
            sg = bc
            hid = sb("hid", [P, D])
            hidT = sb("hidT", [P, KD, P])
            act_hid, dve_hid, hid_t, hid_out, ye_out = (sem("act_hid"), sem("dve_hid"), sem("hid_t"), sem("hid_out"),
                                                        sem("ye_out"))
            comb_done, comb_out = sem("comb_done"), sem("comb_out")
            put_mm, put_bc, put_done = sem("put_mm"), sem("put_bc"), sem("put_done")
            t0 = counts["tiles"]
            for p in range(NE // 2):
                for i in range(12):
                    last_tile[EXP[p][i]] = t0 + 12 * p + i + 1
            with nc.Block() as block:
                @block.sync
                def _(sp):
                    issue_blocks(sp, EXP[-1][-1] + WIDE + 1)

                def combine(pe, c):
                    q = c // 2
                    pe.wait_ge(ye_out, 4 * q + 4)
                    pe.wait_ge(put_done, min(c + 2, KD))
                    for i in range(4):
                        n, m = 4 * c + i, 4 * (c % 2) + i
                        if n >= 3:
                            pe.wait_ge(comb_out, n - 2)
                        for k in (2 * q, 2 * q + 1):
                            mm = pe.matmul(bank[5 + n % 3][:, :], ye[:, k, m * P:(m + 1) * P], put[:, k, :],
                                           start=k == 2 * q, stop=k == 2 * q + 1)
                        mm.then_inc(comb_done, 1)

                def add_combined(dve, c):
                    for i in range(4):
                        n, m = 4 * c + i, 4 * (c % 2) + i
                        dve.wait_ge(comb_done, n + 1)
                        if n >= 1:
                            dve.wait_ge(comb_out, n)
                        dve.tensor_tensor(res[:, m, :], bank[5 + n % 3][:, :], res[:, m, :], ALU.add)\
                           .then_inc(comb_out, 1)

                @block.tensor
                def _(pe):
                    for p in range(NE // 2):
                        base = t0 + 12 * p
                        for i in range(8):
                            n, which, e = i // 4, (i // 2) % 2, i % 2
                            j = EXP[p][i]
                            wait_block(pe, j)
                            if e == 0 and p + n > 0:
                                pe.wait_ge(dve_hid, 2 * p + n)
                            if e == 0 and n == 1:
                                pe.wait_ge(dve_hid, 2 * p + 1)
                            for k in range(KD):
                                mm = pe.matmul(bank[which][e * 64:(e + 1) * 64, :],
                                               xg[:, k, (2 * p + e) * CAP:(2 * p + e + 1) * CAP], block_ap(j)[:, k, :],
                                               start=k == 0, stop=k == KD - 1)
                            mm.then_inc(tiles_done, 1)
                        if p >= 2:
                            combine(pe, p - 2)
                            pe.wait_ge(comb_out, 4 * (p - 1))
                        row = pick[:, p * P:(p + 1) * P]
                        pe.matmul(bank[5][:, :], row, rankT[:, :], start=True, stop=True)
                        pe.matmul(bank[6][:, :], row, affT[:, :], start=True, stop=True).then_inc(put_mm, 1)
                        for n in range(2):
                            pe.wait_ge(dve_hid, 2 * p + n + 1)
                            if p + n > 0:
                                pe.wait_ge(hid_out, 2 * p + n)
                            for k in range(4):
                                mm = pe.transpose(bank[2][:, k * P:(k + 1) * P],
                                                  hid[:, n * 512 + k * P:n * 512 + (k + 1) * P], ident)
                            mm.then_inc(hid_t, 1)
                        pe.wait_ge(hid_out, 2 * p + 2)
                        for i in range(8, 12):
                            n, e = (i - 8) // 2, i % 2
                            j = EXP[p][i]
                            wait_block(pe, j)
                            if e == 0 and p > 0:
                                pe.wait_ge(ye_out, 2 * p - 1 + n)
                            for k in range(KD):
                                mm = pe.matmul(bank[3 + n][e * 64:(e + 1) * 64, :], hidT[:, k, e * CAP:(e + 1) * CAP],
                                               block_ap(j)[:, k, :], start=k == 0, stop=k == KD - 1)
                            mm.then_inc(tiles_done, 1)
                    combine(pe, 6)
                    combine(pe, 7)

                @block.scalar
                def _(act):
                    for p in range(NE // 2):
                        base = t0 + 12 * p
                        for n in range(2):
                            act.wait_ge(tiles_done, base + 4 * n + 2)
                            if p > 0:
                                act.wait_ge(put_done, p)
                            if p + n > 0:
                                act.wait_ge(dve_hid, 2 * p + n)
                            act.activation(sg[:, :], bank[0][:, :], ACT.Silu).then_inc(act_hid, 1)
                        act.wait_ge(put_mm, p + 1)
                        act.wait_ge(dve_hid, 2 * p + 2)
                        act.activation(bc[:, :], bank[6][:, :], ACT.Copy).then_inc(put_bc, 1)
                        for n in range(2):
                            act.wait_ge(hid_t, 2 * p + n + 1)
                            act.activation(hidT[:, 4 * n:4 * n + 4, :].rearrange("p k s -> p (k s)"), bank[2][:, :],
                                           ACT.Copy).then_inc(hid_out, 1)

                @block.vector
                def _(dve):
                    for p in range(NE // 2):
                        base = t0 + 12 * p
                        for n in range(2):
                            dve.wait_ge(act_hid, 2 * p + n + 1)
                            dve.wait_ge(tiles_done, base + 4 * n + 4)
                            if p > 0:
                                dve.wait_ge(hid_t, 2 * p)
                            dve.tensor_tensor(hid[:, n * 512:(n + 1) * 512], bank[1][:, :], sg[:, :], ALU.mult)\
                               .then_inc(dve_hid, 1)
                        if p >= 2:
                            add_combined(dve, p - 2)
                        dve.wait_ge(put_bc, p + 1)
                        dve.scalar_tensor_tensor(put[:, p, :], bank[5][:, :], con("slot"), bc[:, :],
                                                 ALU.is_equal, ALU.mult).then_inc(put_done, 1)
                        for n in range(2):
                            dve.wait_ge(tiles_done, base + 8 + 2 * n + 2)
                            dve.tensor_copy(ye[:, p, n * 512:(n + 1) * 512], bank[3 + n][:, :]).then_inc(ye_out, 1)
                    add_combined(dve, 6)
                    add_combined(dve, 7)
            counts["tiles"] += 96

        PL = ExitStack()
        with PL:
            live = PL
            hT = xT
            gate = sb("ple_gate", [P, KD, T])
            pT_ = sb("pleT", [P, 2, T])
            ple_loaded = sem("ple_loaded")
            with nc.Block() as block:
                @block.scalar
                def _(act):
                    act.dma_start(pT_[:, :, :], a["pT"].rearrange("(k p) n -> p k n", p=P)).then_inc(ple_loaded, 16)
            normed = norm_parts(res, hT, "g_ple", gate[:, 7, :])

            def norm_then_embedding(pe):
                normed["pe"](pe)
                pe.wait_ge(ple_loaded, 16)
            jobs = [dict(block=WPG[m // 4], mats=fm_mats(WPG[m // 4], (m % 4) * P, hT), out=whole, eng="act",
                         evac=to(gate[:, m, :], ACT.Sigmoid)) for m in range(8)]

            def ple_evac(m):
                def evac(dve, ps, own):
                    own(dve.tensor_tensor(gate[:, m, :], ps, gate[:, m, :], ALU.mult))
                    own.wait(dve)
                    return dve.tensor_tensor(res[:, m, :], res[:, m, :], gate[:, m, :], ALU.add)
                return evac
            jobs += [dict(block=WPL, mats=[(block_ap(WPL)[:, k, m * P:(m + 1) * P], pT_[:, k, :]) for k in range(2)],
                          out=whole, eng="dve", evac=ple_evac(m), **{"with": m}) for m in range(8)]
            behind = (normed["acts"], 1, len(normed["ready"]) + 2 + 8)
            ended = norm_parts(res, hT, "g_last", pT_[:, 0, :], behind=behind, of=range(8, 16))

            def store(sp):
                for k in range(0, KD, 2):
                    sp.wait_ge(dve_self, ended["ready"][k + 1])
                    sp.dma_start(out.rearrange("(k p) n -> p k n", p=P)[:, k:k + 2, :], hT[:, k:k + 2, :])\
                      .then_inc(stored, 16)
                sp.wait_ge(stored, 16 * KD // 2)
            run_products(jobs, first=dict(normed, pe=norm_then_embedding), last=dict(ended, sync=store))


WEIGHTS = ["l0_w_in", "l0_w_mem_kv", "l0_w_out", "l1_w_in", "l1_w_mem_kv", "l1_w_out", "l0_cmp_w1_k", "l0_cmp_w1_v",
           "l0_cmp_w2_k", "l0_cmp_w2_v", "w_in_2", "gla_gate_up_fwd_2", "gla_gate_up_bwd_2", "w_branch_attn_2",
           "w_branch_gla_2", "w_out_2", "w_router_2", "w_exp_gate_2", "w_exp_up_2", "w_exp_down_2", "w_ple_gate_2",
           "w_ple_2"]


def kernel(**inputs):
    import concourse.bacc as _bacc
    from concourse.bass_utils import run_bass_kernel_spmd as _run

    x = {k: np.asarray(v) for k, v in inputs.items()}

    def columns(v, k):
        return v.reshape(k, P).T

    def rows(v):
        return np.broadcast_to(v.reshape(1, -1), (P, v.size))

    parts = {
        "g_l0": columns(x["l0_norm_g"], KD), "g_mem": columns(x["mem_norm_g"], KD), "g_l1": columns(x["l1_norm_g"], KD),
        "g_fin": columns(x["final_norm_g"], KD), "g_mix": columns(x["norm_mix_2"], KD),
        "g_ffn": columns(x["norm_ffn_2"], KD), "g_ple": columns(x["norm_ple_2"], KD),
        "g_last": columns(x["norm_final_2"], KD), "g_gla": columns(x["gla_norm_2"], KD),
        "nsa_b": rows(x["l0_nsa_gate_b"]), "sink": rows(x["attn_sink_2"]),
        "bias_f": columns(x["gla_gate_bias_fwd_2"], 4), "bias_b": columns(x["gla_gate_bias_bwd_2"], 4),
        "pe_k": np.tile(x["l0_cmp_pe_k"].T, (2, 1)), "pe_v": np.tile(x["l0_cmp_pe_v"].T, (2, 1)),
    }
    consts, decay, pick = shape_constants()
    arrays = {
        "consts": consts, "decay": decay, "pick": pick,
        "vecs": np.ascontiguousarray(np.concatenate([parts[name] for name in VEC], axis=1)),
        "pos": np.ascontiguousarray(np.broadcast_to(np.stack([x["positions"][0], x["positions_2"][0]])[None], (P, 2, T))),
        "xT": np.ascontiguousarray(x["x"][0].T),
        "memT": np.ascontiguousarray(x["mem"][0].T),
        "pT": np.ascontiguousarray(x["p_2"][0, 0].T),
    }
    for name in WEIGHTS:
        arrays[name] = np.ascontiguousarray(x[name])
    nc = _bacc.Bacc("TRN2", target_bir_lowering=False, num_devices=1)
    aps = {n: nc.dram_tensor(f"in_{n}", v.shape, mybir.dt.from_np(v.dtype), kind="ExternalInput").ap()
           for n, v in arrays.items()}
    out = nc.dram_tensor("out_0", (D, T), F32, kind="ExternalOutput").ap()
    build(nc, aps, out)
    r = _run(nc, [{f"in_{n}": v for n, v in arrays.items()}], core_ids=[0])
    return np.ascontiguousarray(r.results[0]["out_0"].T)[None]
```
